# Optimizing a Trainium2 kernel written in Bass

```python
import math
import jax, jax.numpy as jnp
from jax import lax
import numpy as np

D_MODEL = 1024
BATCH = 1
SEQ = 512
DEPTH = 2

N_EVEN = (DEPTH + 1) // 2
N_ODD = DEPTH // 2
EPS = 1e-6

S5_WIDTH = D_MODEL // 2
S5_GROUP = 16
S5_GROUPS = S5_WIDTH // S5_GROUP
S5_STATE = 64

HG_WIDTH = D_MODEL - S5_WIDTH
HG_HEAD_DIM = 128
HG_HEADS = HG_WIDTH // HG_HEAD_DIM
HG_CHUNK = 32

EVEN_IN = S5_WIDTH + 4 * HG_WIDTH

HEAD_DIM = 64
N_Q_HEADS = D_MODEL // HEAD_DIM
N_KV_HEADS = max(1, N_Q_HEADS // 8)
GQA_GROUP = N_Q_HEADS // N_KV_HEADS
Q_WIDTH = N_Q_HEADS * HEAD_DIM
KV_WIDTH = N_KV_HEADS * HEAD_DIM
WINDOW = 128
ATT_BLOCK = 128

N_GROUPS = 4
EXPERTS_PER_GROUP = 4
N_EXPERTS = N_GROUPS * EXPERTS_PER_GROUP
TOP_K = 2
D_EXPERT = D_MODEL // 4

kernel_name = "hybrid_s5_hgrn2_swa_hmoe"

def rms_norm(x, gain):
    xf = x.astype(jnp.float32)
    return xf * lax.rsqrt(jnp.mean(xf * xf, axis=-1, keepdims=True) + EPS) * gain.astype(jnp.float32)

def alibi_slopes():
    return jnp.asarray(2.0 ** (-8.0 * np.arange(1, N_Q_HEADS + 1) / N_Q_HEADS), dtype=jnp.float32)

def s5_mixer(u, lam_re, lam_im, log_step, b_re, b_im, c_re, c_im, d_skip, w_glu):
    f32 = jnp.float32
    bsz, seqlen, _ = u.shape
    uf = u.astype(f32).reshape(bsz, seqlen, S5_GROUPS, S5_GROUP)
    lr, li = lam_re.astype(f32), lam_im.astype(f32)
    step = jnp.exp(log_step.astype(f32))[:, None]
    mag = jnp.exp(lr * step)
    ab_re = mag * jnp.cos(li * step)
    ab_im = mag * jnp.sin(li * step)
    den = lr * lr + li * li
    nr, ni = ab_re - 1.0, ab_im
    z_re = (nr * lr + ni * li) / den
    z_im = (ni * lr - nr * li) / den
    br, bi = b_re.astype(f32), b_im.astype(f32)
    bb_re = z_re[..., None] * br - z_im[..., None] * bi
    bb_im = z_re[..., None] * bi + z_im[..., None] * br
    bu_re = jnp.einsum('blgh,gph->blgp', uf, bb_re)
    bu_im = jnp.einsum('blgh,gph->blgp', uf, bb_im)
    a_re = jnp.broadcast_to(ab_re[None, None], (1, seqlen, S5_GROUPS, S5_STATE))
    a_im = jnp.broadcast_to(ab_im[None, None], (1, seqlen, S5_GROUPS, S5_STATE))

    def combine(left, right):
        a1r, a1i, b1r, b1i = left
        a2r, a2i, b2r, b2i = right
        return (a2r * a1r - a2i * a1i,
                a2r * a1i + a2i * a1r,
                a2r * b1r - a2i * b1i + b2r,
                a2r * b1i + a2i * b1r + b2i)

    _, _, xs_re, xs_im = lax.associative_scan(combine, (a_re, a_im, bu_re, bu_im), axis=1)
    y = (jnp.einsum('blgp,ghp->blgh', xs_re, c_re.astype(f32))
         - jnp.einsum('blgp,ghp->blgh', xs_im, c_im.astype(f32)))
    y = y.reshape(bsz, seqlen, S5_WIDTH) + d_skip.astype(f32) * u.astype(f32)
    y = jax.nn.gelu(y)
    return y * jax.nn.sigmoid(jnp.einsum('blc,ce->ble', y, w_glu.astype(f32)))

def hgrn2_mixer(q, f_logit, i_val, g, lower_bound, o_gain):
    f32 = jnp.float32
    bsz, seqlen, _ = q.shape
    nc = seqlen // HG_CHUNK
    qs = jax.nn.silu(q.astype(f32))
    f = lower_bound + (1.0 - lower_bound) * jax.nn.sigmoid(f_logit.astype(f32))
    log_f = jnp.log(f)
    k = 1.0 - f

    def split(t):
        return t.reshape(bsz, nc, HG_CHUNK, HG_HEADS, HG_HEAD_DIM).transpose(0, 3, 1, 2, 4)

    qc, kc, vc, lfc = split(qs), split(k), split(i_val.astype(f32)), split(log_f)
    b = jnp.cumsum(lfc, axis=3)
    b_last = b[:, :, :, -1:, :]
    b_ref = b[:, :, :, HG_CHUNK // 2 - 1:HG_CHUNK // 2, :]
    scores = jnp.einsum('bhntd,bhnsd->bhnts', qc * jnp.exp(b - b_ref), kc * jnp.exp(b_ref - b))
    causal = jnp.tril(jnp.ones((HG_CHUNK, HG_CHUNK), dtype=bool))
    scores = jnp.where(causal, scores, 0.0)
    o_intra = jnp.einsum('bhnts,bhnsv->bhntv', scores, vc)
    u_chunk = jnp.einsum('bhnsd,bhnsv->bhndv', kc * jnp.exp(b_last - b), vc)
    decay = jnp.exp(b_last[:, :, :, 0, :])

    def step(state, inp):
        dec, uc = inp
        return dec[..., None] * state + uc, state

    s0 = jnp.zeros((bsz, HG_HEADS, HG_HEAD_DIM, HG_HEAD_DIM), f32)
    _, s_prev = lax.scan(step, s0, (jnp.moveaxis(decay, 2, 0), jnp.moveaxis(u_chunk, 2, 0)))
    s_prev = jnp.moveaxis(s_prev, 0, 2)
    o_inter = jnp.einsum('bhntd,bhndv->bhntv', qc * jnp.exp(b), s_prev)
    o = (o_intra + o_inter).transpose(0, 2, 3, 1, 4).reshape(bsz, seqlen, HG_HEADS, HG_HEAD_DIM)
    o = rms_norm(o, o_gain).reshape(bsz, seqlen, HG_WIDTH)
    return o * jax.nn.silu(g.astype(f32))

def sliding_window_attention(h, w_qkv, q_gain, k_gain, sinks):
    f32 = jnp.float32
    bsz, seqlen, _ = h.shape
    nb = seqlen // ATT_BLOCK
    qkv = jnp.einsum('bld,de->ble', h, w_qkv)
    q = qkv[..., :Q_WIDTH].reshape(bsz, seqlen, N_KV_HEADS, GQA_GROUP, HEAD_DIM)
    k = qkv[..., Q_WIDTH:Q_WIDTH + KV_WIDTH].reshape(bsz, seqlen, N_KV_HEADS, HEAD_DIM)
    v = qkv[..., Q_WIDTH + KV_WIDTH:].reshape(bsz, seqlen, N_KV_HEADS, HEAD_DIM).astype(f32)
    q = rms_norm(q, q_gain) * (HEAD_DIM ** -0.5)
    k = rms_norm(k, k_gain)
    qb = q.reshape(bsz, nb, ATT_BLOCK, N_KV_HEADS, GQA_GROUP, HEAD_DIM)

    def band(t):
        tb = t.reshape(bsz, nb, ATT_BLOCK, N_KV_HEADS, HEAD_DIM)
        prev = jnp.concatenate([jnp.zeros_like(tb[:, :1]), tb[:, :-1]], axis=1)
        return jnp.concatenate([prev, tb], axis=2)

    kw, vw = band(k), band(v)
    s = jnp.einsum('bnqhgd,bnkhd->bhgnqk', qb, kw)
    qi = jnp.arange(ATT_BLOCK)[:, None]
    ki = jnp.arange(2 * ATT_BLOCK)[None, :]
    dist = qi - ki + ATT_BLOCK
    blk = jnp.arange(nb)[:, None, None]
    valid = (dist >= 0) & (dist < WINDOW) & (blk * ATT_BLOCK + ki - ATT_BLOCK >= 0)
    slopes = alibi_slopes().reshape(N_KV_HEADS, GQA_GROUP)[:, :, None, None, None]
    s = s - slopes * dist.astype(f32)
    s = jnp.where(valid, s, -jnp.inf)
    sink = sinks.astype(f32).reshape(N_KV_HEADS, GQA_GROUP)[:, :, None, None, None]
    m = jnp.maximum(jnp.max(s, axis=-1, keepdims=True), sink)
    p = jnp.exp(s - m)
    p = p / (jnp.sum(p, axis=-1, keepdims=True) + jnp.exp(sink - m))
    o = jnp.einsum('bhgnqk,bnkhd->bnqhgd', p, vw)
    return o.reshape(bsz, seqlen, Q_WIDTH)

def hierarchical_moe(h, w_rg, b_rg, w_re, b_re, w_gate, w_up, w_down):
    f32 = jnp.float32
    bsz, seqlen, dm = h.shape
    t = h.reshape(bsz * seqlen, dm)
    g_prob = jax.nn.softmax(jnp.einsum('nd,dg->ng', t, w_rg).astype(f32) + b_rg.astype(f32), axis=-1)
    g_gate, g_idx = lax.top_k(g_prob, 1)
    e_logits = (jnp.einsum('nd,de->ne', t, w_re).astype(f32) + b_re.astype(f32))
    e_logits = e_logits.reshape(-1, N_GROUPS, EXPERTS_PER_GROUP)
    grp_onehot = jax.nn.one_hot(g_idx[:, 0], N_GROUPS, dtype=f32)
    e_sel = jnp.sum(e_logits * grp_onehot[:, :, None], axis=1)
    e_prob = jax.nn.softmax(e_sel, axis=-1)
    e_w, e_idx = lax.top_k(e_prob, TOP_K)
    e_w = e_w / jnp.sum(e_w, axis=-1, keepdims=True)
    weights = g_gate * e_w
    expert = g_idx * EXPERTS_PER_GROUP + e_idx
    combine = jnp.sum(jax.nn.one_hot(expert, N_EXPERTS, dtype=f32) * weights[..., None], axis=1)
    hid = jax.nn.silu(jnp.einsum('nd,edf->nef', t, w_gate)) * jnp.einsum('nd,edf->nef', t, w_up)
    hid = hid * combine[:, :, None].astype(hid.dtype)
    y = jnp.einsum('nef,efd->nd', hid, w_down)
    return y.reshape(bsz, seqlen, dm)

def setup_inputs(seed: int = 0) -> dict:
    key = jax.random.key(seed)
    ks = iter(jax.random.split(key, 40))

    def nrm(shape, scale):
        return jax.random.normal(next(ks), shape, jnp.float32) * scale

    n_idx = jnp.arange(S5_STATE, dtype=jnp.float32)
    return {
        "x": nrm((BATCH, SEQ, D_MODEL), 1.0),
        "even_mix_norm": 1.0 + nrm((N_EVEN, D_MODEL), 0.02),
        "even_in_proj": nrm((N_EVEN, D_MODEL, EVEN_IN), D_MODEL ** -0.5),
        "s5_lambda_re": -0.5 + nrm((N_EVEN, S5_GROUPS, S5_STATE), 0.01),
        "s5_lambda_im": math.pi * n_idx + nrm((N_EVEN, S5_GROUPS, S5_STATE), 0.01),
        "s5_log_step": jax.random.uniform(next(ks), (N_EVEN, S5_GROUPS), jnp.float32, math.log(1e-3), math.log(1e-1)),
        "s5_b_re": nrm((N_EVEN, S5_GROUPS, S5_STATE, S5_GROUP), (2 * S5_GROUP) ** -0.5),
        "s5_b_im": nrm((N_EVEN, S5_GROUPS, S5_STATE, S5_GROUP), (2 * S5_GROUP) ** -0.5),
        "s5_c_re": nrm((N_EVEN, S5_GROUPS, S5_GROUP, S5_STATE), S5_STATE ** -0.5),
        "s5_c_im": nrm((N_EVEN, S5_GROUPS, S5_GROUP, S5_STATE), S5_STATE ** -0.5),
        "s5_d": nrm((N_EVEN, S5_WIDTH), 0.5),
        "s5_glu_w": nrm((N_EVEN, S5_WIDTH, S5_WIDTH), S5_WIDTH ** -0.5),
        "hgrn_lower_bounds": nrm((DEPTH + 1, HG_WIDTH), 0.1),
        "hgrn_o_norm": 1.0 + nrm((N_EVEN, HG_HEAD_DIM), 0.02),
        "even_out_proj": nrm((N_EVEN, D_MODEL, D_MODEL), D_MODEL ** -0.5),
        "odd_mix_norm": 1.0 + nrm((N_ODD, D_MODEL), 0.02),
        "odd_wqkv": nrm((N_ODD, D_MODEL, Q_WIDTH + 2 * KV_WIDTH), D_MODEL ** -0.5),
        "odd_q_norm": 1.0 + nrm((N_ODD, HEAD_DIM), 0.02),
        "odd_k_norm": 1.0 + nrm((N_ODD, HEAD_DIM), 0.02),
        "odd_sinks": nrm((N_ODD, N_Q_HEADS), 0.5),
        "odd_out_proj": nrm((N_ODD, Q_WIDTH, D_MODEL), Q_WIDTH ** -0.5),
        "moe_norm": 1.0 + nrm((DEPTH, D_MODEL), 0.02),
        "moe_router_group": nrm((DEPTH, D_MODEL, N_GROUPS), D_MODEL ** -0.5),
        "moe_router_group_bias": nrm((DEPTH, N_GROUPS), 0.01),
        "moe_router_expert": nrm((DEPTH, D_MODEL, N_EXPERTS), D_MODEL ** -0.5),
        "moe_router_expert_bias": nrm((DEPTH, N_EXPERTS), 0.01),
        "moe_w_gate": nrm((DEPTH, N_EXPERTS, D_MODEL, D_EXPERT), D_MODEL ** -0.5),
        "moe_w_up": nrm((DEPTH, N_EXPERTS, D_MODEL, D_EXPERT), D_MODEL ** -0.5),
        "moe_w_down": nrm((DEPTH, N_EXPERTS, D_EXPERT, D_MODEL), D_EXPERT ** -0.5),
    }

def reference(x, even_mix_norm, even_in_proj, s5_lambda_re, s5_lambda_im, s5_log_step,
              s5_b_re, s5_b_im, s5_c_re, s5_c_im, s5_d, s5_glu_w, hgrn_lower_bounds,
              hgrn_o_norm, even_out_proj, odd_mix_norm, odd_wqkv, odd_q_norm, odd_k_norm,
              odd_sinks, odd_out_proj, moe_norm, moe_router_group, moe_router_group_bias,
              moe_router_expert, moe_router_expert_bias, moe_w_gate, moe_w_up, moe_w_down):
    lower_bounds = jnp.cumsum(jax.nn.softmax(hgrn_lower_bounds.astype(jnp.float32), axis=0), axis=0)
    for layer in range(DEPTH):
        j = layer // 2
        if layer % 2 == 0:
            h = rms_norm(x, even_mix_norm[j])
            proj = jnp.einsum('bld,de->ble', h, even_in_proj[j])
            u = proj[..., :S5_WIDTH]
            hq, hf, hi, hg = jnp.split(proj[..., S5_WIDTH:], 4, axis=-1)
            a_out = s5_mixer(u, s5_lambda_re[j], s5_lambda_im[j], s5_log_step[j], s5_b_re[j],
                             s5_b_im[j], s5_c_re[j], s5_c_im[j], s5_d[j], s5_glu_w[j])
            b_out = hgrn2_mixer(hq, hf, hi, hg, lower_bounds[layer], hgrn_o_norm[j])
            mix = jnp.einsum('blc,cd->bld', jnp.concatenate([a_out, b_out], axis=-1), even_out_proj[j])
        else:
            h = rms_norm(x, odd_mix_norm[j])
            att = sliding_window_attention(h, odd_wqkv[j], odd_q_norm[j], odd_k_norm[j], odd_sinks[j])
            mix = jnp.einsum('blc,cd->bld', att, odd_out_proj[j])
        x = x + mix.astype(x.dtype)
        h = rms_norm(x, moe_norm[layer])
        ffn = hierarchical_moe(h, moe_router_group[layer], moe_router_group_bias[layer],
                               moe_router_expert[layer], moe_router_expert_bias[layer],
                               moe_w_gate[layer], moe_w_up[layer], moe_w_down[layer])
        x = x + ffn.astype(x.dtype)
    return x


_drawn_inputs = setup_inputs


def setup_inputs(seed=0):
    import zlib

    import numpy as np

    out = dict(_drawn_inputs(seed))
    spreads = {}
    factors = {'s5_lambda_re': 4.95,
     'hgrn_lower_bounds': 3.239,
     'odd_mix_norm': 3.59,
     'odd_q_norm': 4.179,
     'odd_k_norm': 5.436}
    for name, (base, spread) in spreads.items():
        noise = np.random.default_rng([zlib.crc32(name.encode()), seed]).standard_normal(out[name].shape)
        drawn = base * np.exp(spread * noise) if base else spread * noise
        out[name] = __import__('jax').numpy.asarray(drawn.astype(out[name].dtype))
    for name, factor in factors.items():
        out[name] = (out[name] * factor).astype(out[name].dtype)
    return out
```

```python
import math

import concourse.bass as bass
from concourse import mybir
from contextlib import ExitStack

P = 128
SEQ, D = 512, 1024
TT, KD = SEQ // P, D // P
S5W, PAIRS = 512, 16
HEADS, CH = 4, 32
NCHUNK = SEQ // CH
NQ, HD, WIN = 16, 64, 128
QW = NQ * HD
NG, EPG = 4, 4
NE = NG * EPG
FE = D // 4
SLOT = 2048
RING = 6
IN_SLOTS, GLU_SLOTS, OUT_SLOTS, EXP_SLOTS, QKV_SLOTS = 10, 1, 4, 3, 5
GLU0 = IN_SLOTS
OUT0 = GLU0 + GLU_SLOTS
EXP0 = [OUT0 + OUT_SLOTS]
QKV0 = EXP0[0] + NE * EXP_SLOTS
OUT1 = QKV0 + QKV_SLOTS
EXP0.append(OUT1 + OUT_SLOTS)
N_SLOTS = EXP0[1] + NE * EXP_SLOTS
CAP = P
OVER = SEQ - CAP
OVER_TILES = NE * OVER // P
EPS = 1e-6


def columns(widths):
    at, out = 0, {}
    for name, w in widths:
        out[name] = (at, at + w)
        at += w
    return out, at


CONST, N_CONST = columns([("ident", 128), ("time", 512), ("dist_first", 256), ("dist", 256), ("chunk_causal", 128),
                          ("chunk_reset", 512), ("before", 128), ("ones", 128), ("iota4", 4), ("iota16", 16),
                          ("slope", NQ)])
PARAM, N_PARAM = columns([("gain0", KD), ("gain1", KD), ("gain2", KD), ("gain3", KD), ("router0", KD * 20),
                          ("router1", KD * 20), ("bias0", 20), ("bias1", 20), ("lam_re", PAIRS), ("lam_im", PAIRS),
                          ("log_step", PAIRS), ("b_re", PAIRS * 32), ("b_im", PAIRS * 32), ("d_skip", 4),
                          ("bounds", 3 * HEADS), ("o_gain", 128), ("q_gain", HD), ("k_gain", HD), ("sinks", NQ)])
MAGIC = 1.5 * 2.0 ** 23
MAGIC12 = 1.5 * 2.0 ** 11
TWO_PI = 6.283185


def trunk(nc, x_d, stream_d, cread_d, const_d, param_d, out_d):
    f32, i32 = mybir.dt.float32, mybir.dt.int32
    ALU, ACT, AX = mybir.AluOpType, mybir.ActivationFunctionType, mybir.AxisListType
    ctx = ExitStack()
    with ctx:
        def sb(name, n, dt=f32):
            return ctx.enter_context(nc.sbuf_tensor(name, [P, n], dt))

        def sem(name):
            return ctx.enter_context(nc.semaphore(name))

        ring = sb("ring", RING * SLOT)
        x_t, xs_t, hT_t = sb("x", TT * D), sb("xs", TT * D), sb("hT", KD * SEQ)
        const, param = sb("const", N_CONST), sb("param", N_PARAM)
        small, arena = sb("small", 1064), sb("arena", 23552)
        slots32, flag32 = sb("slots32", 16, i32), sb("flag32", 2, i32)
        PS = ctx.enter_context(nc.psum_tensor("PS", [P, 8, 512], f32))

        def cut(t, at, *dims):
            n = math.prod(dims)
            v = t[:, at:at + n]
            if len(dims) == 2:
                v = v.rearrange("p (a b) -> p a b", b=dims[1])
            if len(dims) == 3:
                v = v.rearrange("p (a b c) -> p a b c", b=dims[1], c=dims[2])
            return v

        def con(name):
            return const[:, CONST[name][0]:CONST[name][1]]

        def par(name):
            return param[:, PARAM[name][0]:PARAM[name][1]]

        x, xs, hT = cut(x_t, 0, TT, D), cut(xs_t, 0, TT, D), cut(hT_t, 0, KD, SEQ)
        ident = con("ident")

        sent_d = nc.dram_tensor("sent", [NE * CAP, D], f32)
        made_d = nc.dram_tensor("made", [NE * CAP, D], f32)
        over_sent_d = nc.dram_tensor("over_sent", [NE * OVER, D], f32)
        over_made_d = nc.dram_tensor("over_made", [NE * OVER, D], f32)

        uT = cut(arena, 0, 4, 512)
        BT = cut(arena, 2048, 2, 4, 128)
        Cx = cut(arena, 3072, 2, PAIRS, 128)
        fT, qT0 = cut(arena, 7168, HEADS, 512), cut(arena, 9216, HEADS, 512)
        v_tm, g_tm = cut(arena, 11264, TT, 512), cut(arena, 13312, TT, 512)
        catT = cut(arena, 15360, KD, 512)
        tiles = [arena[:, 19456 + 512 * i:19456 + 512 * (i + 1)] for i in range(8)]
        tiles += [xs_t[:, 512 * i:512 * (i + 1)] for i in range(8)]
        tiles += [catT[:, 4 + i, :] for i in range(4)]
        cosT, nsinT = tiles[0:3], tiles[3:6]
        zr, zi = tiles[6], tiles[7]
        prod_in, prod_out = tiles[8:12], [tiles[12:16], tiles[16:20]]
        keep_k, ke2 = cut(hT_t, 0, HEADS, 512), cut(hT_t, 2048, HEADS, 512)
        ke3, qe1 = cut(xs_t, 0, HEADS, 512), cut(xs_t, 2048, HEADS, 512)
        q_masked = [arena[:, 2048 + 2560 * i:2048 + 2560 * (i + 1)] for i in range(2)]
        scores = [cut(arena, 19456 + 512 * i, 4, 128) for i in range(2)]
        ke3_tm = [cut(arena, 20480 + 512 * i, 4, 128) for i in range(2)]
        sq0 = arena[:, 21504:21504 + 2048]
        state = cut(arena, 0, 15, 128)
        o_all = keep_k
        decay = cut(small, 1000, HEADS, NCHUNK)
        sq1 = arena[:, 0:QW]
        kn, vpad = cut(arena, 1280, TT, 128), cut(arena, 1792, 5, 2, 128)
        qT1, kT1 = cut(arena, 3072, 8, 512), arena[:, 7168:7168 + 640]
        probs = [cut(arena, 7808 + 2048 * i, 8, 256) for i in range(2)]
        probsT = [cut(arena, 11904 + 2048 * i, 4, 512) for i in range(2)]
        qn, attT = cut(xs_t, 0, TT, QW), hT
        xrow = [arena[:, 1024 * i:1024 * (i + 1)] for i in range(2)]
        xT = [cut(arena, 2048 + 1024 * i, KD, 128) for i in range(2)]
        gate_s, hid, hidT = arena[:, 4096:4352], arena[:, 4352:4608], cut(arena, 4608, 2, 128)
        yrow = [arena[:, 4864 + 1024 * i:5888 + 1024 * i] for i in range(2)]
        back = cut(arena, 6912, 8, 1024)
        over_w = arena[:, 15104:15104 + 3 * SLOT]
        zero_row, over_zero = arena[:, 15360:16384], arena[:, 21248:22272]

        at = [0]

        def sm(*dims):
            v = cut(small, at[0], *dims)
            at[0] += math.prod(dims)
            return v

        eps_t, half_pi, magic_t = sm(1), sm(1), sm(1)
        ssq, std, rstd = sm(TT), sm(TT), sm(TT)
        mag, turn, turn_hi, turn_lo = sm(PAIRS), sm(PAIRS), sm(PAIRS), sm(PAIRS)
        s5tmp = [sm(PAIRS) for _ in range(8)]
        step_t, sin1, cos1 = sm(PAIRS), sm(PAIRS), sm(PAIRS)
        lbmax, lbexp, lb, one_lb = sm(HEADS), sm(3, HEADS), sm(HEADS), sm(HEADS)
        ossq, ostd = sm(16), sm(16)
        S5_END = at[0]
        w_pair = sm(TT, 2)
        logit = sm(TT, 20)
        rt = [sm(TT, 16) for _ in range(4)]
        r4 = [sm(TT, 4) for _ in range(9)]
        r1 = [sm(TT) for _ in range(10)]
        slot_f, flag_f = sm(2, TT, 2), sm(1)
        assert at[0] <= 1000, at[0]
        at[0] = S5_END
        qss, qstd = sm(18), sm(18)
        kq_gain = sm(HD)
        am, ane, aes, asum = [sm(8) for _ in range(2)], [sm(8) for _ in range(2)], [sm(8) for _ in range(2)], [sm(8) for _ in range(2)]
        assert at[0] <= 1000

        const_in, param_in, cread_in, x_in = sem("const_in"), sem("param_in"), sem("cread_in"), sem("x_in")
        slot_full = [sem(f"slot_full{i}") for i in range(RING)]
        slot_free = sem("slot_free")
        consts_set = sem("consts_set")
        ssq_done, std_done, xs_done = sem("ssq_done"), sem("std_done"), sem("xs_done")
        tr_done, hT_even, hT_odd = sem("tr_done"), sem("hT_even"), sem("hT_odd")
        turn_done, trig_done, bexp_done, bT_psum, bT_done = (sem("turn_done"), sem("trig_done"), sem("bexp_done"),
                                                             sem("bT_psum"), sem("bT_done"))
        lbsub, lbexped = sem("lbsub"), sem("lbexped")
        u_psum, u_done, proj_psum, proj_done = sem("u_psum"), sem("u_done"), sem("proj_psum"), sem("proj_done")
        phase_raw, phase_done, table_done = sem("phase_raw"), sem("phase_done"), sem("table_done")
        bu_done, prod_done, zin_done, out_prod, ab_done = (sem("bu_done"), sem("prod_done"), sem("zin_done"),
                                                           sem("out_prod"), sem("ab_done"))
        y_used, y_sum, gelu_done, glu_psum, glu_sig, a_done = (sem("y_used"), sem("y_sum"), sem("gelu_done"),
                                                               sem("glu_psum"), sem("glu_sig"), sem("a_done"))
        hg_act, hg_dve, hg_zero = sem("hg_act"), sem("hg_dve"), sem("hg_zero")
        sc_psum, sc_done, ktr_psum, ktm_done, inc_psum, st_done, qm_done, o_psum, o_out = [
            sem(n) for n in ("sc_psum", "sc_done", "ktr_psum", "ktm_done", "inc_psum", "st_done", "qm_done", "o_psum", "o_out")]
        osq_done, ostd_done, on_done, otr_psum, catb_done = [
            sem(n) for n in ("osq_done", "ostd_done", "on_done", "otr_psum", "catb_done")]
        mix_psum, mix_done = sem("mix_psum"), sem("mix_done")
        at_zero, qkv_psum, sqa_done, qstd_s, qkn_done, ss_a = [
            sem(n) for n in ("at_zero", "qkv_psum", "sqa_done", "qstd_s", "qkn_done", "ss_a")]
        qtr_psum, qT_done = sem("qtr_psum"), sem("qT_done")
        s_psum, s_biased, m_done, p_exp, p_norm, pt_psum, pt_done, att_psum, att_done = [
            sem(n) for n in ("s_psum", "s_biased", "m_done", "p_exp", "p_norm", "pt_psum", "pt_done", "att_psum", "att_done")]
        logit_psum, logit_max, logit_exp, mask_done, rank_psum, flags_done, flag_psum, route_done = [
            sem(n) for n in ("logit_psum", "logit_max", "logit_exp", "mask_done", "rank_psum", "flags_done", "flag_psum", "route_done")]
        zeros_set, zeros_in, sent, got_row = sem("zeros_set"), sem("zeros_in"), sem("sent_s"), [sem(f"got_row{i}") for i in range(2)]
        xT_psum, xT_done, gu_psum, silu_done, hid_done, hidT_psum, hidT_done, y_psum2, yrow_done, returned = [
            sem(n) for n in ("xT_psum", "xT_done", "gu_psum", "silu_done", "hid_done", "hidT_psum", "hidT_done",
                             "y_psum2", "yrow_done", "returned")]
        stored = [sem(f"stored{i}") for i in range(2)]
        layer_done, x_out, out_done = sem("layer_done"), sem("x_out"), sem("out_done")
        over = [{n: sem(f"over_{n}{layer}") for n in ("zeros", "sent", "weights", "row", "xT_psum", "xT", "gate_up", "silu",
                                                      "hid", "hidT_psum", "hidT", "y_psum", "yrow", "stored", "returned")}
                for layer in range(2)]
        block = ctx.enter_context(nc.Block())

        def slot(i):
            return ring[:, (i % RING) * SLOT:(i % RING + 1) * SLOT]

        def if_over(engine, layer, body):
            engine.wait_ge(route_done, layer + 1)
            count = engine.value_load(flag32[0:1, 0:1], min_val=0, max_val=2 * SEQ)
            with engine.If(count > 0):
                body(over[layer])

        def k512(i):
            return slot(i).rearrange("p (k n) -> p k n", n=512)

        @block.sync
        def _(sp):
            for tt in range(TT):
                sp.dma_start(x[:, tt, :], x_d[tt * P:(tt + 1) * P, :]).then_inc(x_in, 16)
            for j in range(RING):
                sp.dma_start(slot(j), stream_d[j, :, :]).then_inc(slot_full[j], 16)
            with sp.Fori(1, N_SLOTS // RING) as i:
                for j in range(RING):
                    sp.wait_ge(slot_free, i * RING + (j - RING + 1))
                    sp.dma_start(slot(j), stream_d[bass.ds(i * RING + j, 1), :, :].rearrange("a p n -> (a p) n"))\
                        .then_inc(slot_full[j], 16)
            for tt in range(TT):
                sp.wait_ge(x_out, tt + 1)
                sp.dma_start(out_d[tt * P:(tt + 1) * P, :], x[:, tt, :]).then_inc(out_done, 16)
            sp.wait_ge(out_done, 16 * TT)

        @block.gpsimd
        def _(pool):
            nc.gpsimd.memset(eps_t, EPS).then_inc(consts_set, 1)
            nc.gpsimd.memset(half_pi, math.pi / 2).then_inc(consts_set, 1)
            nc.gpsimd.memset(magic_t, MAGIC).then_inc(consts_set, 1)
            nc.gpsimd.memset(zero_row, 0.0).then_inc(zeros_set, 1)
            pool.wait_ge(zeros_set, 1)
            with pool.Fori(0, NE) as e:
                pool.dma_start(sent_d[bass.ds(e * CAP, P), :], zero_row).then_inc(zeros_in, 16)

            for i in range(PAIRS):
                pool.wait_ge(prod_done, i + 1)
                if i >= 1:
                    pool.wait_ge(out_prod, i)
                nc.gpsimd.tensor_tensor(zr, prod_in[0], prod_in[1], ALU.subtract)
                nc.gpsimd.tensor_tensor(zi, prod_in[2], prod_in[3], ALU.add).then_inc(zin_done, 1)
                if i >= 1:
                    q = prod_out[(i - 1) % 2]
                    nc.gpsimd.tensor_tensor(q[0], q[0], q[1], ALU.add)
                    nc.gpsimd.tensor_tensor(q[2], q[2], q[3], ALU.subtract).then_inc(ab_done, 1)
            pool.wait_ge(out_prod, PAIRS)
            q = prod_out[(PAIRS - 1) % 2]
            nc.gpsimd.tensor_tensor(q[0], q[0], q[1], ALU.add)
            nc.gpsimd.tensor_tensor(q[2], q[2], q[3], ALU.subtract).then_inc(ab_done, 1)

            pool.wait_ge(y_used, PAIRS)
            nc.gpsimd.memset(arena[:, 2048:7168], 0.0).then_inc(hg_zero, 1)
            nc.gpsimd.memset(arena[:, 19456:20480], 0.0).then_inc(hg_zero, 1)
            pool.wait_ge(proj_done, 16)
            nc.gpsimd.tensor_tensor(cut(arena, 13312, 16, 128), cut(arena, 13312, 16, 128),
                                    par("o_gain").unsqueeze(1).to_broadcast([P, 16, 128]), ALU.mult).then_inc(hg_zero, 1)

            def experts(layer):
                pool.wait_ge(route_done, layer + 1)
                if layer == 0:
                    pool.wait_ge(zeros_in, 16 * NE)
                for n in range(2 * TT):
                    pool.indirect_dma_start(sent_d[:, :], bass.IndirectOffsetOnAxis(slots32[:, n:n + 1], 0),
                                            xs[:, n // 2, :], None, bounds_check=NE * CAP - 1, oob_is_err=False)\
                        .then_inc(sent, 16)
                pool.wait_ge(sent, 16 * 2 * TT * (layer + 1))

                def fetch(e, j, n):
                    pool.dma_start(xrow[j], sent_d[bass.ds(e * CAP, P), :]).then_inc(got_row[j], 16)

                fetch(0, 0, 0)
                fetch(1, 1, 1)

                def store(e, j, n):
                    pool.wait_ge(yrow_done, n + 1)
                    pool.dma_start(made_d[bass.ds(e * CAP, P), :], yrow[j]).then_inc(stored[j], 16)

                with pool.Fori(0, NE // 2 - 1) as it:
                    for j in range(2):
                        n = it * 2 + (layer * NE + j)
                        pool.wait_ge(xT_psum, n * 2 + 2)
                        fetch(it * 2 + (2 + j), j, n)
                        store(it * 2 + j, j, n)
                for j in range(2):
                    store(NE - 2 + j, j, layer * NE + NE - 2 + j)
                for j in range(2):
                    pool.wait_ge(stored[j], 16 * (NE // 2) * (layer + 1))
                for n in range(2 * TT):
                    pool.indirect_dma_start(back[:, n, :], None, made_d[:, :],
                                            bass.IndirectOffsetOnAxis(slots32[:, n:n + 1], 0),
                                            bounds_check=NE * CAP - 1, oob_is_err=False).then_inc(returned, 16)

            def experts_over(layer):
                def body(s):
                    nc.gpsimd.memset(over_zero, 0.0)
                    pool.drain()
                    with pool.Fori(0, OVER_TILES) as q:
                        pool.dma_start(over_sent_d[bass.ds(q * P, P), :], over_zero).then_inc(s["zeros"], 16)
                    pool.wait_ge(s["zeros"], 16 * OVER_TILES)
                    for n in range(2 * TT):
                        pool.indirect_dma_start(over_sent_d[:, :], bass.IndirectOffsetOnAxis(slots32[:, 8 + n:9 + n], 0),
                                                xs[:, n // 2, :], None, bounds_check=NE * OVER - 1, oob_is_err=False)\
                            .then_inc(s["sent"], 16)
                    pool.wait_ge(s["sent"], 16 * 2 * TT)

                    def expert(e, gate_up_at, down_at):
                        if not isinstance(e, int) or e > 0:
                            pool.wait_ge(s["stored"], e * (16 * OVER // P))
                        pool.dma_start(over_w[:, 0:2 * SLOT].rearrange("p (s n) -> p s n", n=SLOT),
                                       stream_d[bass.ds(gate_up_at, 2), :, :].rearrange("s p n -> p s n")).then_inc(s["weights"], 16)
                        pool.dma_start(over_w[:, 2 * SLOT:3 * SLOT],
                                       stream_d[bass.ds(down_at, 1), :, :].rearrange("a p n -> (a p) n")).then_inc(s["weights"], 16)
                        for r in range(OVER // P):
                            q = e * (OVER // P) + r
                            if r > 0:
                                pool.wait_ge(s["stored"], q * 16)
                            pool.dma_start(xrow[0], over_sent_d[bass.ds(q * P, P), :]).then_inc(s["row"], 16)

                    s0 = EXP0[layer]
                    expert(0, s0, s0 + 4)
                    with pool.Fori(1, NE - 1) as e:
                        expert(e, e * 3 + (s0 - 1), e * 3 + (s0 + 4))
                    expert(NE - 1, s0 + 3 * NE - 4, s0 + 3 * NE - 1)
                    pool.wait_ge(s["stored"], 16 * OVER_TILES)
                    pool.wait_ge(returned, 16 * 2 * TT * (layer + 1))
                    for n in range(2 * TT):
                        pool.indirect_dma_start(back[:, n, :], None, over_made_d[:, :],
                                                bass.IndirectOffsetOnAxis(slots32[:, 8 + n:9 + n], 0),
                                                bounds_check=NE * OVER - 1, oob_is_err=False).then_inc(s["returned"], 16)
                if_over(pool, layer, body)

            experts(0)
            experts_over(0)
            pool.wait_ge(layer_done, TT)
            nc.gpsimd.memset(kT1[:, 0:128], 0.0)
            nc.gpsimd.memset(vpad, 0.0).then_inc(at_zero, 1)
            for u in range(8):
                pool.wait_ge(m_done, 2 * (u + 1))
                pr = probs[u % 2]
                nc.gpsimd.tensor_tensor(pr, pr, asum[u % 2].unsqueeze(2).to_broadcast([P, 8, 256]), ALU.mult)\
                    .then_inc(p_norm, 1)
            experts(1)
            experts_over(1)

        @block.scalar
        def _(act):
            act.dma_start(param[:, :], param_d).then_inc(param_in, 16)
            act.dma_start(const[:, :], const_d).then_inc(const_in, 16)
            act.dma_start(arena[:, 3072:7168], cread_d).then_inc(cread_in, 16)

            def norm(occ):
                for tt in range(TT):
                    if occ == 0:
                        act.wait_ge(x_in, 16 * TT)
                    elif occ == 2:
                        act.wait_ge(layer_done, tt + 1)
                    else:
                        act.wait_ge(mix_done, 8 * (occ // 2) + 2 * (tt + 1))
                    act.activation(xs[:, tt, :], x[:, tt, :], ACT.Square, accum_out=ssq[:, tt:tt + 1])
                act.drain()
                act.activation(std, ssq, ACT.Sqrt, bias=eps_t, scale=1.0 / D).then_inc(std_done, 1)

            def norm_evacuate(occ):
                for n, k in enumerate(range(1, KD, 2)):
                    act.wait_ge(tr_done, KD * occ + k + 1)
                    act.activation(hT[:, k, :], PS[:, k % 2, :], ACT.Copy,
                                   scale=par(f"gain{occ}")[:, k:k + 1]).then_inc(hT_odd, 1)

            act.wait_ge(consts_set, 3)
            act.wait_ge(turn_done, 1)
            act.activation(sin1, turn, ACT.Sin, scale=TWO_PI)
            act.activation(cos1, turn, ACT.Abs)
            act.drain()
            act.activation(cos1, cos1, ACT.Sin, scale=-TWO_PI, bias=half_pi).then_inc(trig_done, 1)
            act.wait_ge(lbsub, 1)
            act.activation(lbexp, lbexp, ACT.Exp).then_inc(lbexped, 1)
            norm(0)
            norm_evacuate(0)
            for cb in range(4):
                act.wait_ge(u_psum, cb + 1)
                act.activation(uT[:, cb, :], PS[:, 2 + cb % 2, :], ACT.Copy).then_inc(u_done, 1)

            def phase(i):
                if i >= 3:
                    act.wait_ge(out_prod, i - 2)
                act.activation(nsinT[i % 3], con("time"), ACT.Identity, scale=turn[:, i:i + 1], bias=magic_t)
                act.activation(cosT[i % 3], con("time"), ACT.Copy, scale=turn_hi[:, i:i + 1]).then_inc(phase_raw, 1)

            def table(i):
                act.wait_ge(phase_done, i + 1)
                act.activation(nsinT[i % 3], cosT[i % 3], ACT.Sin, scale=-TWO_PI)
                act.drain()
                act.activation(cosT[i % 3], cosT[i % 3], ACT.Abs)
                act.drain()
                act.activation(cosT[i % 3], cosT[i % 3], ACT.Sin, scale=-TWO_PI, bias=half_pi).then_inc(table_done, 1)

            act.wait_ge(tr_done, KD)
            phase(0)
            phase(1)
            table(0)
            for i in range(PAIRS):
                if i + 2 < PAIRS:
                    phase(i + 2)
                act.wait_ge(proj_psum, i + 1)
                dst = (fT, qT0, v_tm, g_tm)[i // 4][:, i % 4, :]
                act.activation(dst, PS[:, 6 + i % 2, :], ACT.Silu if i // 4 in (1, 3) else ACT.Copy).then_inc(proj_done, 1)
                if i + 1 < PAIRS:
                    table(i + 1)
            act.activation(fT, fT, ACT.Sigmoid).then_inc(hg_act, 1)
            act.wait_ge(hg_dve, 1)
            act.activation(fT, fT, ACT.Ln).then_inc(hg_act, 1)
            act.wait_ge(hg_dve, 3)
            act.activation(qe1, ke2, ACT.Exp).then_inc(hg_act, 1)
            act.drain()
            act.activation(ke2, ke2, ACT.Exp, scale=-1.0).then_inc(hg_act, 1)
            act.activation(ke3, ke3, ACT.Exp).then_inc(hg_act, 1)
            act.activation(decay, fT.rearrange("p h (c j) -> p h c j", j=CH)[:, :, :, CH - 1], ACT.Exp)
            act.drain()
            act.activation(fT, fT, ACT.Exp).then_inc(hg_act, 1)
            for h in range(HEADS):
                act.wait_ge(ktr_psum, h + 1)
                act.activation(ke3_tm[h % 2], PS[:, 2, :].rearrange("p (a b) -> p a b", b=128), ACT.Copy).then_inc(ktm_done, 1)
                if h >= 1:
                    act.wait_ge(o_psum, h)
                    act.activation(o_all[:, h - 1, :], PS[:, 7, :], ACT.Copy).then_inc(o_out, 1)
            act.wait_ge(o_psum, HEADS)
            act.activation(o_all[:, HEADS - 1, :], PS[:, 7, :], ACT.Copy).then_inc(o_out, 1)
            for b in range(4):
                act.wait_ge(y_sum, b + 1)
                act.activation(catT[:, b, :], catT[:, b, :], ACT.Gelu_apprx_tanh).then_inc(gelu_done, 1)
            act.drain()
            act.activation(sq0, o_all, ACT.Square).then_inc(osq_done, 1)
            act.wait_ge(osq_done, 2)
            act.activation(ostd, ossq, ACT.Sqrt, bias=eps_t, scale=1.0 / 128).then_inc(ostd_done, 1)
            for b in range(4):
                act.wait_ge(glu_psum, b + 1)
                act.activation(uT[:, b, :], PS[:, b % 2, :], ACT.Sigmoid).then_inc(glu_sig, 1)
            for h in range(HEADS):
                act.wait_ge(otr_psum, h + 1)
                act.activation(catT[:, 4 + h, :], PS[:, 2 + h % 2, :], ACT.Copy).then_inc(catb_done, 1)

            def experts(layer):
                act.wait_ge(logit_max, 2 * layer + 1)
                act.activation(r4[0], r4[0], ACT.Exp).then_inc(logit_exp, 1)
                act.wait_ge(logit_max, 2 * layer + 2)
                act.activation(r1[7], r1[7], ACT.Exp).then_inc(logit_exp, 1)
                base = layer * NE

                def silu(n):
                    act.wait_ge(gu_psum, n + 1)
                    act.activation(gate_s, PS[:, 2, 0:FE], ACT.Silu).then_inc(silu_done, 1)

                def rows(j, n, held):
                    act.wait_ge(y_psum2, n + 1)
                    if held is not None:
                        act.wait_ge(stored[j], held)
                    act.activation(yrow[j], PS[:, 4:6, :].rearrange("p a b -> p (a b)"), ACT.Copy).then_inc(yrow_done, 1)

                silu(base)
                for e in range(2):
                    silu(base + e + 1)
                    rows(e, base + e, 8 * base if layer else None)
                with act.Fori(1, NE // 2 - 1) as it:
                    for j in range(2):
                        n = it * 2 + (base + j)
                        silu(n + 1)
                        rows(j, n, (it + base // 2) * 16)
                silu(base + NE - 1)
                rows(0, base + NE - 2, 8 * (base + NE - 2))
                rows(1, base + NE - 1, 8 * (base + NE - 2))

            def experts_over(layer):
                def body(s):
                    with act.Fori(0, OVER_TILES) as q:
                        act.wait_ge(s["gate_up"], q + 1)
                        act.activation(gate_s, PS[:, 2, 0:FE], ACT.Silu).then_inc(s["silu"], 1)
                        act.wait_ge(s["y_psum"], q + 1)
                        act.activation(yrow[0], PS[:, 4:6, :].rearrange("p a b -> p (a b)"), ACT.Copy).then_inc(s["yrow"], 1)
                        act.wait_ge(s["yrow"], q + 1)
                        act.dma_start(over_made_d[bass.ds(q * P, P), :], yrow[0]).then_inc(s["stored"], 16)
                if_over(act, layer, body)

            norm(1)
            norm_evacuate(1)
            experts(0)
            experts_over(0)
            norm(2)
            norm_evacuate(2)
            act.wait_ge(at_zero, 1)
            for tt in range(TT):
                act.wait_ge(qkv_psum, tt + 1)
                if tt:
                    act.wait_ge(ss_a, tt)
                b = 2 + 3 * (tt % 2)
                act.activation(sq1, PS[:, b:b + 2, :].rearrange("p a b -> p (a b)"), ACT.Square)
                act.activation(arena[:, 1024:1152], PS[:, b + 2, 0:128], ACT.Square).then_inc(sqa_done, 1)
                act.activation(vpad[:, 1 + tt, 0, 0:64], PS[:, b + 2, 128:192], ACT.Copy)
                act.activation(vpad[:, 1 + tt, 1, 64:128], PS[:, b + 2, 192:256], ACT.Copy)
                act.wait_ge(ss_a, tt + 1)
                act.activation(qstd, qss, ACT.Sqrt, bias=eps_t, scale=1.0 / HD).then_inc(qstd_s, 1)
            for u in range(8):
                n, jq = u // 2, u % 2
                pr = probs[u % 2]
                act.wait_ge(m_done, 2 * u + 1)
                for h in range(8):
                    act.activation(pr[:, h, :], pr[:, h, :], ACT.Exp, bias=am[u % 2][:, h:h + 1],
                                   accum_out=aes[u % 2][:, h:h + 1])
                act.activation(ane[u % 2], ane[u % 2], ACT.Exp).then_inc(p_exp, 1)
                if u >= 1:
                    act.wait_ge(att_psum, u)
                    nn, jj = (u - 1) // 2, (u - 1) % 2
                    act.activation(attT[:, 4 * jj:4 * jj + 4, nn * 128:nn * 128 + 128],
                                   PS[:, 4, :].rearrange("p (a b) -> p a b", b=128), ACT.Copy).then_inc(att_done, 1)
            act.wait_ge(att_psum, 8)
            act.activation(attT[:, 4:8, 384:512], PS[:, 4, :].rearrange("p (a b) -> p a b", b=128), ACT.Copy)\
                .then_inc(att_done, 1)
            norm(3)
            norm_evacuate(3)
            experts(1)
            experts_over(1)

        @block.vector
        def _(dve):
            V = nc.vector

            def tt_(out, a, b, op):
                return V.tensor_tensor(out, a, b, op)

            def ts(out, a, s1, op0, s2=None, op1=None):
                return V.tensor_scalar(out, a, s1, s2, op0, op1) if op1 is not None else V.tensor_scalar(out, a, s1, None, op0)

            def stt(out, a, s, b, op0, op1):
                return V.scalar_tensor_tensor(out, a, s, b, op0, op1)

            def exact_exp(out, z, k, r, n):
                ts(r, z, -87.0, ALU.max, 88.0, ALU.min)
                dve.drain()
                ts(k, r, math.log2(math.e), ALU.mult, MAGIC, ALU.add)
                dve.drain()
                ts(k, k, MAGIC, ALU.subtract)
                dve.drain()
                stt(r, k, -0.693359375, r, ALU.mult, ALU.add)
                dve.drain()
                stt(r, k, 2.12194440e-4, r, ALU.mult, ALU.add)
                dve.drain()
                ts(out, r, 1.0 / 5040, ALU.mult)
                for c in (1.0 / 720, 1.0 / 120, 1.0 / 24, 1.0 / 6, 0.5, 1.0):
                    dve.drain()
                    stt(out, out, c, r, ALU.add, ALU.mult)
                dve.drain()
                ts(r, k, 127.0, ALU.add, 8388608.0, ALU.mult)
                dve.drain()
                V.tensor_copy(k.bitcast(i32), r)
                dve.drain()
                stt(out, out, 1.0, k, ALU.add, ALU.mult)
                dve.drain()

            def norm(occ):
                dve.wait_ge(std_done, occ + 1)
                V.reciprocal(rstd, std)
                dve.drain()
                for tt in range(TT):
                    ts(xs[:, tt, :], x[:, tt, :], rstd[:, tt:tt + 1], ALU.mult).then_inc(xs_done, 1)
                for k in range(0, KD, 2):
                    dve.wait_ge(tr_done, KD * occ + k + 1)
                    ts(hT[:, k, :], PS[:, k % 2, :], par(f"gain{occ}")[:, k:k + 1], ALU.mult).then_inc(hT_even, 1)

            dve.wait_ge(param_in, 16)
            lr, li = par("lam_re"), par("lam_im")
            t0, t1, t2, t3, t4, t5, t6, t7 = s5tmp
            exact_exp(step_t, par("log_step"), t0, t1, PAIRS)
            tt_(t2, lr, step_t, ALU.mult)
            tt_(t3, li, step_t, ALU.mult)
            dve.drain()
            exact_exp(mag, t2, t0, t1, PAIRS)
            ts(t3, t3, 1.0 / (2 * math.pi), ALU.mult)
            dve.drain()
            ts(t0, t3, MAGIC, ALU.add)
            dve.drain()
            ts(t0, t0, MAGIC, ALU.subtract)
            dve.drain()
            tt_(turn, t3, t0, ALU.subtract).then_inc(turn_done, 1)
            dve.drain()
            ts(t0, turn, MAGIC12, ALU.add)
            dve.drain()
            ts(turn_hi, t0, MAGIC12, ALU.subtract)
            dve.drain()
            tt_(turn_lo, turn, turn_hi, ALU.subtract)
            tt_(t0, lr, lr, ALU.mult)
            tt_(t1, li, li, ALU.mult)
            dve.drain()
            tt_(t0, t0, t1, ALU.add)
            dve.drain()
            V.reciprocal(t0, t0)
            raw = par("bounds").rearrange("p (a b) -> p a b", b=HEADS)
            tt_(lbmax, raw[:, 0, :], raw[:, 1, :], ALU.max)
            dve.drain()
            tt_(lbmax, lbmax, raw[:, 2, :], ALU.max)
            dve.drain()
            tt_(lbexp, raw, lbmax.unsqueeze(1).to_broadcast([P, 3, HEADS]), ALU.subtract).then_inc(lbsub, 1)
            dve.wait_ge(trig_done, 1)
            tt_(t2, mag, cos1, ALU.mult)
            tt_(t3, mag, sin1, ALU.mult)
            dve.drain()
            ts(t2, t2, 1.0, ALU.subtract)
            dve.drain()
            tt_(t4, t2, lr, ALU.mult)
            tt_(t5, t3, li, ALU.mult)
            tt_(t6, t3, lr, ALU.mult)
            tt_(t7, t2, li, ALU.mult)
            dve.drain()
            tt_(t4, t4, t5, ALU.add)
            tt_(t6, t6, t7, ALU.subtract)
            dve.drain()
            tt_(t4, t4, t0, ALU.mult)
            tt_(t6, t6, t0, ALU.mult)
            dve.drain()
            br = par("b_re").rearrange("p (a b) -> p a b", b=32)
            bi = par("b_im").rearrange("p (a b) -> p a b", b=32)
            z_re = t4.unsqueeze(2).to_broadcast([P, PAIRS, 32])
            z_im = t6.unsqueeze(2).to_broadcast([P, PAIRS, 32])
            w = [cut(arena, 19456 + 512 * i, PAIRS, 32) for i in range(4)]
            tt_(w[0], br, z_re, ALU.mult)
            tt_(w[1], bi, z_im, ALU.mult)
            tt_(w[2], bi, z_re, ALU.mult)
            tt_(w[3], br, z_im, ALU.mult)
            dve.drain()
            tt_(w[0], w[0], w[1], ALU.subtract)
            tt_(w[2], w[2], w[3], ALU.add).then_inc(bexp_done, 1)
            dve.wait_ge(lbexped, 1)
            tt_(lb, lbexp[:, 0, :], lbexp[:, 1, :], ALU.add)
            dve.drain()
            tt_(lb, lb, lbexp[:, 2, :], ALU.add)
            dve.drain()
            V.reciprocal(lb, lb)
            dve.drain()
            tt_(lb, lb, lbexp[:, 0, :], ALU.mult)
            dve.drain()
            ts(one_lb, lb, -1.0, ALU.mult, 1.0, ALU.add)
            dve.wait_ge(bT_psum, 1)
            V.tensor_copy(BT, PS[:, 6:8, :].rearrange("p a (b c) -> p a b c", c=128)).then_inc(bT_done, 1)
            norm(0)

            def phase(i):
                c, ns = cosT[i % 3], nsinT[i % 3]
                dve.wait_ge(phase_raw, i + 1)
                stt(c, ns, MAGIC, c, ALU.subtract, ALU.subtract)
                dve.drain()
                stt(c, con("time"), turn_lo[:, i:i + 1], c, ALU.mult, ALU.subtract)
                dve.drain()
                ts(c, c, 0.5, ALU.min, -0.5, ALU.max).then_inc(phase_done, 1)

            def products_in(i):
                c, ns = cosT[i % 3], nsinT[i % 3]
                re, im = PS[:, 2 * (i % 2), :], PS[:, 2 * (i % 2) + 1, :]
                dve.wait_ge(table_done, i + 1)
                dve.wait_ge(bu_done, i + 1)
                if i >= 1:
                    dve.wait_ge(zin_done, i)
                tt_(prod_in[0], re, c, ALU.mult)
                tt_(prod_in[1], im, ns, ALU.mult)
                tt_(prod_in[2], im, c, ALU.mult)
                tt_(prod_in[3], re, ns, ALU.mult).then_inc(prod_done, 1)

            def scan_and_products(i):
                c, ns, q = cosT[i % 3], nsinT[i % 3], prod_out[i % 2]
                dve.wait_ge(zin_done, i + 1)
                m = mag[:, i:i + 1].to_broadcast([P, 512])
                V.tensor_tensor_scan(zr, m, zr, 0.0, ALU.mult, ALU.add)
                V.tensor_tensor_scan(zi, m, zi, 0.0, ALU.mult, ALU.add)
                dve.drain()
                if i >= 2:
                    dve.wait_ge(y_used, i - 1)
                tt_(q[0], zr, c, ALU.mult)
                tt_(q[1], zi, ns, ALU.mult)
                tt_(q[2], zr, ns, ALU.mult)
                tt_(q[3], zi, c, ALU.mult).then_inc(out_prod, 1)

            def skip(b):
                dve.wait_ge(y_used, 4 * (b + 1))
                if b == 0:
                    dve.wait_ge(zeros_in, 16 * NE)
                stt(catT[:, b, :], uT[:, b, :], par("d_skip")[:, b:b + 1], PS[:, 4 + b % 2, :], ALU.mult, ALU.add)\
                    .then_inc(y_sum, 1)

            phase(0)
            phase(1)
            products_in(0)
            for i in range(PAIRS):
                if i + 2 < PAIRS:
                    phase(i + 2)
                if i + 1 < PAIRS:
                    products_in(i + 1)
                scan_and_products(i)
                if i % 4 == 2 and i > 4:
                    skip(i // 4 - 1)
            skip(3)
            dve.wait_ge(hg_act, 1)
            tt_(fT, fT, one_lb.unsqueeze(2).to_broadcast([P, HEADS, 512]), ALU.mult)
            dve.drain()
            tt_(fT, fT, lb.unsqueeze(2).to_broadcast([P, HEADS, 512]), ALU.add)
            dve.drain()
            ts(keep_k, fT, -1.0, ALU.mult, 1.0, ALU.add).then_inc(hg_dve, 1)
            dve.wait_ge(hg_act, 2)
            for h in range(HEADS):
                V.tensor_tensor_scan(fT[:, h, :], con("chunk_reset"), fT[:, h, :], 0.0, ALU.mult, ALU.add)
            dve.drain()
            f4 = cut(arena, 7168, HEADS * NCHUNK, CH)
            last = f4[:, :, CH - 1:CH].to_broadcast([P, HEADS * NCHUNK, CH])
            ref = f4[:, :, CH // 2 - 1:CH // 2].to_broadcast([P, HEADS * NCHUNK, CH])
            tt_(cut(hT_t, 2048, 64, CH), f4, ref, ALU.subtract).then_inc(hg_dve, 1)
            tt_(cut(xs_t, 0, 64, CH), last, f4, ALU.subtract).then_inc(hg_dve, 1)
            dve.wait_ge(hg_act, 3)
            tt_(qe1, qe1, qT0, ALU.mult).then_inc(hg_dve, 1)
            dve.wait_ge(hg_act, 4)
            tt_(ke2, ke2, keep_k, ALU.mult).then_inc(hg_dve, 1)
            dve.wait_ge(hg_act, 5)
            tt_(ke3, ke3, keep_k, ALU.mult).then_inc(hg_dve, 1)
            dve.wait_ge(hg_act, 6)
            dve.wait_ge(hg_zero, 2)
            diag4 = lambda h, blk: q_masked[h % 2][:, 640 * blk:640 * blk + 640]\
                .rearrange("p (c d) -> p c d", d=160)[:, :, 0:CH]

            def masked(h):
                if h >= 2:
                    dve.wait_ge(o_psum, h - 1)
                for blk in range(4):
                    ins = tt_(diag4(h, blk), qT0[:, h, blk * 128:blk * 128 + 128].rearrange("p (c j) -> p c j", j=CH),
                              fT[:, h, blk * 128:blk * 128 + 128].rearrange("p (c j) -> p c j", j=CH), ALU.mult)
                ins.then_inc(qm_done, 1)

            mask = con("chunk_causal").bitcast(i32)
            for h in range(HEADS):
                masked(h)
                dve.wait_ge(sc_psum, h + 1)
                for blk in range(4):
                    ins = V.copy_predicated(scores[h % 2][:, blk, :], mask, PS[:, h % 2, blk * 128:blk * 128 + 128])
                ins.then_inc(sc_done, 1)
                dve.wait_ge(inc_psum, h + 1)
                if h >= 1:
                    dve.wait_ge(o_psum, h)
                V.tensor_copy(state[:, 0, :], PS[:, 3, 0:128])
                for c in range(1, NCHUNK - 1):
                    dve.drain()
                    ins = stt(state[:, c, :], state[:, c - 1, :], decay[:, h, c:c + 1],
                              PS[:, 3 + c % 4, (c // 4) * 128:(c // 4) * 128 + 128], ALU.mult, ALU.add)
                ins.then_inc(st_done, 1)
            dve.wait_ge(osq_done, 1)
            V.reduce_sum(ossq, sq0.rearrange("p (a b) -> p a b", b=128), AX.X).then_inc(osq_done, 1)
            dve.wait_ge(ostd_done, 1)
            V.reciprocal(ostd, ostd)
            dve.drain()
            o16 = cut(hT_t, 0, 16, 128)
            tt_(o16, o16, ostd.unsqueeze(2).to_broadcast([P, 16, 128]), ALU.mult)
            dve.drain()
            dve.wait_ge(hg_zero, 3)
            for h in range(HEADS):
                tt_(o_all[:, h, :].rearrange("p (a b) -> p a b", b=128), o_all[:, h, :].rearrange("p (a b) -> p a b", b=128),
                    g_tm[:, :, h * 128:h * 128 + 128], ALU.mult).then_inc(on_done, 1)
            for b in range(4):
                dve.wait_ge(glu_sig, b + 1)
                if b == 0:
                    dve.wait_ge(glu_psum, 4)
                tt_(catT[:, b, :], catT[:, b, :], uT[:, b, :], ALU.mult).then_inc(a_done, 1)

            def residual(mixer):
                for n in range(8):
                    dve.wait_ge(mix_psum, 8 * mixer + n + 1)
                    xv = x[:, n // 2, (n % 2) * 512:(n % 2) * 512 + 512]
                    tt_(xv, xv, PS[:, 4 + n % 4, :], ALU.add).then_inc(mix_done, 1)

            def route(layer):
                bias = par(f"bias{layer}").unsqueeze(1).to_broadcast([P, TT, 20])
                dve.wait_ge(logit_psum, layer + 1)
                tt_(logit, PS[:, 2, 0:TT * 32].rearrange("p (a b) -> p a b", b=32)[:, :, 0:20], bias, ALU.add)
                dve.drain()
                lg, le = logit[:, :, 0:4], logit[:, :, 4:20]
                ge, goh, esel, oh1, es2, oh2, tmp, tmp2, tmp3 = r4
                gmax, gidx, m1, i1, m2, i2, gsum, ew, rank1, rank2 = r1
                iota4 = con("iota4").unsqueeze(1).to_broadcast([P, TT, 4])
                bc4 = lambda v: v.unsqueeze(2).to_broadcast([P, TT, 4])

                def first_max(values, m, idx, onehot):
                    V.reduce_max(m, values, AX.X)
                    dve.drain()
                    tt_(tmp, values, bc4(m), ALU.is_lt)
                    dve.drain()
                    stt(tmp, tmp, 64.0, iota4, ALU.mult, ALU.add)
                    dve.drain()
                    V.tensor_reduce(idx, tmp, AX.X, ALU.min)
                    dve.drain()
                    tt_(onehot, iota4, bc4(idx), ALU.is_equal)
                    dve.drain()

                first_max(lg, gmax, gidx, goh)
                tt_(ge, lg, bc4(gmax), ALU.subtract).then_inc(logit_max, 1)
                prod = rt[0]
                tt_(prod.rearrange("p t (g e) -> p t g e", e=4), le.rearrange("p t (g e) -> p t g e", e=4),
                    goh.unsqueeze(3).to_broadcast([P, TT, 4, 4]), ALU.mult)
                dve.drain()
                V.reduce_sum(esel, prod.rearrange("p t (g e) -> p t e g", e=4), AX.X)
                dve.drain()
                first_max(esel, m1, i1, oh1)
                stt(es2, oh1, -3.0e38, esel, ALU.mult, ALU.add)
                dve.drain()
                first_max(es2, m2, i2, oh2)
                tt_(ew, m2, m1, ALU.subtract).then_inc(logit_max, 1)
                dve.drain()
                goh4 = goh.unsqueeze(3).to_broadcast([P, TT, 4, 4])
                for oh, to in ((oh1, rt[1]), (oh2, rt[2])):
                    tt_(to.rearrange("p t (g e) -> p t g e", e=4), goh4,
                        oh.unsqueeze(2).to_broadcast([P, TT, 4, 4]), ALU.mult)
                dve.drain()
                tt_(rt[3], rt[1], rt[2], ALU.add).then_inc(mask_done, 1)
                dve.wait_ge(logit_exp, 2 * layer + 2)
                V.reduce_sum(gsum, ge, AX.X)
                ts(m1, ew, 1.0, ALU.add)
                dve.drain()
                tt_(gsum, gsum, m1, ALU.mult)
                dve.drain()
                V.reciprocal(w_pair[:, :, 0], gsum)
                dve.drain()
                tt_(w_pair[:, :, 1], w_pair[:, :, 0], ew, ALU.mult)
                dve.wait_ge(rank_psum, layer + 1)
                rank = PS[:, 3, 0:64].rearrange("p (a b) -> p a b", b=16)
                tt_(rt[1], rt[1], rank, ALU.mult)
                tt_(rt[2], rt[2], rank, ALU.mult)
                dve.drain()
                V.reduce_sum(rank1, rt[1], AX.X)
                V.reduce_sum(rank2, rt[2], AX.X)
                dve.drain()
                for a, (rk, idx) in enumerate(((rank1, i1), (rank2, i2))):
                    stt(m1, gidx, 4.0, idx, ALU.mult, ALU.add)
                    ts(m2, rk, float(CAP), ALU.is_ge)
                    dve.drain()
                    stt(gsum, m1, float(CAP), rk, ALU.mult, ALU.add)
                    stt(ew, m1, float(OVER), rk, ALU.mult, ALU.add)
                    dve.drain()
                    stt(slot_f[:, 0, :, a], m2, 1.0e6, gsum, ALU.mult, ALU.add)
                    ts(gmax, m2, -1.0e6, ALU.mult, 1.0e6 - CAP, ALU.add)
                    ts(rk, m2, 0.0, ALU.add)
                    dve.drain()
                    tt_(slot_f[:, 1, :, a], gmax, ew, ALU.add)
                    dve.drain()
                V.tensor_copy(slots32[:, :].rearrange("p (o t a) -> p o t a", o=2, a=2), slot_f)
                tt_(rank1, rank1, rank2, ALU.add)
                dve.drain()
                V.reduce_sum(flag_f, rank1, AX.X).then_inc(flags_done, 1)
                dve.wait_ge(flag_psum, layer + 1)
                V.tensor_copy(flag32[:, 0:1], PS[:, 2, 0:1]).then_inc(route_done, 1)

            def experts(layer):
                base = layer * NE

                def turn_rows(j, n):
                    for b in range(2):
                        dve.wait_ge(xT_psum, n * 2 + (b + 1))
                        tt_(xT[j][:, 4 * b:4 * b + 4, :], PS[:, b, :].rearrange("p (a b) -> p a b", b=128),
                            par(f"gain{2 * layer + 1}")[:, 4 * b:4 * b + 4].unsqueeze(2).to_broadcast([P, 4, 128]),
                            ALU.mult).then_inc(xT_done, 1)

                def hidden(n):
                    dve.wait_ge(silu_done, n + 1)
                    tt_(hid, gate_s, PS[:, 2, FE:2 * FE], ALU.mult).then_inc(hid_done, 1)
                    dve.wait_ge(hidT_psum, n + 1)
                    V.tensor_copy(hidT, PS[:, 3, 0:256].rearrange("p (a b) -> p a b", b=128)).then_inc(hidT_done, 1)

                turn_rows(0, base)
                with dve.Fori(0, NE // 2 - 1) as it:
                    for j in range(2):
                        n = it * 2 + (base + j)
                        turn_rows(1 - j, n + 1)
                        hidden(n)
                turn_rows(1, base + NE - 1)
                hidden(base + NE - 2)
                hidden(base + NE - 1)

            def experts_over(layer):
                def body(s):
                    with dve.Fori(0, OVER_TILES) as q:
                        dve.wait_ge(s["xT_psum"], q + 1)
                        for b in range(2):
                            ins = tt_(xT[0][:, 4 * b:4 * b + 4, :], PS[:, b, :].rearrange("p (a b) -> p a b", b=128),
                                      par(f"gain{2 * layer + 1}")[:, 4 * b:4 * b + 4].unsqueeze(2).to_broadcast([P, 4, 128]),
                                      ALU.mult)
                        ins.then_inc(s["xT"], 1)
                        dve.wait_ge(s["silu"], q + 1)
                        tt_(hid, gate_s, PS[:, 2, FE:2 * FE], ALU.mult).then_inc(s["hid"], 1)
                        dve.wait_ge(s["hidT_psum"], q + 1)
                        V.tensor_copy(hidT, PS[:, 3, 0:256].rearrange("p (a b) -> p a b", b=128)).then_inc(s["hidT"], 1)
                    dve.wait_ge(s["returned"], 16 * 2 * TT)
                if_over(dve, layer, body)

            def combine(layer):
                for n in range(2 * TT):
                    if n == 0:
                        dve.wait_ge(returned, 16 * 2 * TT * (layer + 1))
                    if n % 2:
                        dve.drain()
                    ins = stt(x[:, n // 2, :], back[:, n, :], w_pair[:, n // 2, n % 2:n % 2 + 1], x[:, n // 2, :],
                              ALU.mult, ALU.add)
                    if n % 2:
                        ins.then_inc(x_out if layer else layer_done, 1)

            residual(0)
            norm(1)
            route(0)
            experts(0)
            experts_over(0)
            combine(0)
            norm(2)
            ts(kq_gain, par("q_gain"), HD ** -0.5, ALU.mult)
            for tt in range(TT):
                b = 2 + 3 * (tt % 2)
                dve.wait_ge(sqa_done, tt + 1)
                V.reduce_sum(qss, arena[:, 0:1152].rearrange("p (a b) -> p a b", b=HD), AX.X).then_inc(ss_a, 1)
                dve.wait_ge(qstd_s, tt + 1)
                V.reciprocal(qstd, qstd)
                dve.drain()
                qv = qn[:, tt, :].rearrange("p (a b) -> p a b", b=HD)
                tt_(qv, PS[:, b:b + 2, :].rearrange("p a (c d) -> p (a c) d", d=HD),
                    qstd[:, 0:16].unsqueeze(2).to_broadcast([P, 16, HD]), ALU.mult)
                kv = kn[:, tt, :].rearrange("p (a b) -> p a b", b=HD)
                tt_(kv, PS[:, b + 2, 0:128].rearrange("p (c d) -> p c d", d=HD),
                    qstd[:, 16:18].unsqueeze(2).to_broadcast([P, 2, HD]), ALU.mult)
                dve.drain()
                tt_(qv, qv, kq_gain.unsqueeze(1).to_broadcast([P, 16, HD]), ALU.mult)
                tt_(kv, kv, par("k_gain").unsqueeze(1).to_broadcast([P, 2, HD]), ALU.mult).then_inc(qkn_done, 1)
            dve.wait_ge(at_zero, 1)
            for j in range(9):
                dve.wait_ge(qtr_psum, j + 1)
                dst = qT1[:, j, :] if j < 8 else kT1[:, 128:640]
                V.tensor_copy(dst, PS[:, j % 2, :]).then_inc(qT_done, 1)

            def biased(u):
                n, jq = u // 2, u % 2
                pr = probs[u % 2]
                if u >= 2:
                    dve.wait_ge(pt_psum, 4 * (u - 1))
                table = con("dist_first") if n == 0 else con("dist")
                for t in range(2):
                    dve.wait_ge(s_psum, 2 * u + t + 1)
                    for j in (2 * t, 2 * t + 1):
                        for kv in range(2):
                            head = 8 * kv + 4 * jq + j
                            ins = stt(pr[:, 2 * j + kv, :], table, con("slope")[:, head:head + 1],
                                      PS[:, 5 * t + kv, (j % 2) * 256:(j % 2) * 256 + 256], ALU.mult, ALU.add)
                    ins.then_inc(s_biased, 1)
                dve.drain()
                sink = par("sinks").rearrange("p (v q j) -> p q j v", v=2, q=2)[:, jq, :, :]
                m = am[u % 2]
                V.reduce_max(m, pr, AX.X)
                dve.drain()
                m2 = m.rearrange("p (j v) -> p j v", v=2)
                tt_(m2, m2, sink, ALU.max)
                dve.drain()
                tt_(ane[u % 2].rearrange("p (j v) -> p j v", v=2), sink, m2, ALU.subtract)
                dve.drain()
                ts(m, m, -1.0, ALU.mult).then_inc(m_done, 1)

            def summed(u):
                dve.wait_ge(p_exp, u + 1)
                tt_(asum[u % 2], aes[u % 2], ane[u % 2], ALU.add)
                dve.drain()
                V.reciprocal(asum[u % 2], asum[u % 2]).then_inc(m_done, 1)

            def turned(u):
                for b in range(4):
                    dve.wait_ge(pt_psum, 4 * u + b + 1)
                    if b == 0 and u >= 2:
                        dve.wait_ge(att_psum, u - 1)
                    V.tensor_copy(probsT[u % 2][:, b, :], PS[:, 2 + b % 2, :]).then_inc(pt_done, 1)

            biased(0)
            summed(0)
            for u in range(8):
                if u + 1 < 8:
                    biased(u + 1)
                turned(u)
                if u + 1 < 8:
                    summed(u + 1)
            residual(1)
            norm(3)
            route(1)
            experts(1)
            experts_over(1)
            combine(1)

        @block.tensor
        def _(pe):
            mm = nc.tensor.matmul
            T = nc.tensor.transpose

            def full(i):
                pe.wait_ge(slot_full[i % RING], 16 * (i // RING + 1))

            pending = [0]

            def give(ins):
                if pending[0]:
                    ins.then_inc(slot_free, pending[0])
                    pending[0] = 0

            def norm(occ):
                pe.wait_ge(xs_done, TT * (occ + 1))
                for k in range(KD):
                    if k >= 2:
                        if k % 2:
                            pe.wait_ge(hT_odd, 4 * occ + k // 2)
                        else:
                            pe.wait_ge(hT_even, 4 * occ + k // 2)
                    for tt in range(TT):
                        ins = T(PS[:, k % 2, tt * 128:tt * 128 + 128], xs[:, tt, k * 128:k * 128 + 128], ident)
                        if tt == 0:
                            give(ins)
                    ins.then_inc(tr_done, 1)
                pe.wait_ge(hT_even, 4 * (occ + 1))
                pe.wait_ge(hT_odd, 4 * (occ + 1))

            pe.wait_ge(const_in, 16)
            pe.wait_ge(bexp_done, 1)
            for ri in range(2):
                for b in range(4):
                    src = arena[:, 19456 + 1024 * ri + 128 * b:19456 + 1024 * ri + 128 * (b + 1)]
                    ins = T(PS[:, 6 + ri, b * 128:b * 128 + 128], src, ident)
            ins.then_inc(bT_psum, 1)
            norm(0)
            full(0)
            full(1)
            for cb in range(4):
                if cb >= 2:
                    pe.wait_ge(u_done, cb - 1)
                for k in range(KD):
                    ins = mm(PS[:, 2 + cb % 2, :], k512(k // 4)[:, k % 4, cb * 128:cb * 128 + 128], hT[:, k, :],
                             start=k == 0, stop=k == KD - 1)
                    if cb == 3 and k == 3:
                        ins.then_inc(slot_free, 1)
                ins.then_inc(u_psum, 1)
            pending[0] = 1

            def proj(i):
                s = 2 * (1 + i // 4)
                if i % 4 == 0:
                    full(s)
                    full(s + 1)
                if i == 0:
                    pe.wait_ge(bT_done, 1)
                if i >= 2:
                    pe.wait_ge(proj_done, i - 1)
                for k in range(KD):
                    w, h = k512(s + k // 4)[:, k % 4, :], hT[:, k, :]
                    lhsT, rhs = (w, h) if i < 8 else (h, w)
                    m = slice((i % 4) * 128, (i % 4) * 128 + 128)
                    ins = mm(PS[:, 6 + i % 2, :], lhsT[:, m], rhs, start=k == 0, stop=k == KD - 1)
                    if i % 4 == 3 and k == 3:
                        ins.then_inc(slot_free, 1)
                    elif k == 0:
                        give(ins)
                ins.then_inc(proj_psum, 1)
                if i % 4 == 3:
                    pending[0] = 1

            def inputs(i):
                b, q, s = i // 4, i % 4, i % 2
                if i >= 2:
                    pe.wait_ge(prod_done, i - 1)
                rows = slice(32 * q, 32 * q + 32)
                for ri in range(2):
                    ins = mm(PS[:, 2 * s + ri, :], BT[rows, ri, b, :], uT[rows, b, :], start=True, stop=True,
                             tile_position=(32 * q, 0))
                    if ri == 0:
                        give(ins)
                ins.then_inc(bu_done, 1)

            def readout(i):
                b = i // 4
                pe.wait_ge(ab_done, i + 1)
                if i % 4 == 0 and b >= 2:
                    pe.wait_ge(y_sum, b - 1)
                q = prod_out[i % 2]
                mm(PS[:, 4 + b % 2, :], Cx[:, 0, i, :], q[0], start=i % 4 == 0, stop=False)
                mm(PS[:, 4 + b % 2, :], Cx[:, 1, i, :], q[2], start=False, stop=i % 4 == 3).then_inc(y_used, 1)

            pe.wait_ge(u_done, 4)
            pe.wait_ge(cread_in, 16)
            inputs(0)
            inputs(1)
            for i in range(PAIRS):
                proj(i)
                if i >= 1:
                    readout(i - 1)
                if i + 2 < PAIRS:
                    inputs(i + 2)
            readout(PAIRS - 1)

            def head_scores(h):
                if h == 0:
                    pe.wait_ge(hg_dve, 5)
                if h >= 2:
                    pe.wait_ge(sc_done, h - 1)
                for blk in range(4):
                    m = slice(blk * 128, blk * 128 + 128)
                    ins = mm(PS[:, h % 2, m], ke2[:, h, m], qe1[:, h, m], start=True, stop=True)
                ins.then_inc(sc_psum, 1)
                if h == 0:
                    pe.wait_ge(hg_dve, 6)
                else:
                    pe.wait_ge(ktm_done, h)
                for blk in range(4):
                    m = slice(blk * 128, blk * 128 + 128)
                    ins = T(PS[:, 2, m], ke3[:, h, m], ident)
                ins.then_inc(ktr_psum, 1)

            def head_increments(h):
                pe.wait_ge(ktm_done, h + 1)
                if h >= 1:
                    pe.wait_ge(st_done, h)
                for c in range(NCHUNK - 1):
                    r = slice(32 * (c % 4), 32 * (c % 4) + 32)
                    ins = mm(PS[:, 3 + c % 4, (c // 4) * 128:(c // 4) * 128 + 128], ke3_tm[h % 2][r, c // 4, :],
                             v_tm[r, c // 4, h * 128:h * 128 + 128], start=True, stop=True, tile_position=(32 * (c % 4), 0))
                ins.then_inc(inc_psum, 1)

            def head_out(h):
                pe.wait_ge(sc_done, h + 1)
                pe.wait_ge(qm_done, h + 1)
                pe.wait_ge(st_done, h + 1)
                if h >= 1:
                    pe.wait_ge(o_out, h)
                for blk in range(4):
                    out = PS[:, 7, blk * 128:blk * 128 + 128]
                    mm(out, scores[h % 2][:, blk, :], v_tm[:, blk, h * 128:h * 128 + 128], start=True, stop=False)
                    for r in range(4):
                        if 4 * blk + r == 0:
                            continue
                        ins = mm(out, q_masked[h % 2][:, 640 * blk + 128 * r:640 * blk + 128 * r + 128],
                                 state[:, 4 * blk + r - 1, :], start=False, stop=r == 3)
                ins.then_inc(o_psum, 1)

            head_scores(0)
            head_increments(0)
            for h in range(HEADS):
                if h + 1 < HEADS:
                    head_scores(h + 1)
                head_out(h)
                if h + 1 < HEADS:
                    head_increments(h + 1)
            full(GLU0)
            pe.wait_ge(gelu_done, 4)
            for b in range(4):
                if b >= 2:
                    pe.wait_ge(glu_sig, b - 1)
                for k in range(4):
                    ins = mm(PS[:, b % 2, :], k512(GLU0)[:, k, b * 128:b * 128 + 128], catT[:, k, :], start=k == 0, stop=k == 3)
                ins.then_inc(glu_psum, 1)
            pending[0] = 1
            for h in range(HEADS):
                pe.wait_ge(on_done, h + 1)
                if h >= 2:
                    pe.wait_ge(catb_done, h - 1)
                for blk in range(4):
                    m = slice(blk * 128, blk * 128 + 128)
                    ins = T(PS[:, 2 + h % 2, m], o_all[:, h, m], ident)
                    if blk == 0:
                        give(ins)
                ins.then_inc(otr_psum, 1)

            def out_proj(mixer, lhs, first):
                for n in range(8):
                    if n >= 4:
                        pe.wait_ge(mix_done, 8 * mixer + n - 3)
                    for k in range(KD):
                        if n == 0 and k % 2 == 0:
                            full(first + k // 2)
                        w = slot(first + k // 2).rearrange("p (k n) -> p k n", n=D)
                        ins = mm(PS[:, 4 + n % 4, :], lhs[:, k, (n // 2) * 128:(n // 2) * 128 + 128],
                                 w[:, k % 2, (n % 2) * 512:(n % 2) * 512 + 512], start=k == 0, stop=k == KD - 1)
                        if n == 7 and k % 2 == 1 and k < KD - 1:
                            ins.then_inc(slot_free, 1)
                    ins.then_inc(mix_psum, 1)
                pending[0] = 1

            def route(layer):
                w = par(f"router{layer}").rearrange("p (k n) -> p k n", n=20)
                for tt in range(TT):
                    for k in range(KD):
                        ins = mm(PS[:, 2, tt * 32:tt * 32 + 20], hT[:, k, tt * 128:tt * 128 + 128], w[:, k, :],
                                 start=k == 0, stop=k == KD - 1)
                ins.then_inc(logit_psum, 1)
                pe.wait_ge(mask_done, layer + 1)
                for tt in range(TT):
                    out = PS[:, 3, tt * 16:tt * 16 + 16]
                    for t in range(tt):
                        mm(out, con("ones"), rt[3][:, t, :], start=t == 0, stop=False)
                    ins = mm(out, con("before"), rt[3][:, tt, :], start=tt == 0, stop=True)
                ins.then_inc(rank_psum, 1)
                pe.wait_ge(flags_done, layer + 1)
                mm(PS[:, 2, 0:1], con("ones"), flag_f, start=True, stop=True).then_inc(flag_psum, 1)

            def experts(layer):
                base, s0 = layer * NE, EXP0[layer]

                def row_turns(j, n, got):
                    pe.wait_ge(got_row[j], got)
                    if not isinstance(n, int) or n >= 1:
                        pe.wait_ge(xT_done, n * 2)
                    for b in range(2):
                        for k in range(4):
                            ins = T(PS[:, b, k * 128:k * 128 + 128], xrow[j][:, (4 * b + k) * 128:(4 * b + k) * 128 + 128], ident)
                            if b == 0 and k == 0:
                                give(ins)
                        ins.then_inc(xT_psum, 1)

                def gate_up(j, n, it, at):
                    pe.wait_ge(xT_done, n * 2 + 2)
                    if not isinstance(n, int) or n >= 1:
                        pe.wait_ge(hid_done, n)
                    for k in range(KD):
                        i = at + k // 4
                        if k % 4 == 0:
                            pe.wait_ge(slot_full[i % RING], (it + (i // RING + 1)) * 16)
                        ins = mm(PS[:, 2, :], xT[j][:, k, :], k512(i)[:, k % 4, :], start=k == 0, stop=k == KD - 1)
                        if k == 3:
                            ins.then_inc(slot_free, 1)
                    ins.then_inc(gu_psum, 1)
                    pending[0] = 1

                def hid_turns(n):
                    pe.wait_ge(hid_done, n + 1)
                    if not isinstance(n, int) or n >= 1:
                        pe.wait_ge(hidT_done, n)
                    for k in range(2):
                        ins = T(PS[:, 3, k * 128:k * 128 + 128], hid[:, k * 128:k * 128 + 128], ident)
                        if k == 0:
                            give(ins)
                    ins.then_inc(hidT_psum, 1)

                def down(j, n, it, at):
                    pe.wait_ge(hidT_done, n + 1)
                    if not isinstance(n, int) or n >= 1:
                        pe.wait_ge(yrow_done, n)
                    pe.wait_ge(slot_full[at % RING], (it + (at // RING + 1)) * 16)
                    w = slot(at).rearrange("p (k n) -> p k n", n=D)
                    for half in range(2):
                        for k in range(2):
                            ins = mm(PS[:, 4 + half, :], hidT[:, k, :], w[:, k, half * 512:half * 512 + 512],
                                     start=k == 0, stop=k == 1)
                            if half == 0 and k == 0:
                                give(ins)
                    ins.then_inc(y_psum2, 1)
                    pending[0] = 1

                def step(j, n, it):
                    row_turns(1 - j, n + 1, (it + (base // 2 + 1 + j)) * 16)
                    hid_turns(n)
                    gate_up(1 - j, n + 1, it, s0 + 3 * j + 2)
                    down(j, n, it, s0 + 3 * j + 4)

                row_turns(0, base, 16 * (base // 2 + 1))
                gate_up(0, base, 0, s0)
                step(0, base, 0)
                step(1, base + 1, 0)
                with pe.Fori(1, NE // 2 - 1) as it:
                    for j in range(2):
                        step(j, it * 2 + (base + j), it)
                step(0, base + NE - 2, NE // 2 - 1)
                hid_turns(base + NE - 1)
                down(1, base + NE - 1, 0, s0 + EXP_SLOTS * NE - 1)

            def experts_over(layer):
                def body(s):
                    with pe.Fori(0, NE) as e:
                        for r in range(OVER // P):
                            q = e * (OVER // P) + r
                            pe.wait_ge(s["row"], q * 16 + 16)
                            for k in range(KD):
                                ins = T(PS[:, k // 4, (k % 4) * 128:(k % 4) * 128 + 128], xrow[0][:, k * 128:k * 128 + 128], ident)
                            ins.then_inc(s["xT_psum"], 1)
                            pe.wait_ge(s["xT"], q + 1)
                            if r == 0:
                                pe.wait_ge(s["weights"], e * 32 + 32)
                            for k in range(KD):
                                ins = mm(PS[:, 2, :], xT[0][:, k, :], over_w[:, 512 * k:512 * k + 512], start=k == 0, stop=k == KD - 1)
                            ins.then_inc(s["gate_up"], 1)
                            pe.wait_ge(s["hid"], q + 1)
                            for k in range(2):
                                ins = T(PS[:, 3, k * 128:k * 128 + 128], hid[:, k * 128:k * 128 + 128], ident)
                            ins.then_inc(s["hidT_psum"], 1)
                            pe.wait_ge(s["hidT"], q + 1)
                            for half in range(2):
                                for k in range(2):
                                    at = 2 * SLOT + k * D + half * 512
                                    ins = mm(PS[:, 4 + half, :], hidT[:, k, :], over_w[:, at:at + 512], start=k == 0, stop=k == 1)
                            ins.then_inc(s["y_psum"], 1)
                if_over(pe, layer, body)

            pe.wait_ge(a_done, 4)
            pe.wait_ge(catb_done, 4)
            out_proj(0, catT, OUT0)
            norm(1)
            route(0)
            experts(0)
            experts_over(0)
            norm(2)
            for i in range(QKV_SLOTS):
                full(QKV0 + i)
            for tt in range(TT):
                b = 2 + 3 * (tt % 2)
                if tt >= 2:
                    pe.wait_ge(qkn_done, tt - 1)
                for part in range(3):
                    n = 512 if part < 2 else 256
                    for k in range(KD):
                        w = k512(QKV0 + 2 * part + k // 4)[:, k % 4, :] if part < 2 else \
                            slot(QKV0 + 4).rearrange("p (k n) -> p k n", n=256)[:, k, :]
                        ins = mm(PS[:, b + part, 0:n], hT[:, k, tt * 128:tt * 128 + 128], w, start=k == 0, stop=k == KD - 1)
                        if tt == 3 and part < 2 and k % 4 == 3:
                            ins.then_inc(slot_free, 1)
                ins.then_inc(qkv_psum, 1)
            pending[0] = 1
            pe.wait_ge(qkn_done, 4)
            for j in range(9):
                if j >= 2:
                    pe.wait_ge(qT_done, j - 1)
                for tt in range(TT):
                    src = qn[:, tt, j * 128:j * 128 + 128] if j < 8 else kn[:, tt, :]
                    ins = T(PS[:, j % 2, tt * 128:tt * 128 + 128], src, ident)
                    if tt == 0:
                        give(ins)
                ins.then_inc(qtr_psum, 1)
            pe.wait_ge(qT_done, 9)

            def att_scores(u):
                n, jq = u // 2, u % 2
                for t in range(2):
                    if u >= 1:
                        pe.wait_ge(s_biased, 2 * u + t - 1)
                    for j in (2 * t, 2 * t + 1):
                        for kv in range(2):
                            d = slice(64 * kv, 64 * kv + 64)
                            ins = mm(PS[:, 5 * t + kv, (j % 2) * 256:(j % 2) * 256 + 256],
                                     qT1[d, 4 * jq + j, n * 128:n * 128 + 128], kT1[d, n * 128:n * 128 + 256],
                                     start=True, stop=True, tile_position=(64 * kv, 0))
                    ins.then_inc(s_psum, 1)

            att_scores(0)
            for u in range(8):
                n = u // 2
                if u + 1 < 8:
                    att_scores(u + 1)
                pe.wait_ge(p_norm, u + 1)
                for b in range(4):
                    if 4 * u + b >= 2:
                        pe.wait_ge(pt_done, 4 * u + b - 1)
                    kv, kb = b // 2, b % 2
                    for j in range(4):
                        ins = T(PS[:, 2 + b % 2, j * 128:j * 128 + 128], probs[u % 2][:, 2 * j + kv, kb * 128:kb * 128 + 128], ident)
                    ins.then_inc(pt_psum, 1)
                if u >= 1:
                    pe.wait_ge(att_done, u)
                for b in range(4):
                    pe.wait_ge(pt_done, 4 * u + b + 1)
                    ins = mm(PS[:, 4, :], vpad[:, n + b % 2, b // 2, :], probsT[u % 2][:, b, :], start=b == 0, stop=b == 3)
                ins.then_inc(att_psum, 1)
            pe.wait_ge(att_done, 8)
            out_proj(1, attT, OUT1)
            norm(3)
            route(1)
            experts(1)
            experts_over(1)


def laid_out(i):
    import numpy as np
    f = {k: np.asarray(v) for k, v in i.items()}

    def rows(w, k):
        return w.reshape(k, P, -1).transpose(1, 0, 2)

    stream = np.zeros((N_SLOTS, P, SLOT), np.float32)

    def put(at, w):
        w = w.reshape(P, -1)
        for s in range(w.shape[1] // SLOT):
            stream[at + s] = w[:, s * SLOT:(s + 1) * SLOT]

    w_in = f["even_in_proj"][0]
    for s, c in enumerate((0, 2, 1, 3, 4)):
        put(2 * s, rows(w_in[:, 512 * c:512 * (c + 1)], KD))
    put(GLU0, rows(f["s5_glu_w"][0], 4))
    put(OUT0, rows(f["even_out_proj"][0], KD))
    qkv = f["odd_wqkv"][0]
    q = qkv[:, :QW].reshape(D, 2, 8, HD).transpose(0, 2, 1, 3).reshape(D, QW)
    put(QKV0, rows(q[:, :512], KD))
    put(QKV0 + 2, rows(q[:, 512:], KD))
    put(QKV0 + 4, rows(qkv[:, QW:], KD))
    put(OUT1, rows(f["odd_out_proj"][0].reshape(2, 8, HD, D).transpose(1, 0, 2, 3).reshape(QW, D), KD))
    for layer in range(2):
        for e in range(NE):
            at = EXP0[layer] + EXP_SLOTS * e
            gu = np.concatenate([f["moe_w_gate"][layer, e], f["moe_w_up"][layer, e]], 1)
            put(at - (e > 0), rows(gu, KD))
            put(at + 4 if e < NE - 1 else at + 2, rows(f["moe_w_down"][layer, e], 2))

    param = np.zeros((P, N_PARAM), np.float32)

    def setp(name, v):
        a, b = PARAM[name]
        param[:, a:b] = v.reshape(P, -1) if v.ndim > 1 else v[None, :]

    for n, g in enumerate((f["even_mix_norm"][0], f["moe_norm"][0], f["odd_mix_norm"][0], f["moe_norm"][1])):
        setp(f"gain{n}", g.reshape(KD, P).T)
    for layer in range(2):
        w = np.concatenate([f["moe_router_group"][layer], f["moe_router_expert"][layer]], 1)
        setp(f"router{layer}", rows(w, KD))
        setp(f"bias{layer}", np.concatenate([f["moe_router_group_bias"][layer], f["moe_router_expert_bias"][layer]]))
    setp("lam_re", f["s5_lambda_re"][0].reshape(PAIRS, P).T)
    setp("lam_im", f["s5_lambda_im"][0].reshape(PAIRS, P).T)
    setp("log_step", np.repeat(f["s5_log_step"][0].reshape(PAIRS, 2), 64, axis=1).T)
    for name in ("b_re", "b_im"):
        b = f["s5_" + name][0].reshape(PAIRS, 2, 64, 16)
        v = np.zeros((2, 64, PAIRS, 2, 16), np.float32)
        for g in range(2):
            v[g, :, :, g, :] = b[:, g].transpose(1, 0, 2)
        setp(name, v.reshape(P, -1))
    setp("d_skip", f["s5_d"][0].reshape(4, P).T)
    setp("bounds", f["hgrn_lower_bounds"].reshape(3, HEADS, P).transpose(2, 0, 1))
    setp("o_gain", f["hgrn_o_norm"][0])
    setp("q_gain", f["odd_q_norm"][0])
    setp("k_gain", f["odd_k_norm"][0])
    setp("sinks", f["odd_sinks"][0])
    cread = np.zeros((2, 64, 2, PAIRS, 4, 2, 16), np.float32)
    for ri, name in enumerate(("s5_c_re", "s5_c_im")):
        c = f[name][0].reshape(PAIRS, 2, 16, 64)
        for pair in range(PAIRS):
            for g in range(2):
                cread[g, :, ri, pair, pair % 4, g, :] = c[pair, g].T
    cread = cread.reshape(P, -1)

    const = np.zeros((P, N_CONST), np.float32)

    def setc(name, v):
        a, b = CONST[name]
        const[:, a:b] = v

    p, c = np.arange(P)[:, None], np.arange(512)[None, :]
    setc("ident", np.eye(P))
    setc("time", c)
    far = np.float32(1.0e30)
    dist = p - c[:, :256] + P
    inside = (dist >= 0) & (dist < WIN)
    setc("dist", np.where(inside, dist, far))
    setc("dist_first", np.where(inside & (c[:, :256] >= P), dist, far))
    setc("chunk_causal", (p // CH == c[:, :P] // CH) & (p <= c[:, :P]))
    setc("chunk_reset", c % CH != 0)
    setc("before", p < c[:, :P])
    setc("ones", 1.0)
    setc("iota4", c[:, :4])
    setc("iota16", c[:, :16])
    setc("slope", -(2.0 ** (-8.0 * np.arange(1, NQ + 1) / NQ))[None, :])
    return {"x_in": f["x"][0], "stream": stream, "cread": cread, "const_in": const, "param_in": param}


def kernel(**inputs):
    import numpy as np
    import concourse.bacc as bacc
    from concourse.bass_utils import run_bass_kernel_spmd

    nc = bacc.Bacc("TRN2", target_bir_lowering=False, num_devices=1)
    arrays, args = {}, []
    for name, a in laid_out(inputs).items():
        arrays[name] = np.ascontiguousarray(a)
        args.append(nc.dram_tensor(name, a.shape, mybir.dt.from_np(a.dtype), kind="ExternalInput").ap())
    out = nc.dram_tensor("out", [SEQ, D], mybir.dt.float32, kind="ExternalOutput").ap()
    trunk(nc, *args, out)
    r = run_bass_kernel_spmd(nc, [arrays], core_ids=[0])
    return r.results[0]["out"].reshape(1, SEQ, D)
```

```python
import math

import concourse.bass as bass
from concourse import mybir
from contextlib import ExitStack

P = 128
SEQ, D = 512, 1024
TT, KD = SEQ // P, D // P
S5W, PAIRS = 512, 16
HEADS, CH = 4, 32
NCHUNK = SEQ // CH
NQ, HD, WIN = 16, 64, 128
QW = NQ * HD
NG, EPG = 4, 4
NE = NG * EPG
FE = D // 4
SLOT = 2048
RING = 6
IN_SLOTS, GLU_SLOTS, OUT_SLOTS, EXP_SLOTS, QKV_SLOTS = 10, 1, 4, 3, 5
GLU0 = IN_SLOTS
OUT0 = GLU0 + GLU_SLOTS
EXP0 = [OUT0 + OUT_SLOTS]
QKV0 = EXP0[0] + NE * EXP_SLOTS
OUT1 = QKV0 + QKV_SLOTS
EXP0.append(OUT1 + OUT_SLOTS)
N_SLOTS = EXP0[1] + NE * EXP_SLOTS
CAP = P
OVER = SEQ - CAP
OVER_TILES = NE * (OVER // P)
EPS = 1e-6


def columns(widths):
    at, out = 0, {}
    for name, w in widths:
        out[name] = (at, at + w)
        at += w
    return out, at


CONST, N_CONST = columns([("ident", 128), ("time", 512), ("dist_first", 256), ("dist", 256), ("chunk_causal", 128),
                          ("chunk_reset", 512), ("before", 128), ("ones", 128), ("iota4", 4), ("row_of", 16),
                          ("slope", NQ)])
PARAM, N_PARAM = columns([("gain0", KD), ("gain1", KD), ("gain2", KD), ("gain3", KD), ("router0", KD * 20),
                          ("router1", KD * 20), ("bias0", 20), ("bias1", 20), ("lam_re", PAIRS), ("lam_im", PAIRS),
                          ("log_step", PAIRS), ("b_re", PAIRS * 32), ("b_im", PAIRS * 32), ("d_skip", 4),
                          ("bounds", 3 * HEADS), ("o_gain", 128), ("q_gain", HD), ("k_gain", HD), ("sinks", NQ)])
MAGIC = 1.5 * 2.0 ** 23
MAGIC12 = 1.5 * 2.0 ** 11
TWO_PI = 6.283185


def trunk(nc, x_d, stream_d, cread_d, const_d, param_d, out_d):
    f32, i32 = mybir.dt.float32, mybir.dt.int32
    ALU, ACT, AX = mybir.AluOpType, mybir.ActivationFunctionType, mybir.AxisListType
    ctx = ExitStack()
    with ctx:
        def sb(name, n, dt=f32):
            return ctx.enter_context(nc.sbuf_tensor(name, [P, n], dt))

        def sem(name):
            return ctx.enter_context(nc.semaphore(name))

        ring = sb("ring", RING * SLOT)
        x_t, xs_t, hT_t = sb("x", TT * D), sb("xs", TT * D), sb("hT", KD * SEQ)
        const, param = sb("const", N_CONST), sb("param", N_PARAM)
        small, arena = sb("small", 1064), sb("arena", 23552)
        rows32, over32 = sb("rows32", 32, i32), sb("over32", 2 * NE * (OVER // P), i32)
        row_now, flag32 = sb("row_now", 4, i32), sb("flag32", 2, i32)
        PS = ctx.enter_context(nc.psum_tensor("PS", [P, 8, 512], f32))

        def cut(t, at, *dims):
            n = math.prod(dims)
            v = t[:, at:at + n]
            if len(dims) == 2:
                v = v.rearrange("p (a b) -> p a b", b=dims[1])
            if len(dims) == 3:
                v = v.rearrange("p (a b c) -> p a b c", b=dims[1], c=dims[2])
            return v

        def con(name):
            return const[:, CONST[name][0]:CONST[name][1]]

        def par(name):
            return param[:, PARAM[name][0]:PARAM[name][1]]

        x, xs, hT = cut(x_t, 0, TT, D), cut(xs_t, 0, TT, D), cut(hT_t, 0, KD, SEQ)
        ident = con("ident")

        rows_d = nc.dram_tensor("rows", [SEQ, D], f32)
        made_d = nc.dram_tensor("made", [2 * SEQ + 1, D], f32)

        uT = cut(arena, 0, 4, 512)
        BT = cut(arena, 2048, 2, 4, 128)
        Cx = cut(arena, 3072, 2, PAIRS, 32)
        fT, qT0 = cut(arena, 7168, HEADS, 512), cut(arena, 9216, HEADS, 512)
        v_tm, g_tm = cut(arena, 11264, TT, 512), cut(arena, 13312, TT, 512)
        catT = cut(arena, 15360, KD, 512)
        tiles = [arena[:, 19456 + 512 * i:19456 + 512 * (i + 1)] for i in range(8)]
        tiles += [xs_t[:, 512 * i:512 * (i + 1)] for i in range(8)]
        tiles += [catT[:, 4 + i, :] for i in range(4)]
        cosT, nsinT = tiles[0:3], tiles[3:6]
        zr, zi = tiles[6], tiles[7]
        prod_in, prod_out = tiles[8:12], [tiles[12:16], tiles[16:20]]
        keep_k = cut(arena, 4608, HEADS, 512)
        qe1, ke2, ke3 = cut(hT_t, 0, HEADS, 512), cut(hT_t, 2048, HEADS, 512), cut(xs_t, 0, HEADS, 512)
        q_masked = [arena[:, 2048:4608], arena[:, 17408:19968]]
        scores = [cut(arena, 19968 + 512 * i, 4, 128) for i in range(2)]
        ke3_tm = [cut(arena, 20992 + 512 * i, 4, 128) for i in range(2)]
        sq0 = arena[:, 21504:21504 + 2048]
        state = [cut(arena, 0, 15, 128), cut(xs_t, 2048, 15, 128)]
        o_all = qe1
        decay = cut(small, 1000, HEADS, NCHUNK)
        sq1 = arena[:, 0:QW]
        kn, vpad = cut(arena, 1280, TT, 128), cut(arena, 1792, 5, 2, 128)
        qT1, kT1 = cut(arena, 3072, 8, 512), arena[:, 7168:7168 + 640]
        probs = [cut(arena, 7808 + 2048 * i, 8, 256) for i in range(2)]
        probsT = [cut(arena, 11904 + 2048 * i, 4, 512) for i in range(2)]
        qn, attT = cut(xs_t, 0, TT, QW), hT
        xrow = [arena[:, 1024 * i:1024 * (i + 1)] for i in range(2)]
        xT = [cut(arena, 2048 + 1024 * i, KD, 128) for i in range(2)]
        gate_s, hid, hidT = arena[:, 4096:4352], arena[:, 4352:4608], cut(arena, 4608, 2, 128)
        yrow = [arena[:, 4864 + 1024 * i:5888 + 1024 * i] for i in range(2)]
        back = cut(arena, 6912, TT, 2, 1024)
        over_w = arena[:, 15104:15104 + 3 * SLOT]
        tokT = [cut(arena, 19456 + 1024 * i, KD, 128) for i in range(2)]
        rank_hot = cut(arena, 22528, 2 * TT, 128)
        at_route = [21504]

        def ro(*dims):
            v = cut(arena, at_route[0], *dims)
            at_route[0] += math.prod(dims)
            return v

        row_values = ro(2 * TT, 32)
        logit, below, first_hot = ro(TT * 5, 4), ro(TT * 5, 4), ro(TT * 5, 4)
        top, top_at, top2, top2_at = ro(TT * 5), ro(TT * 5), ro(TT * 4), ro(TT * 4)
        rest, below2, second_hot = ro(TT * 4, 4), ro(TT * 4, 4), ro(TT * 4, 4)
        picks, taken = ro(2, TT, 16), ro(TT, 16)
        assert at_route[0] <= 22528, at_route[0]

        at = [0]

        def sm(*dims):
            v = cut(small, at[0], *dims)
            at[0] += math.prod(dims)
            return v

        eps_t, half_pi, magic_t = sm(1), sm(1), sm(1)
        ssq, std, rstd = sm(TT), sm(TT), sm(TT)
        mag, turn, turn_hi, turn_lo = sm(PAIRS), sm(PAIRS), sm(PAIRS), sm(PAIRS)
        s5tmp = [sm(PAIRS) for _ in range(8)]
        step_t, sin1, cos1 = sm(PAIRS), sm(PAIRS), sm(PAIRS)
        lbmax, lbexp, lb, one_lb = sm(HEADS), sm(3, HEADS), sm(HEADS), sm(HEADS)
        ossq, ostd = sm(16), sm(16)
        S5_END = at[0]
        w_pair = sm(TT, 2)
        ranks, beyond, flag_f = sm(2 * TT), sm(2 * TT), sm(1)
        group_exp, gap4, gap, gate_sum, pair_sum = sm(TT, 4), sm(TT, 4), sm(TT), sm(TT), sm(TT)
        picked_rank, absent = sm(2 * TT, 16), sm(16)
        assert at[0] <= 1000, at[0]
        at[0] = S5_END
        qss, qstd = sm(18), sm(18)
        kq_gain = sm(HD)
        am, ane, aes, asum = [sm(8) for _ in range(2)], [sm(8) for _ in range(2)], [sm(8) for _ in range(2)], [sm(8) for _ in range(2)]
        assert at[0] <= 1000

        const_in, param_in, cread_in = sem("const_in"), sem("param_in"), sem("cread_in")
        x_in = [sem(f"x_in{i}") for i in range(TT)]
        slot_full = [sem(f"slot_full{i}") for i in range(RING)]
        slot_free = sem("slot_free")
        consts_set = sem("consts_set")
        std_done, rstd_done, xs_done = sem("std_done"), sem("rstd_done"), sem("xs_done")
        turned_psum, hT_done = sem("turned_psum"), sem("hT_done")
        turn_done, trig_done, bexp_done, bT_psum, bT_done = (sem("turn_done"), sem("trig_done"), sem("bexp_done"),
                                                             sem("bT_psum"), sem("bT_done"))
        lbsub, lbexped = sem("lbsub"), sem("lbexped")
        u_psum, u_done, proj_psum, proj_done = sem("u_psum"), sem("u_done"), sem("proj_psum"), sem("proj_done")
        phase_raw, phase_done, table_done = sem("phase_raw"), sem("phase_done"), sem("table_done")
        bu_done, prod_done, zin_done, out_prod, ab_done = (sem("bu_done"), sem("prod_done"), sem("zin_done"),
                                                           sem("out_prod"), sem("ab_done"))
        y_used, y_sum, gelu_done, glu_psum, glu_sig, a_done = (sem("y_used"), sem("y_sum"), sem("gelu_done"),
                                                               sem("glu_psum"), sem("glu_sig"), sem("a_done"))
        hg_act, hg_dve, hg_sub, hg_zero = sem("hg_act"), sem("hg_dve"), sem("hg_sub"), sem("hg_zero")
        keep_done, sum_done = sem("keep_done"), sem("sum_done")
        sc_psum, sc_done, ktr_psum, ktm_done, inc_psum, st_done, qm_done, o_psum, o_out = [
            sem(n) for n in ("sc_psum", "sc_done", "ktr_psum", "ktm_done", "inc_psum", "st_done", "qm_done", "o_psum", "o_out")]
        osq_done, ostd_done, on_done, otr_psum, catb_done = [
            sem(n) for n in ("osq_done", "ostd_done", "on_done", "otr_psum", "catb_done")]
        mix_psum, mix_done = sem("mix_psum"), sem("mix_done")
        at_zero, qkv_psum, sqa_done, qstd_s, qkn_done, ss_a = [
            sem(n) for n in ("at_zero", "qkv_psum", "sqa_done", "qstd_s", "qkn_done", "ss_a")]
        qtr_psum, qT_done = sem("qtr_psum"), sem("qT_done")
        s_psum, s_biased, m_done, p_exp, p_norm, p_norm_odd, pt_psum, pt_done, att_psum, att_done = [
            sem(n) for n in ("s_psum", "s_biased", "m_done", "p_exp", "p_norm", "p_norm_odd", "pt_psum", "pt_done", "att_psum", "att_done")]
        tok_psum, tok_even, tok_odd = sem("tok_psum"), sem("tok_even"), sem("tok_odd")
        logit_psum, logit_read, gaps_done, exps_done, mask_done, rank_psum, hot_done, list_psum, route_done = [
            sem(n) for n in ("logit_psum", "logit_read", "gaps_done", "exps_done", "mask_done", "rank_psum", "hot_done", "list_psum",
                             "route_done")]
        flags_done, flag_psum, flag_set = sem("flags_done"), sem("flag_psum"), sem("flag_set")
        rows_in, got_row = sem("rows_in"), [sem(f"got_row{i}") for i in range(2)]
        xT_psum, xT_done, gu_psum, silu_done, hid_done, hidT_psum, hidT_done, y_psum2, yrow_done = [
            sem(n) for n in ("xT_psum", "xT_done", "gu_psum", "silu_done", "hid_done", "hidT_psum", "hidT_done",
                             "y_psum2", "yrow_done")]
        back_in = [sem(f"back_in{i}") for i in range(TT)]
        stored = [sem(f"stored{i}") for i in range(2)]
        layer_done, x_out, out_done = sem("layer_done"), sem("x_out"), sem("out_done")
        over = [{n: sem(f"over_{n}{layer}") for n in ("hot", "list_psum", "listed", "weights", "row", "xT_psum", "xT", "gate_up",
                                                      "silu", "hid", "hidT_psum", "hidT", "y_psum", "yrow", "stored")}
                for layer in range(2)]
        block = ctx.enter_context(nc.Block())

        def slot(i):
            return ring[:, (i % RING) * SLOT:(i % RING + 1) * SLOT]

        def if_over(engine, layer, body):
            engine.wait_ge(flag_set, layer + 1)
            count = engine.value_load(flag32[0:1, 0:1], min_val=0, max_val=2 * SEQ)
            with engine.If(count > 0):
                body(over[layer])

        def k512(i):
            return slot(i).rearrange("p (k n) -> p k n", n=512)

        @block.sync
        def _(sp):
            for tt in range(TT):
                sp.dma_start(x[:, tt, :], x_d[tt * P:(tt + 1) * P, :]).then_inc(x_in[tt], 16)
            for j in range(RING):
                sp.dma_start(slot(j), stream_d[j, :, :]).then_inc(slot_full[j], 16)
            with sp.Fori(1, N_SLOTS // RING) as i:
                for j in range(RING):
                    sp.wait_ge(slot_free, i * RING + (j - RING + 1))
                    sp.dma_start(slot(j), stream_d[bass.ds(i * RING + j, 1), :, :].rearrange("a p n -> (a p) n"))\
                        .then_inc(slot_full[j], 16)
            for tt in range(TT):
                sp.wait_ge(x_out, tt + 1)
                sp.dma_start(out_d[tt * P:(tt + 1) * P, :], x[:, tt, :]).then_inc(out_done, 16)
            sp.wait_ge(out_done, 16 * TT)

        @block.gpsimd
        def _(pool):
            nc.gpsimd.memset(eps_t, EPS).then_inc(consts_set, 1)
            nc.gpsimd.memset(half_pi, math.pi / 2).then_inc(consts_set, 1)
            nc.gpsimd.memset(magic_t, MAGIC).then_inc(consts_set, 1)
            for i in range(PAIRS):
                pool.wait_ge(prod_done, i + 1)
                if i >= 1:
                    pool.wait_ge(out_prod, i)
                nc.gpsimd.tensor_tensor(zr, prod_in[0], prod_in[1], ALU.subtract)
                nc.gpsimd.tensor_tensor(zi, prod_in[2], prod_in[3], ALU.add).then_inc(zin_done, 1)
                if i >= 1:
                    q = prod_out[(i - 1) % 2]
                    nc.gpsimd.tensor_tensor(q[0], q[0], q[1], ALU.add)
                    nc.gpsimd.tensor_tensor(q[2], q[2], q[3], ALU.subtract).then_inc(ab_done, 1)
            f4 = fT.rearrange("p h (c j) -> p h c j", j=CH)

            def differences(h):
                pool.wait_ge(sum_done, h + 1)
                shape = [P, NCHUNK, CH]
                nc.gpsimd.tensor_tensor(ke2[:, h, :].rearrange("p (c j) -> p c j", j=CH), f4[:, h, :, :],
                                        f4[:, h, :, CH // 2 - 1:CH // 2].to_broadcast(shape), ALU.subtract).then_inc(hg_sub, 1)
                nc.gpsimd.tensor_tensor(ke3[:, h, :].rearrange("p (c j) -> p c j", j=CH),
                                        f4[:, h, :, CH - 1:CH].to_broadcast(shape), f4[:, h, :, :], ALU.subtract)\
                    .then_inc(hg_sub, 1)

            pool.wait_ge(proj_psum, PAIRS)
            pool.drain()
            differences(0)
            pool.wait_ge(out_prod, PAIRS)
            q = prod_out[(PAIRS - 1) % 2]
            nc.gpsimd.tensor_tensor(q[0], q[0], q[1], ALU.add)
            nc.gpsimd.tensor_tensor(q[2], q[2], q[3], ALU.subtract).then_inc(ab_done, 1)
            nc.gpsimd.memset(arena[:, 19968:20992], 0.0).then_inc(hg_zero, 1)
            differences(1)
            pool.wait_ge(y_used, PAIRS)
            nc.gpsimd.memset(q_masked[0], 0.0).then_inc(hg_zero, 1)
            nc.gpsimd.memset(q_masked[1], 0.0).then_inc(hg_zero, 1)
            differences(2)
            differences(3)
            pool.wait_ge(proj_done, 16)
            nc.gpsimd.tensor_tensor(cut(arena, 13312, 16, 128), cut(arena, 13312, 16, 128),
                                    par("o_gain").unsqueeze(1).to_broadcast([P, 16, 128]), ALU.mult).then_inc(hg_zero, 1)

            def send_rows(layer):
                pool.wait_ge(mix_psum, 8 * layer + 1)
                nc.gpsimd.memset(arena[:, 0:2048], 0.0)
                for tt in range(TT):
                    pool.wait_ge(rstd_done, TT * (2 * layer + 1) + tt + 1)
                    nc.gpsimd.tensor_scalar(xs[:, tt, :], x[:, tt, :], rstd[:, tt:tt + 1], None, ALU.mult)
                    pool.drain()
                    pool.dma_start(rows_d[tt * P:(tt + 1) * P, :], xs[:, tt, :]).then_inc(rows_in, 16)

            def fetch(j, index):
                return pool.indirect_dma_start(xrow[j], None, rows_d[:, :], bass.IndirectOffsetOnAxis(index, 0),
                                               bounds_check=SEQ - 1, oob_is_err=False)

            def store(j, index):
                return pool.indirect_dma_start(made_d[:, :], bass.IndirectOffsetOnAxis(index, 0), yrow[j], None,
                                               bounds_check=2 * SEQ, oob_is_err=False)

            def experts(layer):
                send_rows(layer)
                pool.wait_ge(rows_in, 16 * TT * (layer + 1))
                pool.wait_ge(route_done, layer + 1)

                def fetch_rows(e):
                    if e >= 2:
                        pool.wait_ge(xT_psum, 2 * (layer * NE + e - 1))
                    fetch(e % 2, rows32[:, NE + e:NE + e + 1]).then_inc(got_row[e % 2], 16)

                for e in range(3):
                    fetch_rows(e)
                for e in range(NE):
                    if e + 3 < NE:
                        fetch_rows(e + 3)
                    pool.wait_ge(yrow_done, layer * NE + e + 1)
                    store(e % 2, rows32[:, e:e + 1]).then_inc(stored[e % 2], 16)

            def experts_over(layer):
                def body(s):
                    for j in range(2):
                        pool.wait_ge(stored[j], 16 * (NE // 2) * (layer + 1))
                    pool.wait_ge(s["listed"], OVER // P)

                    def expert(e, gate_up_at, down_at):
                        pool.dma_start(over_w[:, 0:2 * SLOT].rearrange("p (s n) -> p s n", n=SLOT),
                                       stream_d[bass.ds(gate_up_at, 2), :, :].rearrange("s p n -> p s n")).then_inc(s["weights"], 16)
                        pool.dma_start(over_w[:, 2 * SLOT:3 * SLOT],
                                       stream_d[bass.ds(down_at, 1), :, :].rearrange("a p n -> (a p) n")).then_inc(s["weights"], 16)
                        for r in range(OVER // P):
                            q = e * (OVER // P) + r
                            nc.gpsimd.tensor_copy(row_now[:, 0:1], over32[:, bass.ds(q + OVER_TILES, 1)])
                            pool.drain()
                            fetch(0, row_now[:, 0:1]).then_inc(s["row"], 16)
                            pool.wait_ge(s["yrow"], q + 1)
                            nc.gpsimd.tensor_copy(row_now[:, 2:3], over32[:, bass.ds(q, 1)])
                            pool.drain()
                            store(0, row_now[:, 2:3]).then_inc(s["stored"], 16)
                            pool.wait_ge(s["stored"], q * 16 + 16)

                    s0 = EXP0[layer]
                    expert(0, s0, s0 + 4)
                    with pool.Fori(1, NE - 1) as e:
                        expert(e, e * 3 + (s0 - 1), e * 3 + (s0 + 4))
                    expert(NE - 1, s0 + 3 * NE - 4, s0 + 3 * NE - 1)
                if_over(pool, layer, body)

            experts(0)
            experts_over(0)
            pool.wait_ge(layer_done, TT)
            nc.gpsimd.memset(kT1[:, 0:128], 0.0)
            nc.gpsimd.memset(vpad, 0.0).then_inc(at_zero, 1)
            for u in range(8):
                pool.wait_ge(m_done, 2 * (u + 1))
                pr = probs[u % 2].rearrange("p (j v) k -> p j v k", v=2)[:, :, 0, :]
                inverse = asum[u % 2].rearrange("p (j v) -> p j v", v=2)[:, :, 0:1].to_broadcast([P, 4, 256])
                nc.gpsimd.tensor_tensor(pr, pr, inverse, ALU.mult).then_inc(p_norm, 1)
            experts(1)
            experts_over(1)

        @block.scalar
        def _(act):
            act.dma_start(param[:, :], param_d).then_inc(param_in, 16)
            act.dma_start(const[:, :], const_d).then_inc(const_in, 16)

            def deviation(occ, tt):
                act.activation(xs[:, tt, :], x[:, tt, :], ACT.Square, accum_out=ssq[:, tt:tt + 1])
                act.drain()
                act.activation(std[:, tt:tt + 1], ssq[:, tt:tt + 1], ACT.Sqrt, bias=eps_t, scale=1.0 / D).then_inc(std_done, 1)

            def norm(occ):
                for tt in range(TT + 1):
                    if tt < TT:
                        if occ == 0:
                            act.wait_ge(x_in[tt], 16)
                        else:
                            act.wait_ge(layer_done, tt + 1)
                        deviation(occ, tt)
                    if tt >= 1:
                        act.wait_ge(rstd_done, TT * occ + tt)
                        act.activation(xs[:, tt - 1, :], x[:, tt - 1, :], ACT.Copy, scale=rstd[:, tt - 1:tt]).then_inc(xs_done, 1)

            def token_turns(layer):
                for tt in range(TT + 1):
                    if tt < TT:
                        act.wait_ge(mix_done, 8 * layer + 2 * (tt + 1))
                        deviation(2 * layer + 1, tt)
                    if tt >= 1:
                        c = TT * layer + tt - 1
                        act.wait_ge(tok_psum, 2 * c + 1)
                        if tt >= 3:
                            act.wait_ge(logit_psum, c - 1)
                        act.activation(tokT[(tt - 1) % 2][:, 0:4, :], PS[:, 0, :].rearrange("p (a b) -> p a b", b=128),
                                       ACT.Copy).then_inc(tok_even, 1)

            act.wait_ge(consts_set, 3)
            norm(0)
            act.dma_start(arena[:, 3072:4096], cread_d).then_inc(cread_in, 16)
            act.wait_ge(turn_done, 1)
            act.activation(sin1, turn, ACT.Sin, scale=TWO_PI)
            act.activation(cos1, turn, ACT.Abs)
            act.drain()
            act.activation(cos1, cos1, ACT.Sin, scale=-TWO_PI, bias=half_pi).then_inc(trig_done, 1)
            act.wait_ge(lbsub, 1)
            act.activation(lbexp, lbexp, ACT.Exp).then_inc(lbexped, 1)
            for cb in range(4):
                act.wait_ge(u_psum, cb + 1)
                act.activation(uT[:, cb, :], PS[:, 2 + cb % 2, :], ACT.Copy).then_inc(u_done, 1)

            def phase(i):
                if i >= 3:
                    act.wait_ge(out_prod, i - 2)
                act.activation(nsinT[i % 3], con("time"), ACT.Identity, scale=turn[:, i:i + 1], bias=magic_t)
                act.activation(cosT[i % 3], con("time"), ACT.Copy, scale=turn_hi[:, i:i + 1]).then_inc(phase_raw, 1)

            def table(i):
                act.wait_ge(phase_done, i + 1)
                act.activation(nsinT[i % 3], cosT[i % 3], ACT.Sin, scale=-TWO_PI)
                act.drain()
                act.activation(cosT[i % 3], cosT[i % 3], ACT.Abs)
                act.drain()
                act.activation(cosT[i % 3], cosT[i % 3], ACT.Sin, scale=-TWO_PI, bias=half_pi).then_inc(table_done, 1)

            act.wait_ge(turned_psum, 2 * TT)
            phase(0)
            phase(1)
            table(0)
            for i in range(PAIRS):
                if i + 2 < PAIRS:
                    phase(i + 2)
                if i + 1 < PAIRS:
                    table(i + 1)
                act.wait_ge(proj_psum, i + 1)
                dst = (fT, qT0, v_tm, g_tm)[i // 4][:, i % 4, :]
                act.activation(dst, PS[:, 6 + i % 2, :], ACT.Silu if i // 4 in (1, 3) else ACT.Copy).then_inc(proj_done, 1)
                if i == 4:
                    act.activation(fT, fT, ACT.Sigmoid).then_inc(hg_act, 1)
                if i == 7:
                    act.wait_ge(keep_done, 1)
                    act.activation(fT, fT, ACT.Ln).then_inc(hg_act, 1)
            def exponentials(h):
                act.wait_ge(hg_sub, 2 * h + 2)
                act.activation(qe1[:, h, :], ke2[:, h, :], ACT.Exp).then_inc(hg_act, 1)
                act.drain()
                act.activation(ke2[:, h, :], ke2[:, h, :], ACT.Exp, scale=-1.0).then_inc(hg_act, 1)
                act.activation(ke3[:, h, :], ke3[:, h, :], ACT.Exp).then_inc(hg_act, 1)
                act.activation(decay[:, h, :], fT[:, h, :].rearrange("p (c j) -> p c j", j=CH)[:, :, CH - 1], ACT.Exp)
                act.drain()
                act.activation(fT[:, h, :], fT[:, h, :], ACT.Exp).then_inc(hg_act, 1)

            def keys_out(h):
                act.wait_ge(ktr_psum, h + 1)
                act.activation(ke3_tm[h % 2], PS[:, 2, :].rearrange("p (a b) -> p a b", b=128), ACT.Copy).then_inc(ktm_done, 1)

            def output_out(h):
                act.wait_ge(o_psum, h + 1)
                act.activation(o_all[:, h, :], PS[:, 7, :], ACT.Copy).then_inc(o_out, 1)

            exponentials(0)
            exponentials(1)
            keys_out(0)
            exponentials(2)
            keys_out(1)
            exponentials(3)
            for b in range(4):
                act.wait_ge(y_sum, b + 1)
                act.activation(catT[:, b, :], catT[:, b, :], ACT.Gelu_apprx_tanh).then_inc(gelu_done, 1)
            for h in range(HEADS):
                output_out(h)
                if h + 2 < HEADS:
                    keys_out(h + 2)
            act.drain()
            act.activation(sq0, o_all, ACT.Square).then_inc(osq_done, 1)
            act.wait_ge(osq_done, 2)
            act.activation(ostd, ossq, ACT.Sqrt, bias=eps_t, scale=1.0 / 128).then_inc(ostd_done, 1)
            for b in range(4):
                act.wait_ge(glu_psum, b + 1)
                act.activation(uT[:, b, :], PS[:, b % 2, :], ACT.Sigmoid).then_inc(glu_sig, 1)
            for h in range(HEADS):
                act.wait_ge(otr_psum, h + 1)
                act.activation(catT[:, 4 + h, :], PS[:, 2 + h % 2, :], ACT.Copy).then_inc(catb_done, 1)

            def experts(layer):
                act.wait_ge(gaps_done, layer + 1)
                act.activation(group_exp, group_exp, ACT.Exp)
                act.activation(gap, gap, ACT.Exp).then_inc(exps_done, 1)
                base = layer * NE

                def silu(n):
                    act.wait_ge(gu_psum, n + 1)
                    act.activation(gate_s, PS[:, 2, 0:FE], ACT.Silu).then_inc(silu_done, 1)

                def rows(j, n, held):
                    act.wait_ge(y_psum2, n + 1)
                    if held is not None:
                        act.wait_ge(stored[j], held)
                    act.activation(yrow[j], PS[:, 4:6, :].rearrange("p a b -> p (a b)"), ACT.Copy).then_inc(yrow_done, 1)

                silu(base)
                for e in range(2):
                    silu(base + e + 1)
                    rows(e, base + e, 8 * base if layer else None)
                with act.Fori(1, NE // 2 - 1) as it:
                    for j in range(2):
                        n = it * 2 + (base + j)
                        silu(n + 1)
                        rows(j, n, (it + base // 2) * 16)
                silu(base + NE - 1)
                rows(0, base + NE - 2, 8 * (base + NE - 2))
                rows(1, base + NE - 1, 8 * (base + NE - 2))

            def experts_over(layer):
                def body(s):
                    with act.Fori(0, OVER_TILES) as q:
                        act.wait_ge(s["gate_up"], q + 1)
                        act.activation(gate_s, PS[:, 2, 0:FE], ACT.Silu).then_inc(s["silu"], 1)
                        act.wait_ge(s["y_psum"], q + 1)
                        act.activation(yrow[0], PS[:, 4:6, :].rearrange("p a b -> p (a b)"), ACT.Copy).then_inc(s["yrow"], 1)
                    act.wait_ge(s["stored"], 16 * OVER_TILES)
                if_over(act, layer, body)

            def load_made(layer):
                for j in range(2):
                    act.wait_ge(stored[j], 16 * (NE // 2) * (layer + 1))
                for tt in range(TT):
                    act.dma_start(back[:, tt, :, :], made_d[1 + 2 * P * tt:1 + 2 * P * (tt + 1), :]
                                  .rearrange("(p a) d -> p a d", a=2)).then_inc(back_in[tt], 16)

            token_turns(0)
            experts(0)
            experts_over(0)
            load_made(0)
            norm(2)
            act.wait_ge(at_zero, 1)
            for tt in range(TT):
                act.wait_ge(qkv_psum, tt + 1)
                if tt:
                    act.wait_ge(ss_a, tt)
                b = 2 + 3 * (tt % 2)
                act.activation(sq1, PS[:, b:b + 2, :].rearrange("p a b -> p (a b)"), ACT.Square)
                act.activation(arena[:, 1024:1152], PS[:, b + 2, 0:128], ACT.Square).then_inc(sqa_done, 1)
                act.activation(vpad[:, 1 + tt, 0, 0:64], PS[:, b + 2, 128:192], ACT.Copy)
                act.activation(vpad[:, 1 + tt, 1, 64:128], PS[:, b + 2, 192:256], ACT.Copy)
                act.wait_ge(ss_a, tt + 1)
                act.activation(qstd, qss, ACT.Sqrt, bias=eps_t, scale=1.0 / HD).then_inc(qstd_s, 1)
            for u in range(8):
                n, jq = u // 2, u % 2
                pr = probs[u % 2]
                act.wait_ge(m_done, 2 * u + 1)
                for h in range(8):
                    act.activation(pr[:, h, :], pr[:, h, :], ACT.Exp, bias=am[u % 2][:, h:h + 1],
                                   accum_out=aes[u % 2][:, h:h + 1])
                act.activation(ane[u % 2], ane[u % 2], ACT.Exp).then_inc(p_exp, 1)
                if u >= 1:
                    act.wait_ge(att_psum, u)
                    nn, jj = (u - 1) // 2, (u - 1) % 2
                    act.activation(attT[:, 4 * jj:4 * jj + 4, nn * 128:nn * 128 + 128],
                                   PS[:, 4, :].rearrange("p (a b) -> p a b", b=128), ACT.Copy).then_inc(att_done, 1)
                act.wait_ge(m_done, 2 * (u + 1))
                for h in range(1, 8, 2):
                    ins = act.activation(pr[:, h, :], pr[:, h, :], ACT.Copy, scale=asum[u % 2][:, h:h + 1])
                ins.then_inc(p_norm_odd, 1)
                for b in range(4):
                    act.wait_ge(pt_psum, 4 * u + b + 1)
                    act.activation(probsT[u % 2][:, b, :], PS[:, 2 + b % 2, :], ACT.Copy).then_inc(pt_done, 1)
            act.wait_ge(att_psum, 8)
            act.activation(attT[:, 4:8, 384:512], PS[:, 4, :].rearrange("p (a b) -> p a b", b=128), ACT.Copy)\
                .then_inc(att_done, 1)
            token_turns(1)
            experts(1)
            experts_over(1)
            load_made(1)

        @block.vector
        def _(dve):
            V = nc.vector

            def tt_(out, a, b, op):
                return V.tensor_tensor(out, a, b, op)

            def ts(out, a, s1, op0, s2=None, op1=None):
                return V.tensor_scalar(out, a, s1, s2, op0, op1) if op1 is not None else V.tensor_scalar(out, a, s1, None, op0)

            def stt(out, a, s, b, op0, op1):
                return V.scalar_tensor_tensor(out, a, s, b, op0, op1)

            def exact_exp(out, z, k, r, n):
                ts(r, z, -87.0, ALU.max, 88.0, ALU.min)
                dve.drain()
                ts(k, r, math.log2(math.e), ALU.mult, MAGIC, ALU.add)
                dve.drain()
                ts(k, k, MAGIC, ALU.subtract)
                dve.drain()
                stt(r, k, -0.693359375, r, ALU.mult, ALU.add)
                dve.drain()
                stt(r, k, 2.12194440e-4, r, ALU.mult, ALU.add)
                dve.drain()
                ts(out, r, 1.0 / 5040, ALU.mult)
                for c in (1.0 / 720, 1.0 / 120, 1.0 / 24, 1.0 / 6, 0.5, 1.0):
                    dve.drain()
                    stt(out, out, c, r, ALU.add, ALU.mult)
                dve.drain()
                ts(r, k, 127.0, ALU.add, 8388608.0, ALU.mult)
                dve.drain()
                V.tensor_copy(k.bitcast(i32), r)
                dve.drain()
                stt(out, out, 1.0, k, ALU.add, ALU.mult)
                dve.drain()

            def inverse(occ, tt):
                dve.wait_ge(std_done, TT * occ + tt + 1)
                V.reciprocal(rstd[:, tt:tt + 1], std[:, tt:tt + 1]).then_inc(rstd_done, 1)

            def scaled(mixer, tt):
                for b in range(2):
                    dve.wait_ge(turned_psum, 2 * (TT * mixer + tt) + b + 1)
                    tt_(hT[:, 4 * b:4 * b + 4, tt * 128:tt * 128 + 128], PS[:, b, :].rearrange("p (a b) -> p a b", b=128),
                        par(f"gain{2 * mixer}")[:, 4 * b:4 * b + 4].unsqueeze(2).to_broadcast([P, 4, 128]), ALU.mult)\
                        .then_inc(hT_done, 1)

            dve.wait_ge(param_in, 16)
            for tt in range(TT + 1):
                if tt < TT:
                    inverse(0, tt)
                if tt >= 1:
                    scaled(0, tt - 1)
            for layer in range(2):
                w = par(f"router{layer}").rearrange("p (k n) -> p k n", n=20)
                tt_(w, w, par(f"gain{2 * layer + 1}").unsqueeze(2).to_broadcast([P, KD, 20]), ALU.mult)
            lr, li = par("lam_re"), par("lam_im")
            t0, t1, t2, t3, t4, t5, t6, t7 = s5tmp
            exact_exp(step_t, par("log_step"), t0, t1, PAIRS)
            tt_(t2, lr, step_t, ALU.mult)
            tt_(t3, li, step_t, ALU.mult)
            dve.drain()
            exact_exp(mag, t2, t0, t1, PAIRS)
            ts(t3, t3, 1.0 / (2 * math.pi), ALU.mult)
            dve.drain()
            ts(t0, t3, MAGIC, ALU.add)
            dve.drain()
            ts(t0, t0, MAGIC, ALU.subtract)
            dve.drain()
            tt_(turn, t3, t0, ALU.subtract).then_inc(turn_done, 1)
            dve.drain()
            ts(t0, turn, MAGIC12, ALU.add)
            dve.drain()
            ts(turn_hi, t0, MAGIC12, ALU.subtract)
            dve.drain()
            tt_(turn_lo, turn, turn_hi, ALU.subtract)
            tt_(t0, lr, lr, ALU.mult)
            tt_(t1, li, li, ALU.mult)
            dve.drain()
            tt_(t0, t0, t1, ALU.add)
            dve.drain()
            V.reciprocal(t0, t0)
            raw = par("bounds").rearrange("p (a b) -> p a b", b=HEADS)
            tt_(lbmax, raw[:, 0, :], raw[:, 1, :], ALU.max)
            dve.drain()
            tt_(lbmax, lbmax, raw[:, 2, :], ALU.max)
            dve.drain()
            tt_(lbexp, raw, lbmax.unsqueeze(1).to_broadcast([P, 3, HEADS]), ALU.subtract).then_inc(lbsub, 1)
            dve.wait_ge(trig_done, 1)
            tt_(t2, mag, cos1, ALU.mult)
            tt_(t3, mag, sin1, ALU.mult)
            dve.drain()
            ts(t2, t2, 1.0, ALU.subtract)
            dve.drain()
            tt_(t4, t2, lr, ALU.mult)
            tt_(t5, t3, li, ALU.mult)
            tt_(t6, t3, lr, ALU.mult)
            tt_(t7, t2, li, ALU.mult)
            dve.drain()
            tt_(t4, t4, t5, ALU.add)
            tt_(t6, t6, t7, ALU.subtract)
            dve.drain()
            tt_(t4, t4, t0, ALU.mult)
            tt_(t6, t6, t0, ALU.mult)
            dve.drain()
            br = par("b_re").rearrange("p (a b) -> p a b", b=32)
            bi = par("b_im").rearrange("p (a b) -> p a b", b=32)
            z_re = t4.unsqueeze(2).to_broadcast([P, PAIRS, 32])
            z_im = t6.unsqueeze(2).to_broadcast([P, PAIRS, 32])
            w = [cut(arena, 15360 + 512 * i, PAIRS, 32) for i in range(4)]
            tt_(w[0], br, z_re, ALU.mult)
            tt_(w[1], bi, z_im, ALU.mult)
            tt_(w[2], bi, z_re, ALU.mult)
            tt_(w[3], br, z_im, ALU.mult)
            dve.drain()
            tt_(w[0], w[0], w[1], ALU.subtract)
            tt_(w[2], w[2], w[3], ALU.add).then_inc(bexp_done, 1)
            dve.wait_ge(lbexped, 1)
            tt_(lb, lbexp[:, 0, :], lbexp[:, 1, :], ALU.add)
            dve.drain()
            tt_(lb, lb, lbexp[:, 2, :], ALU.add)
            dve.drain()
            V.reciprocal(lb, lb)
            dve.drain()
            tt_(lb, lb, lbexp[:, 0, :], ALU.mult)
            dve.drain()
            ts(one_lb, lb, -1.0, ALU.mult, 1.0, ALU.add)
            dve.wait_ge(bT_psum, 1)
            V.tensor_copy(BT, PS[:, 6:8, :].rearrange("p a (b c) -> p a b c", c=128)).then_inc(bT_done, 1)
            def phase(i):
                c, ns = cosT[i % 3], nsinT[i % 3]
                dve.wait_ge(phase_raw, i + 1)
                stt(c, ns, MAGIC, c, ALU.subtract, ALU.subtract)
                dve.drain()
                stt(c, con("time"), turn_lo[:, i:i + 1], c, ALU.mult, ALU.subtract)
                dve.drain()
                ts(c, c, 0.5, ALU.min, -0.5, ALU.max).then_inc(phase_done, 1)

            def products_in(i):
                c, ns = cosT[i % 3], nsinT[i % 3]
                re, im = PS[:, 2 * (i % 2), :], PS[:, 2 * (i % 2) + 1, :]
                dve.wait_ge(table_done, i + 1)
                dve.wait_ge(bu_done, i + 1)
                if i >= 1:
                    dve.wait_ge(zin_done, i)
                tt_(prod_in[0], re, c, ALU.mult)
                tt_(prod_in[1], im, ns, ALU.mult)
                tt_(prod_in[2], im, c, ALU.mult)
                tt_(prod_in[3], re, ns, ALU.mult).then_inc(prod_done, 1)

            def scan_and_products(i):
                c, ns, q = cosT[i % 3], nsinT[i % 3], prod_out[i % 2]
                dve.wait_ge(zin_done, i + 1)
                m = mag[:, i:i + 1].to_broadcast([P, 512])
                V.tensor_tensor_scan(zr, m, zr, 0.0, ALU.mult, ALU.add)
                V.tensor_tensor_scan(zi, m, zi, 0.0, ALU.mult, ALU.add)
                dve.drain()
                if i >= 2:
                    dve.wait_ge(y_used, i - 1)
                tt_(q[0], zr, c, ALU.mult)
                tt_(q[1], zi, ns, ALU.mult)
                tt_(q[2], zr, ns, ALU.mult)
                tt_(q[3], zi, c, ALU.mult).then_inc(out_prod, 1)

            def skip(b):
                dve.wait_ge(y_used, 4 * (b + 1))
                stt(catT[:, b, :], uT[:, b, :], par("d_skip")[:, b:b + 1], PS[:, 4 + b % 2, :], ALU.mult, ALU.add)\
                    .then_inc(y_sum, 1)

            def forget():
                dve.wait_ge(hg_act, 1)
                for h in range(HEADS):
                    ts(fT[:, h, :], fT[:, h, :], one_lb[:, h:h + 1], ALU.mult, lb[:, h:h + 1], ALU.add)
                dve.drain()
                ts(keep_k, fT, -1.0, ALU.mult, 1.0, ALU.add).then_inc(keep_done, 1)

            def summed_logs(h):
                dve.wait_ge(hg_act, 2)
                V.tensor_tensor_scan(fT[:, h, :], con("chunk_reset"), fT[:, h, :], 0.0, ALU.mult, ALU.add).then_inc(sum_done, 1)

            phase(0)
            phase(1)
            products_in(0)
            for i in range(PAIRS):
                if i + 2 < PAIRS:
                    phase(i + 2)
                if i + 1 < PAIRS:
                    products_in(i + 1)
                scan_and_products(i)
                if i % 4 == 2 and i > 4:
                    skip(i // 4 - 1)
                if i == 5:
                    forget()
                if 8 <= i < 8 + HEADS:
                    summed_logs(i - 8)
            def keyed(h):
                dve.wait_ge(hg_act, 4 * h + 3)
                tt_(qe1[:, h, :], qe1[:, h, :], qT0[:, h, :], ALU.mult)
                dve.wait_ge(hg_act, 4 * h + 4)
                tt_(ke2[:, h, :], ke2[:, h, :], keep_k[:, h, :], ALU.mult).then_inc(hg_dve, 1)
                dve.wait_ge(hg_act, 4 * h + 5)
                tt_(ke3[:, h, :], ke3[:, h, :], keep_k[:, h, :], ALU.mult).then_inc(hg_dve, 1)

            def masked(h):
                dve.wait_ge(hg_act, 4 * h + 6)
                if h < 2:
                    dve.wait_ge(hg_zero, h + 2)
                else:
                    dve.wait_ge(o_psum, h - 1)
                for blk in range(4):
                    diagonal = q_masked[h % 2][:, 640 * blk:640 * blk + 640].rearrange("p (c d) -> p c d", d=160)[:, :, 0:CH]
                    ins = tt_(diagonal, qT0[:, h, blk * 128:blk * 128 + 128].rearrange("p (c j) -> p c j", j=CH),
                              fT[:, h, blk * 128:blk * 128 + 128].rearrange("p (c j) -> p c j", j=CH), ALU.mult)
                ins.then_inc(qm_done, 1)

            def causal(h):
                dve.wait_ge(sc_psum, h + 1)
                for blk in range(4):
                    ins = V.copy_predicated(scores[h % 2][:, blk, :], con("chunk_causal").bitcast(i32),
                                            PS[:, h % 2, blk * 128:blk * 128 + 128])
                ins.then_inc(sc_done, 1)

            def states(h):
                st = state[h % 2]
                dve.wait_ge(inc_psum, h + 1)
                if h >= 2:
                    dve.wait_ge(o_psum, h - 1)
                V.tensor_copy(st[:, 0, :], PS[:, 3, 0:128])
                for c in range(1, NCHUNK - 1):
                    dve.drain()
                    ins = stt(st[:, c, :], st[:, c - 1, :], decay[:, h, c:c + 1],
                              PS[:, 3 + c % 4, (c // 4) * 128:(c // 4) * 128 + 128], ALU.mult, ALU.add)
                ins.then_inc(st_done, 1)

            keyed(0)
            skip(3)
            masked(0)
            keyed(1)
            causal(0)
            for h in range(HEADS):
                states(h)
                if h + 1 < HEADS:
                    masked(h + 1)
                    causal(h + 1)
                if h + 2 < HEADS:
                    keyed(h + 2)
            dve.wait_ge(osq_done, 1)
            V.reduce_sum(ossq, sq0.rearrange("p (a b) -> p a b", b=128), AX.X).then_inc(osq_done, 1)
            dve.wait_ge(ostd_done, 1)
            V.reciprocal(ostd, ostd)
            dve.drain()
            o16 = cut(hT_t, 0, 16, 128)
            tt_(o16, o16, ostd.unsqueeze(2).to_broadcast([P, 16, 128]), ALU.mult)
            dve.drain()
            dve.wait_ge(hg_zero, 4)
            for h in range(HEADS):
                tt_(o_all[:, h, :].rearrange("p (a b) -> p a b", b=128), o_all[:, h, :].rearrange("p (a b) -> p a b", b=128),
                    g_tm[:, :, h * 128:h * 128 + 128], ALU.mult).then_inc(on_done, 1)
            for b in range(4):
                dve.wait_ge(glu_sig, b + 1)
                if b == 0:
                    dve.wait_ge(glu_psum, 4)
                tt_(catT[:, b, :], catT[:, b, :], uT[:, b, :], ALU.mult).then_inc(a_done, 1)

            def residual(layer):
                def second_half(tt):
                    c = TT * layer + tt
                    dve.wait_ge(tok_psum, 2 * c + 2)
                    if tt >= 2:
                        dve.wait_ge(logit_psum, c - 1)
                    V.tensor_copy(tokT[tt % 2][:, 4:8, :], PS[:, 1, :].rearrange("p (a b) -> p a b", b=128)).then_inc(tok_odd, 1)

                def logits(tt):
                    dve.wait_ge(logit_psum, TT * layer + tt + 1)
                    stt(logit[:, 5 * tt:5 * tt + 5, :], PS[:, 2 + tt % 2, 0:20].rearrange("p (a b) -> p a b", b=4),
                        rstd[:, tt:tt + 1], par(f"bias{layer}").rearrange("p (a b) -> p a b", b=4), ALU.mult, ALU.add)\
                        .then_inc(logit_read, 1)

                for tt in range(TT + 2):
                    if tt < TT:
                        for n in (2 * tt, 2 * tt + 1):
                            dve.wait_ge(mix_psum, 8 * layer + n + 1)
                            xv = x[:, tt, (n % 2) * 512:(n % 2) * 512 + 512]
                            tt_(xv, xv, PS[:, 4 + n % 4, :], ALU.add).then_inc(mix_done, 1)
                        inverse(2 * layer + 1, tt)
                    if 1 <= tt <= TT:
                        second_half(tt - 1)
                    if tt >= 2:
                        logits(tt - 2)

            def list_rows(into):
                ts(absent, PS[:, 3, 128:144], 0.5, ALU.is_lt, 2.0e6, ALU.mult)
                dve.drain()
                return tt_(into, absent.unsqueeze(1).to_broadcast([P, 2, 16]),
                           PS[:, 3, 128:160].rearrange("p (o e) -> p o e", o=2), ALU.add)

            def hot_ranks():
                return tt_(rank_hot, con("time")[:, 0:128].unsqueeze(1).to_broadcast([P, 2 * TT, 128]),
                           ranks.unsqueeze(2).to_broadcast([P, 2 * TT, 128]), ALU.is_equal)

            def route(layer):
                def first_max(values, n, most, place, scratch, hot):
                    iota = con("iota4").unsqueeze(1).to_broadcast([P, n, 4])
                    V.reduce_max(most, values, AX.X)
                    dve.drain()
                    tt_(scratch, values, most.unsqueeze(2).to_broadcast([P, n, 4]), ALU.is_lt)
                    dve.drain()
                    stt(scratch, scratch, 64.0, iota, ALU.mult, ALU.add)
                    dve.drain()
                    V.tensor_reduce(place, scratch, AX.X, ALU.min)
                    dve.drain()
                    tt_(hot, iota, place.unsqueeze(2).to_broadcast([P, n, 4]), ALU.is_equal)
                    dve.drain()

                def tiles5(v):
                    return v.rearrange("p (t g) e -> p t g e", g=5)

                def tiles4(v):
                    return v.rearrange("p (t g) e -> p t g e", g=4)

                dve.drain()
                first_max(logit, TT * 5, top, top_at, below, first_hot)
                stt(tiles4(rest), tiles5(first_hot)[:, :, 1:5, :], -3.0e38, tiles5(logit)[:, :, 1:5, :], ALU.mult, ALU.add)
                group_hot = tiles5(first_hot)[:, :, 0, :]
                group16 = group_hot.unsqueeze(3).to_broadcast([P, TT, 4, 4])
                tt_(picks[:, 0, :, :].rearrange("p t (g e) -> p t g e", e=4), tiles5(first_hot)[:, :, 1:5, :], group16, ALU.mult)
                dve.drain()
                first_max(rest, TT * 4, top2, top2_at, below2, second_hot)
                tt_(picks[:, 1, :, :].rearrange("p t (g e) -> p t g e", e=4), tiles4(second_hot), group16, ALU.mult)
                dve.drain()
                tt_(taken, picks[:, 0, :, :], picks[:, 1, :, :], ALU.add).then_inc(mask_done, 1)
                top5 = top.rearrange("p (t g) -> p t g", g=5)
                values = con("row_of").rearrange("p (n o) -> p n o", o=2).unsqueeze(3).to_broadcast([P, 2 * TT, 2, 16])
                tt_(row_values.rearrange("p n (o e) -> p n o e", o=2),
                    picks.rearrange("p a t e -> p (a t) e").unsqueeze(2).to_broadcast([P, 2 * TT, 2, 16]), values, ALU.mult)
                tt_(group_exp, tiles5(logit)[:, :, 0, :], top5[:, :, 0:1].to_broadcast([P, TT, 4]), ALU.subtract)
                tt_(gap4, top2.rearrange("p (t g) -> p t g", g=4), top5[:, :, 1:5], ALU.subtract)
                dve.wait_ge(rank_psum, layer + 1)
                tt_(picked_rank.rearrange("p (a t) e -> p a t e", a=2), picks,
                    PS[:, 3, 0:64].rearrange("p (t e) -> p t e", e=16).unsqueeze(1).to_broadcast([P, 2, TT, 16]), ALU.mult)
                dve.drain()
                V.reduce_sum(ranks, picked_rank, AX.X)
                dve.drain()
                hot_ranks().then_inc(hot_done, 1)
                tt_(gap4, gap4, group_hot, ALU.mult)
                ts(beyond, ranks, float(CAP), ALU.is_ge)
                dve.drain()
                V.reduce_sum(gap, gap4, AX.X).then_inc(gaps_done, 1)
                V.reduce_sum(flag_f, beyond, AX.X).then_inc(flags_done, 1)
                dve.wait_ge(list_psum, layer + 1)
                list_rows(rows32[:, :].rearrange("p (o e) -> p o e", o=2)).then_inc(route_done, 1)
                dve.wait_ge(exps_done, layer + 1)
                V.reduce_sum(gate_sum, group_exp, AX.X)
                ts(pair_sum, gap, 1.0, ALU.add)
                dve.drain()
                tt_(gate_sum, gate_sum, pair_sum, ALU.mult)
                dve.drain()
                V.reciprocal(w_pair[:, :, 0], gate_sum)
                dve.drain()
                tt_(w_pair[:, :, 1], w_pair[:, :, 0], gap, ALU.mult)
                dve.wait_ge(flag_psum, layer + 1)
                V.tensor_copy(flag32[:, 0:1], PS[:, 2, 0:1]).then_inc(flag_set, 1)

            def experts(layer):
                base = layer * NE

                def turn_rows(j, n):
                    for b in range(2):
                        dve.wait_ge(xT_psum, n * 2 + (b + 1))
                        tt_(xT[j][:, 4 * b:4 * b + 4, :], PS[:, b, :].rearrange("p (a b) -> p a b", b=128),
                            par(f"gain{2 * layer + 1}")[:, 4 * b:4 * b + 4].unsqueeze(2).to_broadcast([P, 4, 128]),
                            ALU.mult).then_inc(xT_done, 1)

                def gated(n):
                    dve.wait_ge(silu_done, n + 1)
                    tt_(hid, gate_s, PS[:, 2, FE:2 * FE], ALU.mult).then_inc(hid_done, 1)

                def turned_hidden(n):
                    dve.wait_ge(hidT_psum, n + 1)
                    V.tensor_copy(hidT, PS[:, 3, 0:256].rearrange("p (a b) -> p a b", b=128)).then_inc(hidT_done, 1)

                turn_rows(0, base)
                gated(base)
                turn_rows(1, base + 1)
                with dve.Fori(0, NE // 2 - 1) as it:
                    for j in range(2):
                        n = it * 2 + (base + j)
                        turned_hidden(n)
                        gated(n + 1)
                        turn_rows(j, n + 2)
                turned_hidden(base + NE - 2)
                gated(base + NE - 1)
                turned_hidden(base + NE - 1)

            def experts_over(layer):
                def body(s):
                    for r in range(OVER // P):
                        ts(ranks, ranks, float(P), ALU.subtract)
                        dve.drain()
                        hot_ranks().then_inc(s["hot"], 1)
                        dve.wait_ge(s["list_psum"], r + 1)
                        list_rows(over32[:, :].rearrange("p (o e r) -> p o e r", o=2, r=OVER // P)[:, :, :, r])\
                            .then_inc(s["listed"], 1)
                    with dve.Fori(0, OVER_TILES) as q:
                        dve.wait_ge(s["xT_psum"], q + 1)
                        for b in range(2):
                            ins = tt_(xT[0][:, 4 * b:4 * b + 4, :], PS[:, b, :].rearrange("p (a b) -> p a b", b=128),
                                      par(f"gain{2 * layer + 1}")[:, 4 * b:4 * b + 4].unsqueeze(2).to_broadcast([P, 4, 128]),
                                      ALU.mult)
                        ins.then_inc(s["xT"], 1)
                        dve.wait_ge(s["silu"], q + 1)
                        tt_(hid, gate_s, PS[:, 2, FE:2 * FE], ALU.mult).then_inc(s["hid"], 1)
                        dve.wait_ge(s["hidT_psum"], q + 1)
                        V.tensor_copy(hidT, PS[:, 3, 0:256].rearrange("p (a b) -> p a b", b=128)).then_inc(s["hidT"], 1)
                if_over(dve, layer, body)

            def combine(layer, tt):
                dve.wait_ge(back_in[tt], 16 * (layer + 1))
                for a in range(2):
                    ins = stt(x[:, tt, :], back[:, tt, a, :], w_pair[:, tt, a:a + 1], x[:, tt, :], ALU.mult, ALU.add)
                    if a == 0:
                        dve.drain()
                ins.then_inc(x_out if layer else layer_done, 1)

            residual(0)
            route(0)
            experts(0)
            experts_over(0)
            for tt in range(TT):
                combine(0, tt)
                if tt >= 1:
                    inverse(2, tt - 1)
                if tt == 2:
                    scaled(1, 0)
            inverse(2, TT - 1)
            for tt in range(1, TT):
                scaled(1, tt)
            ts(kq_gain, par("q_gain"), HD ** -0.5, ALU.mult)
            for tt in range(TT):
                b = 2 + 3 * (tt % 2)
                dve.wait_ge(sqa_done, tt + 1)
                V.reduce_sum(qss, arena[:, 0:1152].rearrange("p (a b) -> p a b", b=HD), AX.X).then_inc(ss_a, 1)
                dve.wait_ge(qstd_s, tt + 1)
                V.reciprocal(qstd, qstd)
                dve.drain()
                qv = qn[:, tt, :].rearrange("p (a b) -> p a b", b=HD)
                tt_(qv, PS[:, b:b + 2, :].rearrange("p a (c d) -> p (a c) d", d=HD),
                    qstd[:, 0:16].unsqueeze(2).to_broadcast([P, 16, HD]), ALU.mult)
                kv = kn[:, tt, :].rearrange("p (a b) -> p a b", b=HD)
                tt_(kv, PS[:, b + 2, 0:128].rearrange("p (c d) -> p c d", d=HD),
                    qstd[:, 16:18].unsqueeze(2).to_broadcast([P, 2, HD]), ALU.mult)
                dve.drain()
                tt_(qv, qv, kq_gain.unsqueeze(1).to_broadcast([P, 16, HD]), ALU.mult)
                tt_(kv, kv, par("k_gain").unsqueeze(1).to_broadcast([P, 2, HD]), ALU.mult).then_inc(qkn_done, 1)
            dve.wait_ge(at_zero, 1)
            for j in range(9):
                dve.wait_ge(qtr_psum, j + 1)
                dst = qT1[:, j, :] if j < 8 else kT1[:, 128:640]
                V.tensor_copy(dst, PS[:, j % 2, :]).then_inc(qT_done, 1)

            def biased(u):
                n, jq = u // 2, u % 2
                pr = probs[u % 2]
                if u >= 2:
                    dve.wait_ge(pt_psum, 4 * (u - 1))
                table = con("dist_first") if n == 0 else con("dist")
                for t in range(2):
                    dve.wait_ge(s_psum, 2 * u + t + 1)
                    for j in (2 * t, 2 * t + 1):
                        for kv in range(2):
                            head = 8 * kv + 4 * jq + j
                            ins = stt(pr[:, 2 * j + kv, :], table, con("slope")[:, head:head + 1],
                                      PS[:, 5 * t + kv, (j % 2) * 256:(j % 2) * 256 + 256], ALU.mult, ALU.add)
                    ins.then_inc(s_biased, 1)
                dve.drain()
                sink = par("sinks").rearrange("p (v q j) -> p q j v", v=2, q=2)[:, jq, :, :]
                m = am[u % 2]
                V.reduce_max(m, pr, AX.X)
                dve.drain()
                m2 = m.rearrange("p (j v) -> p j v", v=2)
                tt_(m2, m2, sink, ALU.max)
                dve.drain()
                tt_(ane[u % 2].rearrange("p (j v) -> p j v", v=2), sink, m2, ALU.subtract)
                dve.drain()
                ts(m, m, -1.0, ALU.mult).then_inc(m_done, 1)

            def summed(u):
                dve.wait_ge(p_exp, u + 1)
                tt_(asum[u % 2], aes[u % 2], ane[u % 2], ALU.add)
                dve.drain()
                V.reciprocal(asum[u % 2], asum[u % 2]).then_inc(m_done, 1)

            biased(0)
            summed(0)
            for u in range(8):
                if u + 1 < 8:
                    biased(u + 1)
                if u + 1 < 8:
                    summed(u + 1)
            residual(1)
            route(1)
            experts(1)
            experts_over(1)
            for tt in range(TT):
                combine(1, tt)

        @block.tensor
        def _(pe):
            mm = nc.tensor.matmul
            T = nc.tensor.transpose

            def full(i):
                pe.wait_ge(slot_full[i % RING], 16 * (i // RING + 1))

            pending = [0]

            def give(ins):
                if pending[0]:
                    ins.then_inc(slot_free, pending[0])
                    pending[0] = 0

            def turn_tile(mixer, tt):
                c = TT * mixer + tt
                pe.wait_ge(xs_done, c + 1)
                for b in range(2):
                    if c >= 1:
                        pe.wait_ge(hT_done, 2 * c + b - 1)
                    for k in range(4):
                        at = (4 * b + k) * 128
                        ins = T(PS[:, b, k * 128:k * 128 + 128], xs[:, tt, at:at + 128], ident)
                        if b == 0 and k == 0:
                            give(ins)
                    ins.then_inc(turned_psum, 1)

            pe.wait_ge(const_in, 16)
            for tt in range(TT):
                turn_tile(0, tt)
            pe.wait_ge(hT_done, 2 * TT)
            full(0)
            full(1)
            for cb in range(4):
                if cb >= 2:
                    pe.wait_ge(u_done, cb - 1)
                for k in range(KD):
                    ins = mm(PS[:, 2 + cb % 2, :], k512(k // 4)[:, k % 4, cb * 128:cb * 128 + 128], hT[:, k, :],
                             start=k == 0, stop=k == KD - 1)
                    if cb == 3 and k == 3:
                        ins.then_inc(slot_free, 1)
                ins.then_inc(u_psum, 1)
            pending[0] = 1
            pe.wait_ge(bexp_done, 1)
            for ri in range(2):
                for b in range(4):
                    src = arena[:, 15360 + 1024 * ri + 128 * b:15360 + 1024 * ri + 128 * (b + 1)]
                    ins = T(PS[:, 6 + ri, b * 128:b * 128 + 128], src, ident)
                    if b == 0 and ri == 0:
                        give(ins)
            ins.then_inc(bT_psum, 1)

            def proj(i):
                s = 2 * (1 + i // 4)
                if i % 4 == 0:
                    full(s)
                    full(s + 1)
                if i >= 2:
                    pe.wait_ge(proj_done, i - 1)
                for k in range(KD):
                    w, h = k512(s + k // 4)[:, k % 4, :], hT[:, k, :]
                    lhsT, rhs = (w, h) if i < 8 else (h, w)
                    m = slice((i % 4) * 128, (i % 4) * 128 + 128)
                    ins = mm(PS[:, 6 + i % 2, :], lhsT[:, m], rhs, start=k == 0, stop=k == KD - 1)
                    if i % 4 == 3 and k == 3:
                        ins.then_inc(slot_free, 1)
                    elif k == 0:
                        give(ins)
                ins.then_inc(proj_psum, 1)
                if i % 4 == 3:
                    pending[0] = 1

            def inputs(i):
                b, q, s = i // 4, i % 4, i % 2
                if i >= 2:
                    pe.wait_ge(prod_done, i - 1)
                rows = slice(32 * q, 32 * q + 32)
                for ri in range(2):
                    ins = mm(PS[:, 2 * s + ri, :], BT[rows, ri, b, :], uT[rows, b, :], start=True, stop=True,
                             tile_position=(32 * q, 0))
                    if ri == 0:
                        give(ins)
                ins.then_inc(bu_done, 1)

            def readout(i):
                b = i // 4
                pe.wait_ge(ab_done, i + 1)
                if i % 4 == 0 and b >= 2:
                    pe.wait_ge(y_sum, b - 1)
                q = prod_out[i % 2]
                rows = 32 * (i % 4)
                out = PS[rows:rows + 32, 4 + b % 2, :]
                mm(out, Cx[:, 0, i, :], q[0], start=True, stop=False, tile_position=(0, rows))
                mm(out, Cx[:, 1, i, :], q[2], start=False, stop=True, tile_position=(0, rows)).then_inc(y_used, 1)

            pe.wait_ge(u_done, 4)
            pe.wait_ge(bT_done, 1)
            pe.wait_ge(cread_in, 16)
            inputs(0)
            inputs(1)
            for i in range(PAIRS):
                proj(i)
                if i >= 1:
                    readout(i - 1)
                if i + 2 < PAIRS:
                    inputs(i + 2)
            readout(PAIRS - 1)

            def head_scores(h):
                pe.wait_ge(hg_dve, 2 * h + 1)
                if h >= 2:
                    pe.wait_ge(sc_done, h - 1)
                for blk in range(4):
                    m = slice(blk * 128, blk * 128 + 128)
                    ins = mm(PS[:, h % 2, m], ke2[:, h, m], qe1[:, h, m], start=True, stop=True)
                ins.then_inc(sc_psum, 1)
                pe.wait_ge(hg_dve, 2 * h + 2)
                if h >= 1:
                    pe.wait_ge(ktm_done, h)
                for blk in range(4):
                    m = slice(blk * 128, blk * 128 + 128)
                    ins = T(PS[:, 2, m], ke3[:, h, m], ident)
                ins.then_inc(ktr_psum, 1)

            def head_increments(h):
                pe.wait_ge(ktm_done, h + 1)
                if h == 0:
                    pe.wait_ge(y_sum, 4)
                    pe.wait_ge(proj_done, PAIRS)
                else:
                    pe.wait_ge(st_done, h)
                for c in range(NCHUNK - 1):
                    r = slice(32 * (c % 4), 32 * (c % 4) + 32)
                    ins = mm(PS[:, 3 + c % 4, (c // 4) * 128:(c // 4) * 128 + 128], ke3_tm[h % 2][r, c // 4, :],
                             v_tm[r, c // 4, h * 128:h * 128 + 128], start=True, stop=True, tile_position=(32 * (c % 4), 0))
                ins.then_inc(inc_psum, 1)

            def head_out(h):
                pe.wait_ge(sc_done, h + 1)
                pe.wait_ge(qm_done, h + 1)
                pe.wait_ge(st_done, h + 1)
                if h >= 1:
                    pe.wait_ge(o_out, h)
                for blk in range(4):
                    out = PS[:, 7, blk * 128:blk * 128 + 128]
                    mm(out, scores[h % 2][:, blk, :], v_tm[:, blk, h * 128:h * 128 + 128], start=True, stop=False)
                    for r in range(4):
                        if 4 * blk + r == 0:
                            continue
                        ins = mm(out, q_masked[h % 2][:, 640 * blk + 128 * r:640 * blk + 128 * r + 128],
                                 state[h % 2][:, 4 * blk + r - 1, :], start=False, stop=r == 3)
                ins.then_inc(o_psum, 1)

            head_scores(0)
            head_increments(0)
            head_scores(1)
            for h in range(HEADS):
                if h + 1 < HEADS:
                    head_increments(h + 1)
                head_out(h)
                if h + 2 < HEADS:
                    head_scores(h + 2)
            full(GLU0)
            pe.wait_ge(gelu_done, 4)
            for b in range(4):
                if b >= 2:
                    pe.wait_ge(glu_sig, b - 1)
                for k in range(4):
                    ins = mm(PS[:, b % 2, :], k512(GLU0)[:, k, b * 128:b * 128 + 128], catT[:, k, :], start=k == 0, stop=k == 3)
                ins.then_inc(glu_psum, 1)
            pending[0] = 1
            for h in range(HEADS):
                pe.wait_ge(on_done, h + 1)
                if h >= 2:
                    pe.wait_ge(catb_done, h - 1)
                for blk in range(4):
                    m = slice(blk * 128, blk * 128 + 128)
                    ins = T(PS[:, 2 + h % 2, m], o_all[:, h, m], ident)
                    if blk == 0:
                        give(ins)
                ins.then_inc(otr_psum, 1)

            def out_proj(layer, lhs, first):
                def turn_tokens(tt):
                    c = TT * layer + tt
                    pe.wait_ge(mix_done, 2 * c + 2)
                    for b in range(2):
                        if c >= 1:
                            pe.wait_ge((tok_even, tok_odd)[b], c)
                        for k in range(4):
                            at = (4 * b + k) * 128
                            ins = T(PS[:, b, k * 128:k * 128 + 128], x[:, tt, at:at + 128], ident)
                            if b == 0 and k == 0:
                                give(ins)
                        ins.then_inc(tok_psum, 1)

                def logits(tt):
                    w = par(f"router{layer}").rearrange("p (k n) -> p k n", n=20)
                    pe.wait_ge(tok_even, TT * layer + tt + 1)
                    pe.wait_ge(tok_odd, TT * layer + tt + 1)
                    if TT * layer + tt >= 2:
                        pe.wait_ge(logit_read, TT * layer + tt - 1)
                    for k in range(KD):
                        ins = mm(PS[:, 2 + tt % 2, 0:20], tokT[tt % 2][:, k, :], w[:, k, :], start=k == 0, stop=k == KD - 1)
                    ins.then_inc(logit_psum, 1)

                for tt in range(TT + 2):
                    if tt < TT:
                        for n in (2 * tt, 2 * tt + 1):
                            if n >= 4:
                                pe.wait_ge(mix_done, 8 * layer + n - 3)
                            for k in range(KD):
                                if n == 0 and k % 2 == 0:
                                    full(first + k // 2)
                                w = slot(first + k // 2).rearrange("p (k n) -> p k n", n=D)
                                ins = mm(PS[:, 4 + n % 4, :], lhs[:, k, tt * 128:tt * 128 + 128],
                                         w[:, k % 2, (n % 2) * 512:(n % 2) * 512 + 512], start=k == 0, stop=k == KD - 1)
                                if n == 7 and k % 2 == 1 and k < KD - 1:
                                    ins.then_inc(slot_free, 1)
                            ins.then_inc(mix_psum, 1)
                        if tt == TT - 1:
                            pending[0] = 1
                    if 1 <= tt <= TT:
                        turn_tokens(tt - 1)
                    if tt >= 2:
                        logits(tt - 2)

            def route(layer):
                pe.wait_ge(mask_done, layer + 1)
                mm(PS[:, 3, 0:64], con("before"), taken.rearrange("p t e -> p (t e)"), start=True, stop=False)
                for t in range(TT - 1):
                    ins = mm(PS[:, 3, 16 * (t + 1):64].rearrange("p (t e) -> p t e", e=16), con("ones"),
                             taken[:, t:t + 1, :].to_broadcast([P, TT - 1 - t, 16]), start=False, stop=t == TT - 2)
                ins.then_inc(rank_psum, 1)
                pe.wait_ge(hot_done, layer + 1)
                lists().then_inc(list_psum, 1)
                pe.wait_ge(flags_done, layer + 1)
                mm(PS[:, 2, 0:1], con("ones"), flag_f, start=True, stop=True).then_inc(flag_psum, 1)

            def lists():
                for n in range(2 * TT):
                    ins = mm(PS[:, 3, 128:160], rank_hot[:, n, :], row_values[:, n, :], start=n == 0, stop=n == 2 * TT - 1)
                return ins

            def experts(layer):
                base, s0 = layer * NE, EXP0[layer]

                def row_turns(j, n, got):
                    pe.wait_ge(got_row[j], got)
                    if not isinstance(n, int) or n >= 1:
                        pe.wait_ge(xT_done, n * 2)
                    for b in range(2):
                        for k in range(4):
                            ins = T(PS[:, b, k * 128:k * 128 + 128], xrow[j][:, (4 * b + k) * 128:(4 * b + k) * 128 + 128], ident)
                            if b == 0 and k == 0:
                                give(ins)
                        ins.then_inc(xT_psum, 1)

                def gate_up(j, n, it, at):
                    pe.wait_ge(xT_done, n * 2 + 2)
                    if not isinstance(n, int) or n >= 1:
                        pe.wait_ge(hid_done, n)
                    for k in range(KD):
                        i = at + k // 4
                        if k % 4 == 0:
                            pe.wait_ge(slot_full[i % RING], (it + (i // RING + 1)) * 16)
                        ins = mm(PS[:, 2, :], xT[j][:, k, :], k512(i)[:, k % 4, :], start=k == 0, stop=k == KD - 1)
                        if k == 3:
                            ins.then_inc(slot_free, 1)
                    ins.then_inc(gu_psum, 1)
                    pending[0] = 1

                def hid_turns(n):
                    pe.wait_ge(hid_done, n + 1)
                    if not isinstance(n, int) or n >= 1:
                        pe.wait_ge(hidT_done, n)
                    for k in range(2):
                        ins = T(PS[:, 3, k * 128:k * 128 + 128], hid[:, k * 128:k * 128 + 128], ident)
                        if k == 0:
                            give(ins)
                    ins.then_inc(hidT_psum, 1)

                def down(j, n, it, at):
                    pe.wait_ge(hidT_done, n + 1)
                    if not isinstance(n, int) or n >= 1:
                        pe.wait_ge(yrow_done, n)
                    pe.wait_ge(slot_full[at % RING], (it + (at // RING + 1)) * 16)
                    w = slot(at).rearrange("p (k n) -> p k n", n=D)
                    for half in range(2):
                        for k in range(2):
                            ins = mm(PS[:, 4 + half, :], hidT[:, k, :], w[:, k, half * 512:half * 512 + 512],
                                     start=k == 0, stop=k == 1)
                            if half == 0 and k == 0:
                                give(ins)
                    ins.then_inc(y_psum2, 1)
                    pending[0] = 1

                def step(j, n, it, more=True):
                    hid_turns(n)
                    gate_up(1 - j, n + 1, it, s0 + 3 * j + 2)
                    if more:
                        row_turns(j, n + 2, (it + (base // 2 + 2)) * 16)
                    down(j, n, it, s0 + 3 * j + 4)

                row_turns(0, base, (base // 2 + 1) * 16)
                gate_up(0, base, 0, s0)
                row_turns(1, base + 1, (base // 2 + 1) * 16)
                step(0, base, 0)
                step(1, base + 1, 0)
                with pe.Fori(1, NE // 2 - 1) as it:
                    for j in range(2):
                        step(j, it * 2 + (base + j), it)
                step(0, base + NE - 2, NE // 2 - 1, more=False)
                hid_turns(base + NE - 1)
                down(1, base + NE - 1, 0, s0 + EXP_SLOTS * NE - 1)

            def experts_over(layer):
                def body(s):
                    for r in range(OVER // P):
                        pe.wait_ge(s["hot"], r + 1)
                        lists().then_inc(s["list_psum"], 1)
                    with pe.Fori(0, NE) as e:
                        for r in range(OVER // P):
                            q = e * (OVER // P) + r
                            pe.wait_ge(s["row"], q * 16 + 16)
                            for k in range(KD):
                                ins = T(PS[:, k // 4, (k % 4) * 128:(k % 4) * 128 + 128], xrow[0][:, k * 128:k * 128 + 128], ident)
                            ins.then_inc(s["xT_psum"], 1)
                            pe.wait_ge(s["xT"], q + 1)
                            if r == 0:
                                pe.wait_ge(s["weights"], e * 32 + 32)
                            for k in range(KD):
                                ins = mm(PS[:, 2, :], xT[0][:, k, :], over_w[:, 512 * k:512 * k + 512], start=k == 0, stop=k == KD - 1)
                            ins.then_inc(s["gate_up"], 1)
                            pe.wait_ge(s["hid"], q + 1)
                            for k in range(2):
                                ins = T(PS[:, 3, k * 128:k * 128 + 128], hid[:, k * 128:k * 128 + 128], ident)
                            ins.then_inc(s["hidT_psum"], 1)
                            pe.wait_ge(s["hidT"], q + 1)
                            for half in range(2):
                                for k in range(2):
                                    at = 2 * SLOT + k * D + half * 512
                                    ins = mm(PS[:, 4 + half, :], hidT[:, k, :], over_w[:, at:at + 512], start=k == 0, stop=k == 1)
                            ins.then_inc(s["y_psum"], 1)
                if_over(pe, layer, body)

            pe.wait_ge(a_done, 4)
            pe.wait_ge(catb_done, 4)
            out_proj(0, catT, OUT0)
            route(0)
            experts(0)
            experts_over(0)
            turn_tile(1, 0)
            for i in range(QKV_SLOTS):
                full(QKV0 + i)
            for tt in range(TT):
                if tt == 1:
                    for t in range(1, TT):
                        turn_tile(1, t)
                pe.wait_ge(hT_done, 2 * TT + 2 * tt + 2)
                b = 2 + 3 * (tt % 2)
                if tt >= 2:
                    pe.wait_ge(qkn_done, tt - 1)
                for part in range(3):
                    n = 512 if part < 2 else 256
                    for k in range(KD):
                        w = k512(QKV0 + 2 * part + k // 4)[:, k % 4, :] if part < 2 else \
                            slot(QKV0 + 4).rearrange("p (k n) -> p k n", n=256)[:, k, :]
                        ins = mm(PS[:, b + part, 0:n], hT[:, k, tt * 128:tt * 128 + 128], w, start=k == 0, stop=k == KD - 1)
                        if tt == 3 and part < 2 and k % 4 == 3:
                            ins.then_inc(slot_free, 1)
                ins.then_inc(qkv_psum, 1)
            pending[0] = 1
            pe.wait_ge(qkn_done, 4)
            for j in range(9):
                if j >= 2:
                    pe.wait_ge(qT_done, j - 1)
                for tt in range(TT):
                    src = qn[:, tt, j * 128:j * 128 + 128] if j < 8 else kn[:, tt, :]
                    ins = T(PS[:, j % 2, tt * 128:tt * 128 + 128], src, ident)
                    if tt == 0:
                        give(ins)
                ins.then_inc(qtr_psum, 1)
            pe.wait_ge(qT_done, 9)

            def att_scores(u):
                n, jq = u // 2, u % 2
                for t in range(2):
                    if u >= 1:
                        pe.wait_ge(s_biased, 2 * u + t - 1)
                    for j in (2 * t, 2 * t + 1):
                        for kv in range(2):
                            d = slice(64 * kv, 64 * kv + 64)
                            ins = mm(PS[:, 5 * t + kv, (j % 2) * 256:(j % 2) * 256 + 256],
                                     qT1[d, 4 * jq + j, n * 128:n * 128 + 128], kT1[d, n * 128:n * 128 + 256],
                                     start=True, stop=True, tile_position=(64 * kv, 0))
                    ins.then_inc(s_psum, 1)

            att_scores(0)
            for u in range(8):
                n = u // 2
                if u + 1 < 8:
                    att_scores(u + 1)
                for b in range(4):
                    pe.wait_ge((p_norm, p_norm_odd)[b // 2], u + 1)
                    if 4 * u + b >= 2:
                        pe.wait_ge(pt_done, 4 * u + b - 1)
                    kv, kb = b // 2, b % 2
                    for j in range(4):
                        ins = T(PS[:, 2 + b % 2, j * 128:j * 128 + 128], probs[u % 2][:, 2 * j + kv, kb * 128:kb * 128 + 128], ident)
                    ins.then_inc(pt_psum, 1)
                if u >= 1:
                    pe.wait_ge(att_done, u)
                for b in range(4):
                    pe.wait_ge(pt_done, 4 * u + b + 1)
                    ins = mm(PS[:, 4, :], vpad[:, n + b % 2, b // 2, :], probsT[u % 2][:, b, :], start=b == 0, stop=b == 3)
                ins.then_inc(att_psum, 1)
            pe.wait_ge(att_done, 8)
            out_proj(1, attT, OUT1)
            route(1)
            experts(1)
            experts_over(1)


def laid_out(i):
    import numpy as np
    f = {k: np.asarray(v) for k, v in i.items()}

    def rows(w, k):
        return w.reshape(k, P, -1).transpose(1, 0, 2)

    stream = np.zeros((N_SLOTS, P, SLOT), np.float32)

    def put(at, w):
        w = w.reshape(P, -1)
        for s in range(w.shape[1] // SLOT):
            stream[at + s] = w[:, s * SLOT:(s + 1) * SLOT]

    w_in = f["even_in_proj"][0]
    for s, c in enumerate((0, 2, 1, 3, 4)):
        put(2 * s, rows(w_in[:, 512 * c:512 * (c + 1)], KD))
    put(GLU0, rows(f["s5_glu_w"][0], 4))
    put(OUT0, rows(f["even_out_proj"][0], KD))
    qkv = f["odd_wqkv"][0]
    q = qkv[:, :QW].reshape(D, 2, 8, HD).transpose(0, 2, 1, 3).reshape(D, QW)
    put(QKV0, rows(q[:, :512], KD))
    put(QKV0 + 2, rows(q[:, 512:], KD))
    put(QKV0 + 4, rows(qkv[:, QW:], KD))
    put(OUT1, rows(f["odd_out_proj"][0].reshape(2, 8, HD, D).transpose(1, 0, 2, 3).reshape(QW, D), KD))
    for layer in range(2):
        for e in range(NE):
            at = EXP0[layer] + EXP_SLOTS * e
            gu = np.concatenate([f["moe_w_gate"][layer, e], f["moe_w_up"][layer, e]], 1)
            put(at - (e > 0), rows(gu, KD))
            put(at + 4 if e < NE - 1 else at + 2, rows(f["moe_w_down"][layer, e], 2))

    param = np.zeros((P, N_PARAM), np.float32)

    def setp(name, v):
        a, b = PARAM[name]
        param[:, a:b] = v.reshape(P, -1) if v.ndim > 1 else v[None, :]

    for n, g in enumerate((f["even_mix_norm"][0], f["moe_norm"][0], f["odd_mix_norm"][0], f["moe_norm"][1])):
        setp(f"gain{n}", g.reshape(KD, P).T)
    for layer in range(2):
        w = np.concatenate([f["moe_router_group"][layer], f["moe_router_expert"][layer]], 1)
        setp(f"router{layer}", rows(w, KD))
        setp(f"bias{layer}", np.concatenate([f["moe_router_group_bias"][layer], f["moe_router_expert_bias"][layer]]))
    setp("lam_re", f["s5_lambda_re"][0].reshape(PAIRS, P).T)
    setp("lam_im", f["s5_lambda_im"][0].reshape(PAIRS, P).T)
    setp("log_step", np.repeat(f["s5_log_step"][0].reshape(PAIRS, 2), 64, axis=1).T)
    for name in ("b_re", "b_im"):
        b = f["s5_" + name][0].reshape(PAIRS, 2, 64, 16)
        v = np.zeros((2, 64, PAIRS, 2, 16), np.float32)
        for g in range(2):
            v[g, :, :, g, :] = b[:, g].transpose(1, 0, 2)
        setp(name, v.reshape(P, -1))
    setp("d_skip", f["s5_d"][0].reshape(4, P).T)
    setp("bounds", f["hgrn_lower_bounds"].reshape(3, HEADS, P).transpose(2, 0, 1))
    setp("o_gain", f["hgrn_o_norm"][0])
    setp("q_gain", f["odd_q_norm"][0])
    setp("k_gain", f["odd_k_norm"][0])
    setp("sinks", f["odd_sinks"][0])
    cread = np.zeros((2, 64, 2, PAIRS, 2, 16), np.float32)
    for ri, name in enumerate(("s5_c_re", "s5_c_im")):
        c = f[name][0].reshape(PAIRS, 2, 16, 64)
        for pair in range(PAIRS):
            for g in range(2):
                cread[g, :, ri, pair, g, :] = c[pair, g].T
    cread = cread.reshape(P, -1)

    const = np.zeros((P, N_CONST), np.float32)

    def setc(name, v):
        a, b = CONST[name]
        const[:, a:b] = v

    p, c = np.arange(P)[:, None], np.arange(512)[None, :]
    setc("ident", np.eye(P))
    setc("time", c)
    far = np.float32(1.0e30)
    dist = p - c[:, :256] + P
    inside = (dist >= 0) & (dist < WIN)
    setc("dist", np.where(inside, dist, far))
    setc("dist_first", np.where(inside & (c[:, :256] >= P), dist, far))
    setc("chunk_causal", (p // CH == c[:, :P] // CH) & (p <= c[:, :P]))
    setc("chunk_reset", c % CH != 0)
    setc("before", p < c[:, :P])
    setc("ones", 1.0)
    setc("iota4", c[:, :4])
    n = c[:, :2 * TT]
    token = P * (n % TT) + p
    setc("row_of", np.stack([2 * token + n // TT + 1, token], 2).reshape(P, -1))
    setc("slope", -(2.0 ** (-8.0 * np.arange(1, NQ + 1) / NQ))[None, :])
    return {"x_in": f["x"][0], "stream": stream, "cread": cread, "const_in": const, "param_in": param}


def kernel(**inputs):
    import numpy as np
    import concourse.bacc as bacc
    from concourse.bass_utils import run_bass_kernel_spmd

    nc = bacc.Bacc("TRN2", target_bir_lowering=False, num_devices=1)
    arrays, args = {}, []
    for name, a in laid_out(inputs).items():
        arrays[name] = np.ascontiguousarray(a)
        args.append(nc.dram_tensor(name, a.shape, mybir.dt.from_np(a.dtype), kind="ExternalInput").ap())
    out = nc.dram_tensor("out", [SEQ, D], mybir.dt.float32, kind="ExternalOutput").ap()
    trunk(nc, *args, out)
    r = run_bass_kernel_spmd(nc, [arrays], core_ids=[0])
    return r.results[0]["out"].reshape(1, SEQ, D)
```

```python
import math

import concourse.bass as bass
from concourse import mybir
from contextlib import ExitStack

P = 128
SEQ, D = 512, 1024
TT, KD = SEQ // P, D // P
PAIRS = 16
HEADS, CH = 4, 32
NCHUNK = SEQ // CH
NQ, HD, WIN = 16, 64, 128
QW = NQ * HD
NG, EPG = 4, 4
NE = NG * EPG
FE = D // 4
SLOT = 2048
RING = 6
IN_SLOTS, GLU_SLOTS, OUT_SLOTS, EXP_SLOTS, QKV_SLOTS = 10, 1, 4, 3, 5
GLU0 = IN_SLOTS
OUT0 = GLU0 + GLU_SLOTS
EXP0 = [OUT0 + OUT_SLOTS]
QKV0 = EXP0[0] + NE * EXP_SLOTS
OUT1 = QKV0 + QKV_SLOTS
EXP0.append(OUT1 + OUT_SLOTS)
N_SLOTS = EXP0[1] + NE * EXP_SLOTS
CAP = P
OVER = SEQ - CAP
OVER_TILES = NE * (OVER // P)
EPS = 1e-6


def columns(widths):
    at, out = 0, {}
    for name, w in widths:
        out[name] = (at, at + w)
        at += w
    return out, at


CONST, N_CONST = columns([("ident", 128), ("time", 512), ("dist_first", 256), ("dist", 256), ("chunk_causal", 128),
                          ("chunk_reset", 512), ("before", 128), ("ones", 128), ("iota4", 4), ("row_of", 2 * TT),
                          ("slope", NQ)])
PARAM, N_PARAM = columns([("gain0", KD), ("gain1", KD), ("gain2", KD), ("gain3", KD), ("lam_re", PAIRS),
                          ("lam_im", PAIRS), ("log_step", PAIRS), ("d_skip", 4), ("bounds", 3 * HEADS),
                          ("router0", KD * 20), ("router1", KD * 20), ("bias0", 20), ("bias1", 20),
                          ("b_re", PAIRS * 32), ("b_im", PAIRS * 32), ("o_gain", 128), ("q_gain", HD),
                          ("k_gain", HD), ("sinks", NQ)])
FIRST_PARAM = PARAM["router0"][0]
MAGIC = 1.5 * 2.0 ** 23
MAGIC12 = 1.5 * 2.0 ** 11
TWO_PI = 6.283185


def trunk(nc, x_d, stream_d, cread_d, const_d, param_d, out_d):
    f32, i32 = mybir.dt.float32, mybir.dt.int32
    ALU, ACT, AX = mybir.AluOpType, mybir.ActivationFunctionType, mybir.AxisListType
    ctx = ExitStack()
    with ctx:
        def sb(name, n, dt=f32):
            return ctx.enter_context(nc.sbuf_tensor(name, [P, n], dt))

        def sem(name):
            return ctx.enter_context(nc.semaphore(name))

        def cut(t, at, *dims):
            n = math.prod(dims)
            v = t[:, at:at + n]
            if len(dims) == 2:
                v = v.rearrange("p (a b) -> p a b", b=dims[1])
            if len(dims) == 3:
                v = v.rearrange("p (a b c) -> p a b c", b=dims[1], c=dims[2])
            return v

        ring = sb("ring", RING * SLOT)
        x_t = sb("x", TT * D)
        const, param = sb("const", N_CONST), sb("param", N_PARAM)
        small = sb("small", 1064)
        rows32, over32 = sb("rows32", NE, i32), sb("over32", 2 * OVER_TILES, i32)
        row_now, flag32 = sb("row_now", 1, i32), sb("flag32", 2, i32)
        with ExitStack() as plain:
            xs_t, hT_t, arena = [plain.enter_context(nc.sbuf_tensor(name, [P, n], f32))
                                 for name, n in (("xs", TT * D), ("hT", KD * SEQ), ("arena", 23552))]
        f32r = mybir.dt.float32r
        left_hi, left_lo = cut(sb("left_hi", KD * SEQ, f32r), 0, KD, 512), cut(sb("left_lo", KD * SEQ, f32r), 0, KD, 512)
        sb("kept0", 2048)
        w_hi1, w_lo1 = sb("w_hi1", SLOT, f32r), sb("w_lo1", SLOT, f32r)
        sb("kept1", 17408 - 2048 - 2 * SLOT)
        w_hi0, w_lo0 = sb("w_hi0", SLOT, f32r), sb("w_lo0", SLOT, f32r)
        w_hi, w_lo = [w_hi0[:, :], w_hi1[:, :]], [w_lo0[:, :], w_lo1[:, :]]
        PS = ctx.enter_context(nc.psum_tensor("PS", [P, 8, 512], f32))

        def con(name):
            return const[:, CONST[name][0]:CONST[name][1]]

        def par(name):
            return param[:, PARAM[name][0]:PARAM[name][1]]

        x, xs, hT = cut(x_t, 0, TT, D), cut(xs_t, 0, TT, D), cut(hT_t, 0, KD, SEQ)
        ident = con("ident")

        rows_d = nc.dram_tensor("rows", [SEQ, D], f32)
        sums_d = nc.dram_tensor("sums", [SEQ, D], f32)

        uT = cut(arena, 0, 4, 512)
        BT = cut(arena, 2048, 2, 4, 128)
        Cx = cut(arena, 3072, 2, PAIRS, 32)
        fT, qT0 = cut(arena, 7168, HEADS, 512), cut(arena, 9216, HEADS, 512)
        v_tm, g_tm = cut(arena, 11264, TT, 512), cut(arena, 13312, TT, 512)
        catT = cut(arena, 15360, KD, 512)
        tiles = [arena[:, 19456 + 512 * i:19456 + 512 * (i + 1)] for i in range(8)]
        tiles += [xs_t[:, 512 * i:512 * (i + 1)] for i in range(8)]
        tiles += [catT[:, 4 + i, :] for i in range(4)]
        cosT, nsinT = tiles[0:3], tiles[3:6]
        zr, zi = tiles[6], tiles[7]
        prod_in, prod_out = tiles[8:12], [tiles[12:16], tiles[16:20]]
        keep_k = cut(arena, 4608, HEADS, 512)
        qe1, ke2, ke3 = cut(hT_t, 0, HEADS, 512), cut(hT_t, 2048, HEADS, 512), cut(xs_t, 0, HEADS, 512)
        q_masked = [arena[:, 2048:4608], arena[:, 17408:19968]]
        scores = [cut(arena, 19968 + 512 * i, 4, 128) for i in range(2)]
        ke3_tm = [cut(arena, 20992 + 512 * i, 4, 128) for i in range(2)]
        sq0 = arena[:, 21504:21504 + 2048]
        state = [cut(arena, 0, 15, 128), cut(xs_t, 2048, 15, 128)]
        o_all = qe1
        decay = cut(small, 1000, HEADS, NCHUNK)
        sq1 = arena[:, 0:QW]
        kn, vpad = cut(arena, 1280, TT, 128), cut(arena, 1792, 5, 2, 128)
        qT1, kT1 = cut(arena, 3072, 8, 512), arena[:, 7168:7168 + 640]
        probs = [cut(arena, 7808 + 2048 * i, 8, 256) for i in range(2)]
        probsT = [cut(arena, 11904 + 2048 * i, 4, 512) for i in range(2)]
        qn = cut(xs_t, 0, TT, QW)
        xrow = [arena[:, 1024 * i:1024 * (i + 1)] for i in range(2)]
        xT = [cut(arena, 2048 + 1024 * i, KD, 128) for i in range(2)]
        gate_s, hid, hidT = arena[:, 4096:4352], arena[:, 4352:4608], cut(arena, 4608, 2, 128)
        yrow = [arena[:, 4864 + 1024 * i:5888 + 1024 * i] for i in range(2)]
        over_w = arena[:, 15104:15104 + 3 * SLOT]
        tokT = [cut(arena, 11008 + 1024 * i, KD, 128) for i in range(2)]
        rows = cut(arena, 6912, TT, D)
        rank_hot = cut(arena, 22528, 2 * TT, 128)
        at_route = [21504]

        def ro(*dims):
            v = cut(arena, at_route[0], *dims)
            at_route[0] += math.prod(dims)
            return v

        row_values, weight_values = ro(2 * TT, 16), ro(2 * TT, 16)
        logit, below, first_hot = ro(TT * 5, 4), ro(TT * 5, 4), ro(TT * 5, 4)
        top, top_at, top2, top2_at = ro(TT * 5), ro(TT * 5), ro(TT * 4), ro(TT * 4)
        rest, below2, second_hot = ro(TT * 4, 4), ro(TT * 4, 4), ro(TT * 4, 4)
        picks, taken = ro(2, TT, 16), ro(TT, 16)
        assert at_route[0] <= 22528, at_route[0]

        at = [0]

        def sm(*dims):
            v = cut(small, at[0], *dims)
            at[0] += math.prod(dims)
            return v

        eps_t, half_pi, magic_t = sm(1), sm(1), sm(1)
        ssq, std, rstd = sm(TT), sm(TT), sm(TT)
        mag, turn, turn_hi, turn_lo = sm(PAIRS), sm(PAIRS), sm(PAIRS), sm(PAIRS)
        s5tmp = [sm(PAIRS) for _ in range(8)]
        step_t, sin1, cos1 = sm(PAIRS), sm(PAIRS), sm(PAIRS)
        lbmax, lbexp, lb, one_lb = sm(HEADS), sm(3, HEADS), sm(HEADS), sm(HEADS)
        ossq, ostd = sm(16), sm(16)
        S5_END = at[0]
        w_pair, w_rows, over_weights = sm(2, TT), sm(NE), sm(OVER_TILES)
        ranks, beyond, flag_f = sm(2 * TT), sm(2 * TT), sm(1)
        group_exp, gap4, gap, gate_sum, pair_sum = sm(TT, 4), sm(TT, 4), sm(TT), sm(TT), sm(TT)
        picked_rank, absent = sm(2 * TT, 16), sm(NE)
        assert at[0] <= 1000, at[0]
        at[0] = S5_END
        qss, qstd = sm(18), sm(18)
        kq_gain = sm(HD)
        am, ane, aes, asum = [sm(8) for _ in range(2)], [sm(8) for _ in range(2)], [sm(8) for _ in range(2)], [sm(8) for _ in range(2)]
        assert at[0] <= 1000

        const_in, param_in, cread_in = sem("const_in"), sem("param_in"), sem("cread_in")
        const_rest, param_rest = sem("const_rest"), sem("param_rest")
        x_in = [sem(f"x_in{i}") for i in range(TT)]
        slot_full = [sem(f"slot_full{i}") for i in range(RING)]
        slot_free = sem("slot_free")
        consts_set = sem("consts_set")
        std_done, rstd_done, xs_done = sem("std_done"), sem("rstd_done"), sem("xs_done")
        turned_psum, hT_done = sem("turned_psum"), sem("hT_done")
        turn_done, trig_done, bexp_done, bT_psum, bT_done = (sem("turn_done"), sem("trig_done"), sem("bexp_done"),
                                                             sem("bT_psum"), sem("bT_done"))
        lbsub, lbexped = sem("lbsub"), sem("lbexped")
        u_psum, u_done, proj_psum, proj_done = sem("u_psum"), sem("u_done"), sem("proj_psum"), sem("proj_done")
        phase_raw, phase_done, table_done = sem("phase_raw"), sem("phase_done"), sem("table_done")
        bu_done, prod_done, zin_done, out_prod, ab_done = (sem("bu_done"), sem("prod_done"), sem("zin_done"),
                                                           sem("out_prod"), sem("ab_done"))
        y_used, y_sum, gelu_done, glu_psum, glu_sig, a_done = (sem("y_used"), sem("y_sum"), sem("gelu_done"),
                                                               sem("glu_psum"), sem("glu_sig"), sem("a_done"))
        hg_act, hg_dve, hg_sub, hg_zero = sem("hg_act"), sem("hg_dve"), sem("hg_sub"), sem("hg_zero")
        keep_done, sum_done = sem("keep_done"), sem("sum_done")
        sc_psum, sc_done, ktr_psum, ktm_done, inc_psum, st_done, qm_done, o_psum, o_out = [
            sem(n) for n in ("sc_psum", "sc_done", "ktr_psum", "ktm_done", "inc_psum", "st_done", "qm_done", "o_psum", "o_out")]
        osq_done, ostd_done, on_done, otr_psum = [
            sem(n) for n in ("osq_done", "ostd_done", "on_done", "otr_psum")]
        mix_psum, mix_done = sem("mix_psum"), sem("mix_done")
        left_hi_done, left_lo_done = sem("left_hi_done"), sem("left_lo_done")
        w_hi_done, w_lo_done, w_used = sem("w_hi_done"), sem("w_lo_done"), sem("w_used")
        at_zero, qkv_psum, sqa_done, qstd_s, qkn_done, ss_a = [
            sem(n) for n in ("at_zero", "qkv_psum", "sqa_done", "qstd_s", "qkn_done", "ss_a")]
        qtr_psum, qT_done = sem("qtr_psum"), sem("qT_done")
        s_psum, s_biased, m_done, p_exp, p_norm, p_norm_odd, pt_psum, pt_done, att_psum, att_done = [
            sem(n) for n in ("s_psum", "s_biased", "m_done", "p_exp", "p_norm", "p_norm_odd", "pt_psum", "pt_done", "att_psum", "att_done")]
        tok_psum, tok_even, tok_odd = sem("tok_psum"), sem("tok_even"), sem("tok_odd")
        logit_psum, logit_read, gaps_done, exps_done, mask_done, rank_psum, hot_done, list_psum, route_done = [
            sem(n) for n in ("logit_psum", "logit_read", "gaps_done", "exps_done", "mask_done", "rank_psum", "hot_done", "list_psum",
                             "route_done")]
        flags_done, flag_psum, flag_set = sem("flags_done"), sem("flag_psum"), sem("flag_set")
        rows_in, got_row = sem("rows_in"), [sem(f"got_row{i}") for i in range(2)]
        xT_psum, xT_done, gu_psum, silu_done, hid_done, hidT_psum, hidT_done, y_psum2, yrow_done = [
            sem(n) for n in ("xT_psum", "xT_done", "gu_psum", "silu_done", "hid_done", "hidT_psum", "hidT_done",
                             "y_psum2", "yrow_done")]
        sums_in, weighed, weights_psum = sem("sums_in"), sem("weighed"), sem("weights_psum")
        x_back = [sem(f"x_back{i}") for i in range(TT)]
        stored = [sem(f"stored{i}") for i in range(2)]
        over = [{n: sem(f"over_{n}{layer}") for n in ("hot", "list_psum", "listed", "weights", "row", "xT_psum", "xT", "gate_up",
                                                      "silu", "hid", "hidT_psum", "hidT", "y_psum", "yrow", "stored")}
                for layer in range(2)]
        block = ctx.enter_context(nc.Block())

        def slot(i):
            return ring[:, (i % RING) * SLOT:(i % RING + 1) * SLOT]

        def if_over(engine, layer, body):
            engine.wait_ge(flag_set, layer + 1)
            count = engine.value_load(flag32[0:1, 0:1], min_val=0, max_val=2 * SEQ)
            with engine.If(count > 0):
                body(over[layer])

        def heads_out(tt, banks, copy, engine):
            for g in range(3):
                engine.wait_ge(qtr_psum, 3 * tt + g + 1)
                m = slice(tt * 128, tt * 128 + 128)
                if g < 2:
                    copy(qT1[:, 4 * g:4 * g + 4, m], PS[:, banks[g], :].rearrange("p (a b) -> p a b", b=128)).then_inc(qT_done, 1)
                else:
                    copy(kT1[:, 128 + tt * 128:256 + tt * 128], PS[:, banks[2], 0:128]).then_inc(qT_done, 1)

        def k512(i):
            return slot(i).rearrange("p (k n) -> p k n", n=512)

        @block.sync
        def _(sp):
            for tt in range(TT):
                sp.dma_start(x[:, tt, :], x_d[tt * P:(tt + 1) * P, :]).then_inc(x_in[tt], 16)
            for j in range(RING):
                sp.dma_start(slot(j), stream_d[j, :, :]).then_inc(slot_full[j], 16)
            with sp.Fori(1, N_SLOTS // RING) as i:
                for j in range(RING):
                    sp.wait_ge(slot_free, i * RING + (j - RING + 1))
                    sp.dma_start(slot(j), stream_d[bass.ds(i * RING + j, 1), :, :].rearrange("a p n -> (a p) n"))\
                        .then_inc(slot_full[j], 16)

        @block.gpsimd
        def _(pool):
            nc.gpsimd.memset(eps_t, EPS).then_inc(consts_set, 1)
            nc.gpsimd.memset(half_pi, math.pi / 2).then_inc(consts_set, 1)
            nc.gpsimd.memset(magic_t, MAGIC).then_inc(consts_set, 1)
            for i in range(PAIRS):
                pool.wait_ge(prod_done, i + 1)
                if i >= 1:
                    pool.wait_ge(out_prod, i)
                nc.gpsimd.tensor_tensor(zr, prod_in[0], prod_in[1], ALU.subtract)
                nc.gpsimd.tensor_tensor(zi, prod_in[2], prod_in[3], ALU.add).then_inc(zin_done, 1)
                if i >= 1:
                    q = prod_out[(i - 1) % 2]
                    nc.gpsimd.tensor_tensor(q[0], q[0], q[1], ALU.add)
                    nc.gpsimd.tensor_tensor(q[2], q[2], q[3], ALU.subtract).then_inc(ab_done, 1)
            f4 = fT.rearrange("p h (c j) -> p h c j", j=CH)

            def differences(h):
                pool.wait_ge(sum_done, h + 1)
                shape = [P, NCHUNK, CH]
                nc.gpsimd.tensor_tensor(ke2[:, h, :].rearrange("p (c j) -> p c j", j=CH), f4[:, h, :, :],
                                        f4[:, h, :, CH // 2 - 1:CH // 2].to_broadcast(shape), ALU.subtract).then_inc(hg_sub, 1)
                nc.gpsimd.tensor_tensor(ke3[:, h, :].rearrange("p (c j) -> p c j", j=CH),
                                        f4[:, h, :, CH - 1:CH].to_broadcast(shape), f4[:, h, :, :], ALU.subtract)\
                    .then_inc(hg_sub, 1)

            pool.wait_ge(proj_psum, PAIRS)
            pool.drain()
            differences(0)
            pool.wait_ge(out_prod, PAIRS)
            q = prod_out[(PAIRS - 1) % 2]
            nc.gpsimd.tensor_tensor(q[0], q[0], q[1], ALU.add)
            nc.gpsimd.tensor_tensor(q[2], q[2], q[3], ALU.subtract).then_inc(ab_done, 1)
            nc.gpsimd.memset(arena[:, 19968:20992], 0.0).then_inc(hg_zero, 1)
            differences(1)
            pool.wait_ge(y_used, PAIRS)
            nc.gpsimd.memset(q_masked[0], 0.0).then_inc(hg_zero, 1)
            nc.gpsimd.memset(q_masked[1], 0.0).then_inc(hg_zero, 1)
            differences(2)
            differences(3)
            pool.wait_ge(proj_done, 16)
            nc.gpsimd.tensor_tensor(cut(arena, 13312, 16, 128), cut(arena, 13312, 16, 128),
                                    par("o_gain").unsqueeze(1).to_broadcast([P, 16, 128]), ALU.mult).then_inc(hg_zero, 1)

            def send_rows(layer):
                pool.wait_ge(mix_psum, 8 * layer + 1)
                nc.gpsimd.memset(arena[:, 0:2048], 0.0)
                for tt in range(TT):
                    pool.wait_ge(rstd_done, TT * (2 * layer + 1) + tt + 1)
                    nc.gpsimd.tensor_scalar(rows[:, tt, :], x[:, tt, :], rstd[:, tt:tt + 1], None, ALU.mult)
                    pool.drain()
                    pool.dma_start(rows_d[tt * P:(tt + 1) * P, :], rows[:, tt, :]).then_inc(rows_in, 16)
                    pool.dma_start((sums_d, out_d)[layer][tt * P:(tt + 1) * P, :], x[:, tt, :]).then_inc(sums_in, 16)

            def fetch(j, index):
                return pool.indirect_dma_start(xrow[j], None, rows_d[:, :], bass.IndirectOffsetOnAxis(index, 0),
                                               bounds_check=SEQ - 1, oob_is_err=False)

            def store(layer, j, index):
                return pool.indirect_dma_start((sums_d, out_d)[layer][:, :], bass.IndirectOffsetOnAxis(index, 0), yrow[j], None,
                                               bounds_check=SEQ - 1, oob_is_err=False, compute_op=ALU.add)

            def experts(layer):
                send_rows(layer)
                pool.wait_ge(rows_in, 16 * TT * (layer + 1))
                pool.wait_ge(route_done, layer + 1)

                def fetch_rows(e):
                    if e >= 2:
                        pool.wait_ge(xT_psum, 2 * (layer * NE + e - 1))
                    fetch(e % 2, rows32[:, e:e + 1]).then_inc(got_row[e % 2], 16)

                for e in range(3):
                    fetch_rows(e)
                for e in range(NE):
                    if e + 3 < NE:
                        fetch_rows(e + 3)
                    if e == 0:
                        pool.wait_ge(sums_in, 16 * TT * (layer + 1))
                    else:
                        pool.wait_ge(stored[(e - 1) % 2], 16 * (NE // 2 * layer + (e - 1) // 2 + 1))
                    pool.wait_ge(yrow_done, layer * NE + e + 1)
                    store(layer, e % 2, rows32[:, e:e + 1]).then_inc(stored[e % 2], 16)

            def experts_over(layer):
                def body(s):
                    for j in range(2):
                        pool.wait_ge(stored[j], 16 * (NE // 2) * (layer + 1))
                    pool.wait_ge(s["listed"], OVER // P)

                    def expert(e, gate_up_at, down_at):
                        pool.dma_start(over_w[:, 0:2 * SLOT].rearrange("p (s n) -> p s n", n=SLOT),
                                       stream_d[bass.ds(gate_up_at, 2), :, :].rearrange("s p n -> p s n")).then_inc(s["weights"], 16)
                        pool.dma_start(over_w[:, 2 * SLOT:3 * SLOT],
                                       stream_d[bass.ds(down_at, 1), :, :].rearrange("a p n -> (a p) n")).then_inc(s["weights"], 16)
                        for r in range(OVER // P):
                            q = e * (OVER // P) + r
                            nc.gpsimd.tensor_copy(row_now[:, :], over32[:, bass.ds(q, 1)])
                            pool.drain()
                            fetch(0, row_now[:, :]).then_inc(s["row"], 16)
                            pool.wait_ge(s["yrow"], q + 1)
                            nc.gpsimd.tensor_copy(row_now[:, :], over32[:, bass.ds(q + OVER_TILES, 1)])
                            pool.drain()
                            store(layer, 0, row_now[:, :]).then_inc(s["stored"], 16)
                            pool.wait_ge(s["stored"], q * 16 + 16)

                    s0 = EXP0[layer]
                    expert(0, s0, s0 + 4)
                    with pool.Fori(1, NE - 1) as e:
                        expert(e, e * 3 + (s0 - 1), e * 3 + (s0 + 4))
                    expert(NE - 1, s0 + 3 * NE - 4, s0 + 3 * NE - 1)
                if_over(pool, layer, body)

            experts(0)
            experts_over(0)
            pool.wait_ge(x_back[TT - 1], 16)
            nc.gpsimd.memset(kT1[:, 0:128], 0.0)
            nc.gpsimd.memset(vpad, 0.0).then_inc(at_zero, 1)
            pool.wait_ge(w_hi_done, 5)
            nc.gpsimd.tensor_tensor(w_lo[0], slot(OUT1), w_hi[0], ALU.subtract).then_inc(w_lo_done, 1)
            for u in range(8):
                pool.wait_ge(m_done, 2 * (u + 1))
                pr = probs[u % 2].rearrange("p (j v) k -> p j v k", v=2)[:, :, 0, :]
                inverse = asum[u % 2].rearrange("p (j v) -> p j v", v=2)[:, :, 0:1].to_broadcast([P, 4, 256])
                nc.gpsimd.tensor_tensor(pr, pr, inverse, ALU.mult).then_inc(p_norm, 1)
            experts(1)
            for j in range(2):
                pool.wait_ge(stored[j], 16 * NE)
            experts_over(1)

        @block.scalar
        def _(act):
            act.dma_start(param[:, 0:FIRST_PARAM], param_d[:, 0:FIRST_PARAM]).then_inc(param_in, 16)
            act.dma_start(ident, const_d[:, 0:P]).then_inc(const_in, 16)

            def weights_hi(layer, s):
                i = (OUT0, OUT1)[layer] + s
                act.wait_ge(slot_full[i % RING], 16 * (i // RING + 1))
                if s == 2:
                    act.wait_ge(w_used, layer + 1)
                if s == 3:
                    act.wait_ge(mix_psum, 8 * layer + TT)
                act.activation(w_hi[s % 2], slot(i), ACT.Copy).then_inc(w_hi_done, 1)

            def deviation(occ, tt, squares):
                act.activation(squares[:, tt, :], x[:, tt, :], ACT.Square, accum_out=ssq[:, tt:tt + 1])
                act.drain()
                act.activation(std[:, tt:tt + 1], ssq[:, tt:tt + 1], ACT.Sqrt, bias=eps_t, scale=1.0 / D).then_inc(std_done, 1)

            def norm(occ):
                for tt in range(TT + 1):
                    if tt < TT:
                        if occ == 0:
                            act.wait_ge(x_in[tt], 16)
                        else:
                            act.wait_ge(x_back[tt], 16)
                        deviation(occ, tt, xs)
                    if tt >= 1:
                        act.wait_ge(rstd_done, TT * occ + tt)
                        act.activation(xs[:, tt - 1, :], x[:, tt - 1, :], ACT.Copy, scale=rstd[:, tt - 1:tt]).then_inc(xs_done, 1)

            def token_turns(layer):
                weights_hi(layer, 2)
                weights_hi(layer, 3)
                for tt in range(TT + 1):
                    if tt < TT:
                        act.wait_ge(mix_done, 8 * layer + TT + tt + 1)
                        deviation(2 * layer + 1, tt, rows)
                    if tt >= 1:
                        c = TT * layer + tt - 1
                        act.wait_ge(tok_psum, 2 * c + 1)
                        if tt >= 3:
                            act.wait_ge(logit_psum, c - 1)
                        act.activation(tokT[(tt - 1) % 2][:, 0:4, :], PS[:, 0, :].rearrange("p (a b) -> p a b", b=128),
                                       ACT.Copy).then_inc(tok_even, 1)

            act.wait_ge(consts_set, 3)
            norm(0)
            act.dma_start(param[:, FIRST_PARAM:], param_d[:, FIRST_PARAM:]).then_inc(param_rest, 16)
            act.dma_start(const[:, P:], const_d[:, P:]).then_inc(const_rest, 16)
            act.dma_start(arena[:, 3072:4096], cread_d).then_inc(cread_in, 16)
            act.wait_ge(turn_done, 1)
            act.activation(sin1, turn, ACT.Sin, scale=TWO_PI)
            act.activation(cos1, turn, ACT.Abs)
            act.drain()
            act.activation(cos1, cos1, ACT.Sin, scale=-TWO_PI, bias=half_pi).then_inc(trig_done, 1)
            act.wait_ge(lbsub, 1)
            act.activation(lbexp, lbexp, ACT.Exp).then_inc(lbexped, 1)
            for cb in range(4):
                act.wait_ge(u_psum, cb + 1)
                act.activation(uT[:, cb, :], PS[:, 2 + cb % 2, :], ACT.Copy).then_inc(u_done, 1)

            def phase(i):
                if i >= 3:
                    act.wait_ge(out_prod, i - 2)
                act.activation(nsinT[i % 3], con("time"), ACT.Identity, scale=turn[:, i:i + 1], bias=magic_t)
                act.activation(cosT[i % 3], con("time"), ACT.Copy, scale=turn_hi[:, i:i + 1]).then_inc(phase_raw, 1)

            def table(i):
                act.wait_ge(phase_done, i + 1)
                act.activation(nsinT[i % 3], cosT[i % 3], ACT.Sin, scale=-TWO_PI)
                act.drain()
                act.activation(cosT[i % 3], cosT[i % 3], ACT.Abs)
                act.drain()
                act.activation(cosT[i % 3], cosT[i % 3], ACT.Sin, scale=-TWO_PI, bias=half_pi).then_inc(table_done, 1)

            act.wait_ge(turned_psum, 2 * TT)
            act.wait_ge(const_rest, 16)
            phase(0)
            phase(1)
            table(0)
            for i in range(PAIRS):
                if i + 2 < PAIRS:
                    phase(i + 2)
                if i + 1 < PAIRS:
                    table(i + 1)
                act.wait_ge(proj_psum, i + 1)
                dst = (fT, qT0, v_tm, g_tm)[i // 4][:, i % 4, :]
                act.activation(dst, PS[:, 6 + i % 2, :], ACT.Silu if i // 4 in (1, 3) else ACT.Copy).then_inc(proj_done, 1)
                if i == 4:
                    act.activation(fT, fT, ACT.Sigmoid).then_inc(hg_act, 1)
                if i == 7:
                    act.wait_ge(keep_done, 1)
                    act.activation(fT, fT, ACT.Ln).then_inc(hg_act, 1)
            def exponentials(h):
                act.wait_ge(hg_sub, 2 * h + 2)
                act.activation(qe1[:, h, :], ke2[:, h, :], ACT.Exp).then_inc(hg_act, 1)
                act.drain()
                act.activation(ke2[:, h, :], ke2[:, h, :], ACT.Exp, scale=-1.0).then_inc(hg_act, 1)
                act.activation(ke3[:, h, :], ke3[:, h, :], ACT.Exp).then_inc(hg_act, 1)
                act.activation(decay[:, h, :], fT[:, h, :].rearrange("p (c j) -> p c j", j=CH)[:, :, CH - 1], ACT.Exp)
                act.drain()
                act.activation(fT[:, h, :], fT[:, h, :], ACT.Exp).then_inc(hg_act, 1)

            def keys_out(h):
                act.wait_ge(ktr_psum, h + 1)
                act.activation(ke3_tm[h % 2], PS[:, 2, :].rearrange("p (a b) -> p a b", b=128), ACT.Copy).then_inc(ktm_done, 1)

            def output_out(h):
                act.wait_ge(o_psum, h + 1)
                act.activation(o_all[:, h, :], PS[:, 7, :], ACT.Copy).then_inc(o_out, 1)

            exponentials(0)
            exponentials(1)
            keys_out(0)
            exponentials(2)
            keys_out(1)
            exponentials(3)
            for b in range(4):
                act.wait_ge(y_sum, b + 1)
                act.activation(catT[:, b, :], catT[:, b, :], ACT.Gelu_apprx_tanh).then_inc(gelu_done, 1)
            for h in range(HEADS):
                output_out(h)
                if h + 2 < HEADS:
                    keys_out(h + 2)
            act.drain()
            act.activation(sq0, o_all, ACT.Square).then_inc(osq_done, 1)
            weights_hi(0, 0)
            act.wait_ge(osq_done, 2)
            act.activation(ostd, ossq, ACT.Sqrt, bias=eps_t, scale=1.0 / 128).then_inc(ostd_done, 1)
            for b in range(4):
                act.wait_ge(glu_psum, b + 1)
                act.activation(uT[:, b, :], PS[:, (0, 1, 4, 5)[b], :], ACT.Sigmoid).then_inc(glu_sig, 1)
            for b in range(4):
                act.wait_ge(a_done, b + 1)
                act.activation(left_hi[:, b, :], catT[:, b, :], ACT.Copy).then_inc(left_hi_done, 1)
            for h in range(HEADS):
                act.wait_ge(otr_psum, h + 1)
                act.activation(left_hi[:, 4 + h, :], PS[:, 2 + h % 2, :], ACT.Copy).then_inc(left_hi_done, 1)
            weights_hi(0, 1)

            def experts(layer):
                act.wait_ge(gaps_done, layer + 1)
                act.activation(group_exp, group_exp, ACT.Exp)
                act.activation(gap, gap, ACT.Exp).then_inc(exps_done, 1)
                base = layer * NE

                def silu(n):
                    act.wait_ge(gu_psum, n + 1)
                    act.activation(gate_s, PS[:, 2, 0:FE], ACT.Silu).then_inc(silu_done, 1)

                def rows(j, n, held):
                    act.wait_ge(y_psum2, n + 1)
                    if held is not None:
                        act.wait_ge(stored[j], held)
                    act.activation(yrow[j], PS[:, 4:6, :].rearrange("p a b -> p (a b)"), ACT.Copy).then_inc(yrow_done, 1)

                silu(base)
                for e in range(2):
                    silu(base + e + 1)
                    rows(e, base + e, 8 * base if layer else None)
                with act.Fori(1, NE // 2 - 1) as it:
                    for j in range(2):
                        n = it * 2 + (base + j)
                        silu(n + 1)
                        rows(j, n, (it + base // 2) * 16)
                silu(base + NE - 1)
                rows(0, base + NE - 2, 8 * (base + NE - 2))
                rows(1, base + NE - 1, 8 * (base + NE - 2))

            def experts_over(layer):
                def body(s):
                    with act.Fori(0, OVER_TILES) as q:
                        act.wait_ge(s["gate_up"], q + 1)
                        act.activation(gate_s, PS[:, 2, 0:FE], ACT.Silu).then_inc(s["silu"], 1)
                        act.wait_ge(s["y_psum"], q + 1)
                        act.activation(yrow[0], PS[:, 4:6, :].rearrange("p a b -> p (a b)"), ACT.Copy).then_inc(s["yrow"], 1)
                    act.wait_ge(s["stored"], 16 * OVER_TILES)
                if_over(act, layer, body)

            def load_sums():
                for j in range(2):
                    act.wait_ge(stored[j], 16 * (NE // 2))
                for tt in range(TT):
                    act.dma_start(x[:, tt, :], sums_d[P * tt:P * (tt + 1), :]).then_inc(x_back[tt], 16)

            token_turns(0)
            experts(0)
            experts_over(0)
            load_sums()
            norm(2)
            act.wait_ge(at_zero, 1)
            for tt in range(TT):
                act.wait_ge(qkv_psum, tt + 1)
                if tt:
                    act.wait_ge(ss_a, tt)
                b = 2 + 3 * (tt % 2)
                act.activation(sq1, PS[:, b:b + 2, :].rearrange("p a b -> p (a b)"), ACT.Square)
                act.activation(arena[:, 1024:1152], PS[:, b + 2, 0:128], ACT.Square).then_inc(sqa_done, 1)
                act.activation(vpad[:, 1 + tt, 0, 0:64], PS[:, b + 2, 128:192], ACT.Copy)
                act.activation(vpad[:, 1 + tt, 1, 64:128], PS[:, b + 2, 192:256], ACT.Copy)
                act.wait_ge(ss_a, tt + 1)
                act.activation(qstd, qss, ACT.Sqrt, bias=eps_t, scale=1.0 / HD).then_inc(qstd_s, 1)
            weights_hi(1, 0)
            for tt in (2, 3):
                heads_out(tt, (5, 6, 7), lambda out, src: act.activation(out, src, ACT.Copy), act)
            for u in range(8):
                pr = probs[u % 2]
                act.wait_ge(m_done, 2 * u + 1)
                for h in range(8):
                    act.activation(pr[:, h, :], pr[:, h, :], ACT.Exp, bias=am[u % 2][:, h:h + 1],
                                   accum_out=aes[u % 2][:, h:h + 1])
                act.activation(ane[u % 2], ane[u % 2], ACT.Exp).then_inc(p_exp, 1)
                if u >= 1:
                    act.wait_ge(att_psum, u)
                    nn, jj = (u - 1) // 2, (u - 1) % 2
                    act.activation(left_hi[:, 4 * jj:4 * jj + 4, nn * 128:nn * 128 + 128],
                                   PS[:, 4, :].rearrange("p (a b) -> p a b", b=128), ACT.Copy).then_inc(att_done, 1)
                act.wait_ge(m_done, 2 * (u + 1))
                for h in range(1, 8, 2):
                    ins = act.activation(pr[:, h, :], pr[:, h, :], ACT.Copy, scale=asum[u % 2][:, h:h + 1])
                ins.then_inc(p_norm_odd, 1)
                for b in range(4):
                    act.wait_ge(pt_psum, 4 * u + b + 1)
                    act.activation(probsT[u % 2][:, b, :], PS[:, 5 + b % 2, :], ACT.Copy).then_inc(pt_done, 1)
            act.wait_ge(att_psum, 8)
            act.activation(left_hi[:, 4:8, 384:512], PS[:, 4, :].rearrange("p (a b) -> p a b", b=128), ACT.Copy)\
                .then_inc(att_done, 1)
            weights_hi(1, 1)
            token_turns(1)
            experts(1)
            experts_over(1)

        @block.vector
        def _(dve):
            V = nc.vector

            def tt_(out, a, b, op):
                return V.tensor_tensor(out, a, b, op)

            def ts(out, a, s1, op0, s2=None, op1=None):
                return V.tensor_scalar(out, a, s1, s2, op0, op1) if op1 is not None else V.tensor_scalar(out, a, s1, None, op0)

            def stt(out, a, s, b, op0, op1):
                return V.scalar_tensor_tensor(out, a, s, b, op0, op1)

            def exact_exp(out, z, k, r, n):
                ts(r, z, -87.0, ALU.max, 88.0, ALU.min)
                dve.drain()
                ts(k, r, math.log2(math.e), ALU.mult, MAGIC, ALU.add)
                dve.drain()
                ts(k, k, MAGIC, ALU.subtract)
                dve.drain()
                stt(r, k, -0.693359375, r, ALU.mult, ALU.add)
                dve.drain()
                stt(r, k, 2.12194440e-4, r, ALU.mult, ALU.add)
                dve.drain()
                ts(out, r, 1.0 / 5040, ALU.mult)
                for c in (1.0 / 720, 1.0 / 120, 1.0 / 24, 1.0 / 6, 0.5, 1.0):
                    dve.drain()
                    stt(out, out, c, r, ALU.add, ALU.mult)
                dve.drain()
                ts(r, k, 127.0, ALU.add, 8388608.0, ALU.mult)
                dve.drain()
                V.tensor_copy(k.bitcast(i32), r)
                dve.drain()
                stt(out, out, 1.0, k, ALU.add, ALU.mult)
                dve.drain()

            def inverse(occ, tt):
                dve.wait_ge(std_done, TT * occ + tt + 1)
                V.reciprocal(rstd[:, tt:tt + 1], std[:, tt:tt + 1]).then_inc(rstd_done, 1)

            def scaled(mixer, tt):
                for b in range(2):
                    dve.wait_ge(turned_psum, 2 * (TT * mixer + tt) + b + 1)
                    tt_(hT[:, 4 * b:4 * b + 4, tt * 128:tt * 128 + 128], PS[:, b, :].rearrange("p (a b) -> p a b", b=128),
                        par(f"gain{2 * mixer}")[:, 4 * b:4 * b + 4].unsqueeze(2).to_broadcast([P, 4, 128]), ALU.mult)\
                        .then_inc(hT_done, 1)

            dve.wait_ge(param_in, 16)
            for tt in range(TT + 1):
                if tt < TT:
                    inverse(0, tt)
                if tt >= 1:
                    scaled(0, tt - 1)
            def weights_lo(layer, s):
                dve.wait_ge(w_hi_done, 4 * layer + s + 1)
                tt_(w_lo[s % 2], slot((OUT0, OUT1)[layer] + s), w_hi[s % 2], ALU.subtract).then_inc(w_lo_done, 1)

            lr, li = par("lam_re"), par("lam_im")
            t0, t1, t2, t3, t4, t5, t6, t7 = s5tmp
            exact_exp(step_t, par("log_step"), t0, t1, PAIRS)
            tt_(t2, lr, step_t, ALU.mult)
            tt_(t3, li, step_t, ALU.mult)
            dve.drain()
            exact_exp(mag, t2, t0, t1, PAIRS)
            ts(t3, t3, 1.0 / (2 * math.pi), ALU.mult)
            dve.drain()
            ts(t0, t3, MAGIC, ALU.add)
            dve.drain()
            ts(t0, t0, MAGIC, ALU.subtract)
            dve.drain()
            tt_(turn, t3, t0, ALU.subtract).then_inc(turn_done, 1)
            dve.drain()
            ts(t0, turn, MAGIC12, ALU.add)
            dve.drain()
            ts(turn_hi, t0, MAGIC12, ALU.subtract)
            dve.drain()
            tt_(turn_lo, turn, turn_hi, ALU.subtract)
            tt_(t0, lr, lr, ALU.mult)
            tt_(t1, li, li, ALU.mult)
            dve.drain()
            tt_(t0, t0, t1, ALU.add)
            dve.drain()
            V.reciprocal(t0, t0)
            raw = par("bounds").rearrange("p (a b) -> p a b", b=HEADS)
            tt_(lbmax, raw[:, 0, :], raw[:, 1, :], ALU.max)
            dve.drain()
            tt_(lbmax, lbmax, raw[:, 2, :], ALU.max)
            dve.drain()
            tt_(lbexp, raw, lbmax.unsqueeze(1).to_broadcast([P, 3, HEADS]), ALU.subtract).then_inc(lbsub, 1)
            dve.wait_ge(trig_done, 1)
            tt_(t2, mag, cos1, ALU.mult)
            tt_(t3, mag, sin1, ALU.mult)
            dve.drain()
            ts(t2, t2, 1.0, ALU.subtract)
            dve.drain()
            tt_(t4, t2, lr, ALU.mult)
            tt_(t5, t3, li, ALU.mult)
            tt_(t6, t3, lr, ALU.mult)
            tt_(t7, t2, li, ALU.mult)
            dve.drain()
            tt_(t4, t4, t5, ALU.add)
            tt_(t6, t6, t7, ALU.subtract)
            dve.drain()
            tt_(t4, t4, t0, ALU.mult)
            tt_(t6, t6, t0, ALU.mult)
            dve.drain()
            dve.wait_ge(param_rest, 16)
            br = par("b_re").rearrange("p (a b) -> p a b", b=32)
            bi = par("b_im").rearrange("p (a b) -> p a b", b=32)
            z_re = t4.unsqueeze(2).to_broadcast([P, PAIRS, 32])
            z_im = t6.unsqueeze(2).to_broadcast([P, PAIRS, 32])
            w = [cut(arena, 15360 + 512 * i, PAIRS, 32) for i in range(4)]
            tt_(w[0], br, z_re, ALU.mult)
            tt_(w[1], bi, z_im, ALU.mult)
            tt_(w[2], bi, z_re, ALU.mult)
            tt_(w[3], br, z_im, ALU.mult)
            dve.drain()
            tt_(w[0], w[0], w[1], ALU.subtract)
            tt_(w[2], w[2], w[3], ALU.add).then_inc(bexp_done, 1)
            dve.wait_ge(lbexped, 1)
            tt_(lb, lbexp[:, 0, :], lbexp[:, 1, :], ALU.add)
            dve.drain()
            tt_(lb, lb, lbexp[:, 2, :], ALU.add)
            dve.drain()
            V.reciprocal(lb, lb)
            dve.drain()
            tt_(lb, lb, lbexp[:, 0, :], ALU.mult)
            dve.drain()
            ts(one_lb, lb, -1.0, ALU.mult, 1.0, ALU.add)
            for layer in range(2):
                w = par(f"router{layer}").rearrange("p (k n) -> p k n", n=20)
                tt_(w, w, par(f"gain{2 * layer + 1}").unsqueeze(2).to_broadcast([P, KD, 20]), ALU.mult)
            dve.wait_ge(const_rest, 16)
            dve.wait_ge(bT_psum, 1)
            V.tensor_copy(BT, PS[:, 6:8, :].rearrange("p a (b c) -> p a b c", c=128)).then_inc(bT_done, 1)
            def phase(i):
                c, ns = cosT[i % 3], nsinT[i % 3]
                dve.wait_ge(phase_raw, i + 1)
                stt(c, ns, MAGIC, c, ALU.subtract, ALU.subtract)
                dve.drain()
                stt(c, con("time"), turn_lo[:, i:i + 1], c, ALU.mult, ALU.subtract)
                dve.drain()
                ts(c, c, 0.5, ALU.min, -0.5, ALU.max).then_inc(phase_done, 1)

            def products_in(i):
                c, ns = cosT[i % 3], nsinT[i % 3]
                re, im = PS[:, 2 * (i % 2), :], PS[:, 2 * (i % 2) + 1, :]
                dve.wait_ge(table_done, i + 1)
                dve.wait_ge(bu_done, i + 1)
                if i >= 1:
                    dve.wait_ge(zin_done, i)
                tt_(prod_in[0], re, c, ALU.mult)
                tt_(prod_in[1], im, ns, ALU.mult)
                tt_(prod_in[2], im, c, ALU.mult)
                tt_(prod_in[3], re, ns, ALU.mult).then_inc(prod_done, 1)

            def scan_and_products(i):
                c, ns, q = cosT[i % 3], nsinT[i % 3], prod_out[i % 2]
                dve.wait_ge(zin_done, i + 1)
                m = mag[:, i:i + 1].to_broadcast([P, 512])
                V.tensor_tensor_scan(zr, m, zr, 0.0, ALU.mult, ALU.add)
                V.tensor_tensor_scan(zi, m, zi, 0.0, ALU.mult, ALU.add)
                dve.drain()
                if i >= 2:
                    dve.wait_ge(y_used, i - 1)
                tt_(q[0], zr, c, ALU.mult)
                tt_(q[1], zi, ns, ALU.mult)
                tt_(q[2], zr, ns, ALU.mult)
                tt_(q[3], zi, c, ALU.mult).then_inc(out_prod, 1)

            def skip(b):
                dve.wait_ge(y_used, 4 * (b + 1))
                stt(catT[:, b, :], uT[:, b, :], par("d_skip")[:, b:b + 1], PS[:, 4 + b % 2, :], ALU.mult, ALU.add)\
                    .then_inc(y_sum, 1)

            def forget():
                dve.wait_ge(hg_act, 1)
                for h in range(HEADS):
                    ts(fT[:, h, :], fT[:, h, :], one_lb[:, h:h + 1], ALU.mult, lb[:, h:h + 1], ALU.add)
                dve.drain()
                ts(keep_k, fT, -1.0, ALU.mult, 1.0, ALU.add).then_inc(keep_done, 1)

            def summed_logs(h):
                dve.wait_ge(hg_act, 2)
                V.tensor_tensor_scan(fT[:, h, :], con("chunk_reset"), fT[:, h, :], 0.0, ALU.mult, ALU.add).then_inc(sum_done, 1)

            phase(0)
            phase(1)
            products_in(0)
            for i in range(PAIRS):
                if i + 2 < PAIRS:
                    phase(i + 2)
                if i + 1 < PAIRS:
                    products_in(i + 1)
                scan_and_products(i)
                if i % 4 == 2 and i > 4:
                    skip(i // 4 - 1)
                if i == 5:
                    forget()
                if 8 <= i < 8 + HEADS:
                    summed_logs(i - 8)
            def keyed(h):
                dve.wait_ge(hg_act, 4 * h + 3)
                tt_(qe1[:, h, :], qe1[:, h, :], qT0[:, h, :], ALU.mult)
                dve.wait_ge(hg_act, 4 * h + 4)
                tt_(ke2[:, h, :], ke2[:, h, :], keep_k[:, h, :], ALU.mult).then_inc(hg_dve, 1)
                dve.wait_ge(hg_act, 4 * h + 5)
                tt_(ke3[:, h, :], ke3[:, h, :], keep_k[:, h, :], ALU.mult).then_inc(hg_dve, 1)

            def masked(h):
                dve.wait_ge(hg_act, 4 * h + 6)
                if h < 2:
                    dve.wait_ge(hg_zero, h + 2)
                else:
                    dve.wait_ge(o_psum, h - 1)
                for blk in range(4):
                    diagonal = q_masked[h % 2][:, 640 * blk:640 * blk + 640].rearrange("p (c d) -> p c d", d=160)[:, :, 0:CH]
                    ins = tt_(diagonal, qT0[:, h, blk * 128:blk * 128 + 128].rearrange("p (c j) -> p c j", j=CH),
                              fT[:, h, blk * 128:blk * 128 + 128].rearrange("p (c j) -> p c j", j=CH), ALU.mult)
                ins.then_inc(qm_done, 1)

            def causal(h):
                dve.wait_ge(sc_psum, h + 1)
                for blk in range(4):
                    ins = V.copy_predicated(scores[h % 2][:, blk, :], con("chunk_causal").bitcast(i32),
                                            PS[:, h % 2, blk * 128:blk * 128 + 128])
                ins.then_inc(sc_done, 1)

            def states(h):
                st = state[h % 2]
                dve.wait_ge(inc_psum, h + 1)
                if h >= 2:
                    dve.wait_ge(o_psum, h - 1)
                V.tensor_copy(st[:, 0, :], PS[:, 3, 0:128])
                for c in range(1, NCHUNK - 1):
                    dve.drain()
                    ins = stt(st[:, c, :], st[:, c - 1, :], decay[:, h, c:c + 1],
                              PS[:, 3 + c % 4, (c // 4) * 128:(c // 4) * 128 + 128], ALU.mult, ALU.add)
                ins.then_inc(st_done, 1)

            keyed(0)
            skip(3)
            masked(0)
            keyed(1)
            causal(0)
            for h in range(HEADS):
                states(h)
                if h + 1 < HEADS:
                    masked(h + 1)
                    causal(h + 1)
                if h + 2 < HEADS:
                    keyed(h + 2)
            dve.wait_ge(osq_done, 1)
            V.reduce_sum(ossq, sq0.rearrange("p (a b) -> p a b", b=128), AX.X).then_inc(osq_done, 1)
            dve.wait_ge(ostd_done, 1)
            V.reciprocal(ostd, ostd)
            dve.drain()
            o16 = cut(hT_t, 0, 16, 128)
            tt_(o16, o16, ostd.unsqueeze(2).to_broadcast([P, 16, 128]), ALU.mult)
            dve.drain()
            dve.wait_ge(hg_zero, 4)
            for h in range(HEADS):
                tt_(o_all[:, h, :].rearrange("p (a b) -> p a b", b=128), o_all[:, h, :].rearrange("p (a b) -> p a b", b=128),
                    g_tm[:, :, h * 128:h * 128 + 128], ALU.mult).then_inc(on_done, 1)
            weights_lo(0, 0)
            for b in range(4):
                dve.wait_ge(glu_sig, b + 1)
                if b == 0:
                    dve.wait_ge(glu_psum, 4)
                tt_(catT[:, b, :], catT[:, b, :], uT[:, b, :], ALU.mult).then_inc(a_done, 1)
            for b in range(4):
                dve.wait_ge(left_hi_done, b + 1)
                tt_(left_lo[:, 4 + b, :], catT[:, b, :], left_hi[:, b, :], ALU.subtract).then_inc(left_lo_done, 1)
            for h in range(HEADS):
                dve.wait_ge(left_hi_done, 4 + h + 1)
                tt_(left_lo[:, h, :], PS[:, 2 + h % 2, :], left_hi[:, 4 + h, :], ALU.subtract).then_inc(left_lo_done, 1)
            weights_lo(0, 1)

            def residual(layer):
                def second_half(tt):
                    c = TT * layer + tt
                    dve.wait_ge(tok_psum, 2 * c + 2)
                    if tt >= 2:
                        dve.wait_ge(logit_psum, c - 1)
                    V.tensor_copy(tokT[tt % 2][:, 4:8, :], PS[:, 1, :].rearrange("p (a b) -> p a b", b=128)).then_inc(tok_odd, 1)

                def logits(tt):
                    dve.wait_ge(logit_psum, TT * layer + tt + 1)
                    stt(logit[:, 5 * tt:5 * tt + 5, :], PS[:, 2 + tt % 2, 0:20].rearrange("p (a b) -> p a b", b=4),
                        rstd[:, tt:tt + 1], par(f"bias{layer}").rearrange("p (a b) -> p a b", b=4), ALU.mult, ALU.add)\
                        .then_inc(logit_read, 1)

                def add(half, tt):
                    dve.wait_ge(mix_psum, 8 * layer + TT * half + tt + 1)
                    xv = x[:, tt, half * 512:half * 512 + 512]
                    tt_(xv, xv, PS[:, 4 + tt, :], ALU.add).then_inc(mix_done, 1)

                weights_lo(layer, 2)
                for tt in range(TT):
                    add(0, tt)
                weights_lo(layer, 3)
                for tt in range(TT + 2):
                    if tt < TT:
                        add(1, tt)
                        inverse(2 * layer + 1, tt)
                    if 1 <= tt <= TT:
                        second_half(tt - 1)
                    if tt >= 2:
                        logits(tt - 2)

            def list_rows(into):
                listed = PS[:, 3, 128:128 + NE]
                ts(absent, listed, 0.5, ALU.is_lt, 2.0e6, ALU.mult)
                dve.drain()
                return stt(into, absent, -1.0, listed, ALU.add, ALU.add)

            def hot_ranks():
                return tt_(rank_hot, con("time")[:, 0:128].unsqueeze(1).to_broadcast([P, 2 * TT, 128]),
                           ranks.unsqueeze(2).to_broadcast([P, 2 * TT, 128]), ALU.is_equal)

            def route(layer):
                def first_max(values, n, most, place, scratch, hot):
                    iota = con("iota4").unsqueeze(1).to_broadcast([P, n, 4])
                    V.reduce_max(most, values, AX.X)
                    dve.drain()
                    tt_(scratch, values, most.unsqueeze(2).to_broadcast([P, n, 4]), ALU.is_lt)
                    dve.drain()
                    stt(scratch, scratch, 64.0, iota, ALU.mult, ALU.add)
                    dve.drain()
                    V.tensor_reduce(place, scratch, AX.X, ALU.min)
                    dve.drain()
                    tt_(hot, iota, place.unsqueeze(2).to_broadcast([P, n, 4]), ALU.is_equal)
                    dve.drain()

                def tiles5(v):
                    return v.rearrange("p (t g) e -> p t g e", g=5)

                def tiles4(v):
                    return v.rearrange("p (t g) e -> p t g e", g=4)

                dve.drain()
                first_max(logit, TT * 5, top, top_at, below, first_hot)
                stt(tiles4(rest), tiles5(first_hot)[:, :, 1:5, :], -3.0e38, tiles5(logit)[:, :, 1:5, :], ALU.mult, ALU.add)
                group_hot = tiles5(first_hot)[:, :, 0, :]
                group16 = group_hot.unsqueeze(3).to_broadcast([P, TT, 4, 4])
                tt_(picks[:, 0, :, :].rearrange("p t (g e) -> p t g e", e=4), tiles5(first_hot)[:, :, 1:5, :], group16, ALU.mult)
                dve.drain()
                first_max(rest, TT * 4, top2, top2_at, below2, second_hot)
                tt_(picks[:, 1, :, :].rearrange("p t (g e) -> p t g e", e=4), tiles4(second_hot), group16, ALU.mult)
                dve.drain()
                tt_(taken, picks[:, 0, :, :], picks[:, 1, :, :], ALU.add).then_inc(mask_done, 1)
                top5 = top.rearrange("p (t g) -> p t g", g=5)
                picks8 = picks.rearrange("p a t e -> p (a t) e")
                tt_(row_values, picks8, con("row_of").unsqueeze(2).to_broadcast([P, 2 * TT, 16]), ALU.mult)
                tt_(group_exp, tiles5(logit)[:, :, 0, :], top5[:, :, 0:1].to_broadcast([P, TT, 4]), ALU.subtract)
                tt_(gap4, top2.rearrange("p (t g) -> p t g", g=4), top5[:, :, 1:5], ALU.subtract)
                dve.wait_ge(rank_psum, layer + 1)
                tt_(picked_rank.rearrange("p (a t) e -> p a t e", a=2), picks,
                    PS[:, 3, 0:64].rearrange("p (t e) -> p t e", e=16).unsqueeze(1).to_broadcast([P, 2, TT, 16]), ALU.mult)
                dve.drain()
                V.reduce_sum(ranks, picked_rank, AX.X)
                dve.drain()
                hot_ranks().then_inc(hot_done, 1)
                tt_(gap4, gap4, group_hot, ALU.mult)
                ts(beyond, ranks, float(CAP), ALU.is_ge)
                dve.drain()
                V.reduce_sum(gap, gap4, AX.X).then_inc(gaps_done, 1)
                V.reduce_sum(flag_f, beyond, AX.X).then_inc(flags_done, 1)
                dve.wait_ge(list_psum, layer + 1)
                list_rows(rows32[:, :]).then_inc(route_done, 1)
                dve.wait_ge(exps_done, layer + 1)
                V.reduce_sum(gate_sum, group_exp, AX.X)
                ts(pair_sum, gap, 1.0, ALU.add)
                dve.drain()
                tt_(gate_sum, gate_sum, pair_sum, ALU.mult)
                dve.drain()
                V.reciprocal(w_pair[:, 0, :], gate_sum)
                dve.drain()
                tt_(w_pair[:, 1, :], w_pair[:, 0, :], gap, ALU.mult)
                dve.drain()
                tt_(weight_values, picks8, w_pair.rearrange("p a t -> p (a t)").unsqueeze(2).to_broadcast([P, 2 * TT, 16]),
                    ALU.mult).then_inc(weighed, 1)
                dve.wait_ge(weights_psum, layer + 1)
                V.tensor_copy(w_rows, PS[:, 3, 144:144 + NE])
                dve.wait_ge(flag_psum, layer + 1)
                V.tensor_copy(flag32[:, 0:1], PS[:, 2, 0:1]).then_inc(flag_set, 1)

            def experts(layer):
                base = layer * NE

                def turn_rows(j, n):
                    for b in range(2):
                        dve.wait_ge(xT_psum, n * 2 + (b + 1))
                        tt_(xT[j][:, 4 * b:4 * b + 4, :], PS[:, b, :].rearrange("p (a b) -> p a b", b=128),
                            par(f"gain{2 * layer + 1}")[:, 4 * b:4 * b + 4].unsqueeze(2).to_broadcast([P, 4, 128]),
                            ALU.mult).then_inc(xT_done, 1)

                def gated(n, e):
                    dve.wait_ge(silu_done, n + 1)
                    stt(hid, gate_s, w_rows[:, bass.ds(e, 1)], PS[:, 2, FE:2 * FE], ALU.mult, ALU.mult).then_inc(hid_done, 1)

                def turned_hidden(n):
                    dve.wait_ge(hidT_psum, n + 1)
                    V.tensor_copy(hidT, PS[:, 3, 0:256].rearrange("p (a b) -> p a b", b=128)).then_inc(hidT_done, 1)

                turn_rows(0, base)
                gated(base, 0)
                turn_rows(1, base + 1)
                with dve.Fori(0, NE // 2 - 1) as it:
                    for j in range(2):
                        n = it * 2 + (base + j)
                        turned_hidden(n)
                        gated(n + 1, it * 2 + (j + 1))
                        turn_rows(j, n + 2)
                turned_hidden(base + NE - 2)
                gated(base + NE - 1, NE - 1)
                turned_hidden(base + NE - 1)

            def experts_over(layer):
                def body(s):
                    for r in range(OVER // P):
                        ts(ranks, ranks, float(P), ALU.subtract)
                        dve.drain()
                        hot_ranks().then_inc(s["hot"], 1)
                        dve.wait_ge(s["list_psum"], r + 1)
                        V.tensor_copy(over_weights.rearrange("p (e r) -> p e r", r=OVER // P)[:, :, r], PS[:, 3, 144:144 + NE])
                        for at in (0, OVER_TILES):
                            ins = list_rows(over32[:, at:at + OVER_TILES].rearrange("p (e r) -> p e r", r=OVER // P)[:, :, r])
                            if at == 0:
                                dve.drain()
                        ins.then_inc(s["listed"], 1)
                    with dve.Fori(0, OVER_TILES) as q:
                        dve.wait_ge(s["xT_psum"], q + 1)
                        for b in range(2):
                            ins = tt_(xT[0][:, 4 * b:4 * b + 4, :], PS[:, b, :].rearrange("p (a b) -> p a b", b=128),
                                      par(f"gain{2 * layer + 1}")[:, 4 * b:4 * b + 4].unsqueeze(2).to_broadcast([P, 4, 128]),
                                      ALU.mult)
                        ins.then_inc(s["xT"], 1)
                        dve.wait_ge(s["silu"], q + 1)
                        stt(hid, gate_s, over_weights[:, bass.ds(q, 1)], PS[:, 2, FE:2 * FE], ALU.mult, ALU.mult).then_inc(s["hid"], 1)
                        dve.wait_ge(s["hidT_psum"], q + 1)
                        V.tensor_copy(hidT, PS[:, 3, 0:256].rearrange("p (a b) -> p a b", b=128)).then_inc(s["hidT"], 1)
                if_over(dve, layer, body)

            residual(0)
            route(0)
            experts(0)
            experts_over(0)
            for tt in range(TT + 1):
                if tt < TT:
                    inverse(2, tt)
                if tt >= 1:
                    scaled(1, tt - 1)
            ts(kq_gain, par("q_gain"), HD ** -0.5, ALU.mult)
            for tt in range(TT):
                if tt in (1, 2):
                    heads_out(tt - 1, (0, 1, 0), V.tensor_copy, dve)
                b = 2 + 3 * (tt % 2)
                dve.wait_ge(sqa_done, tt + 1)
                V.reduce_sum(qss, arena[:, 0:1152].rearrange("p (a b) -> p a b", b=HD), AX.X).then_inc(ss_a, 1)
                dve.wait_ge(qstd_s, tt + 1)
                V.reciprocal(qstd, qstd)
                dve.drain()
                qv = qn[:, tt, :].rearrange("p (a b) -> p a b", b=HD)
                tt_(qv, PS[:, b:b + 2, :].rearrange("p a (c d) -> p (a c) d", d=HD),
                    qstd[:, 0:16].unsqueeze(2).to_broadcast([P, 16, HD]), ALU.mult)
                kv = kn[:, tt, :].rearrange("p (a b) -> p a b", b=HD)
                tt_(kv, PS[:, b + 2, 0:128].rearrange("p (c d) -> p c d", d=HD),
                    qstd[:, 16:18].unsqueeze(2).to_broadcast([P, 2, HD]), ALU.mult)
                dve.drain()
                tt_(qv, qv, kq_gain.unsqueeze(1).to_broadcast([P, 16, HD]), ALU.mult)
                tt_(kv, kv, par("k_gain").unsqueeze(1).to_broadcast([P, 2, HD]), ALU.mult).then_inc(qkn_done, 1)
            def biased(u):
                n, jq = u // 2, u % 2
                pr = probs[u % 2]
                if u >= 2:
                    dve.wait_ge(pt_psum, 4 * (u - 1))
                table = con("dist_first") if n == 0 else con("dist")
                for t in range(2):
                    dve.wait_ge(s_psum, 2 * u + t + 1)
                    for j in (2 * t, 2 * t + 1):
                        for kv in range(2):
                            head = 8 * kv + 4 * jq + j
                            ins = stt(pr[:, 2 * j + kv, :], table, con("slope")[:, head:head + 1],
                                      PS[:, 2 * t + kv, (j % 2) * 256:(j % 2) * 256 + 256], ALU.mult, ALU.add)
                    ins.then_inc(s_biased, 1)
                dve.drain()
                sink = par("sinks").rearrange("p (v q j) -> p q j v", v=2, q=2)[:, jq, :, :]
                m = am[u % 2]
                V.reduce_max(m, pr, AX.X)
                dve.drain()
                m2 = m.rearrange("p (j v) -> p j v", v=2)
                tt_(m2, m2, sink, ALU.max)
                dve.drain()
                tt_(ane[u % 2].rearrange("p (j v) -> p j v", v=2), sink, m2, ALU.subtract)
                dve.drain()
                ts(m, m, -1.0, ALU.mult).then_inc(m_done, 1)

            def summed(u):
                dve.wait_ge(p_exp, u + 1)
                tt_(asum[u % 2], aes[u % 2], ane[u % 2], ALU.add)
                dve.drain()
                V.reciprocal(asum[u % 2], asum[u % 2]).then_inc(m_done, 1)

            def attended(u):
                n, jq = u // 2, u % 2
                dve.wait_ge(att_done, u + 1)
                tt_(left_lo[:, 4 * jq:4 * jq + 4, n * 128:n * 128 + 128], PS[:, 4, :].rearrange("p (a b) -> p a b", b=128),
                    left_hi[:, 4 * jq:4 * jq + 4, n * 128:n * 128 + 128], ALU.subtract).then_inc(left_lo_done, 1)

            for u in range(8):
                biased(u)
                summed(u)
                if u >= 1:
                    attended(u - 1)
            attended(7)
            weights_lo(1, 1)
            residual(1)
            route(1)
            experts(1)
            experts_over(1)

        @block.tensor
        def _(pe):
            mm = nc.tensor.matmul
            T = nc.tensor.transpose

            def full(i):
                pe.wait_ge(slot_full[i % RING], 16 * (i // RING + 1))

            pending = [0]

            def give(ins):
                if pending[0]:
                    ins.then_inc(slot_free, pending[0])
                    pending[0] = 0

            def turn_tile(mixer, tt):
                c = TT * mixer + tt
                pe.wait_ge(xs_done, c + 1)
                for b in range(2):
                    if c >= 1:
                        pe.wait_ge(hT_done, 2 * c + b - 1)
                    for k in range(4):
                        at = (4 * b + k) * 128
                        ins = T(PS[:, b, k * 128:k * 128 + 128], xs[:, tt, at:at + 128], ident)
                        if b == 0 and k == 0:
                            give(ins)
                    ins.then_inc(turned_psum, 1)

            pe.wait_ge(const_in, 16)
            for tt in range(TT):
                turn_tile(0, tt)
            pe.wait_ge(hT_done, 2 * TT)
            full(0)
            full(1)
            for cb in range(4):
                if cb >= 2:
                    pe.wait_ge(u_done, cb - 1)
                for k in range(KD):
                    ins = mm(PS[:, 2 + cb % 2, :], k512(k // 4)[:, k % 4, cb * 128:cb * 128 + 128], hT[:, k, :],
                             start=k == 0, stop=k == KD - 1)
                    if cb == 3 and k == 3:
                        ins.then_inc(slot_free, 1)
                ins.then_inc(u_psum, 1)
            pending[0] = 1
            pe.wait_ge(bexp_done, 1)
            for ri in range(2):
                for b in range(4):
                    src = arena[:, 15360 + 1024 * ri + 128 * b:15360 + 1024 * ri + 128 * (b + 1)]
                    ins = T(PS[:, 6 + ri, b * 128:b * 128 + 128], src, ident)
                    if b == 0 and ri == 0:
                        give(ins)
            ins.then_inc(bT_psum, 1)

            def proj(i):
                s = 2 * (1 + i // 4)
                if i % 4 == 0:
                    full(s)
                    full(s + 1)
                if i >= 2:
                    pe.wait_ge(proj_done, i - 1)
                for k in range(KD):
                    w, h = k512(s + k // 4)[:, k % 4, :], hT[:, k, :]
                    lhsT, rhs = (w, h) if i < 8 else (h, w)
                    m = slice((i % 4) * 128, (i % 4) * 128 + 128)
                    ins = mm(PS[:, 6 + i % 2, :], lhsT[:, m], rhs, start=k == 0, stop=k == KD - 1)
                    if i % 4 == 3 and k == 3:
                        ins.then_inc(slot_free, 1)
                    elif k == 0:
                        give(ins)
                ins.then_inc(proj_psum, 1)
                if i % 4 == 3:
                    pending[0] = 1

            def inputs(i):
                b, q, s = i // 4, i % 4, i % 2
                if i >= 2:
                    pe.wait_ge(prod_done, i - 1)
                rows = slice(32 * q, 32 * q + 32)
                for ri in range(2):
                    ins = mm(PS[:, 2 * s + ri, :], BT[rows, ri, b, :], uT[rows, b, :], start=True, stop=True,
                             tile_position=(32 * q, 0))
                    if ri == 0:
                        give(ins)
                ins.then_inc(bu_done, 1)

            def readout(i):
                b = i // 4
                pe.wait_ge(ab_done, i + 1)
                if i % 4 == 0 and b >= 2:
                    pe.wait_ge(y_sum, b - 1)
                q = prod_out[i % 2]
                rows = 32 * (i % 4)
                out = PS[rows:rows + 32, 4 + b % 2, :]
                mm(out, Cx[:, 0, i, :], q[0], start=True, stop=False, tile_position=(0, rows))
                mm(out, Cx[:, 1, i, :], q[2], start=False, stop=True, tile_position=(0, rows)).then_inc(y_used, 1)

            pe.wait_ge(u_done, 4)
            pe.wait_ge(bT_done, 1)
            pe.wait_ge(cread_in, 16)
            inputs(0)
            inputs(1)
            for i in range(PAIRS):
                proj(i)
                if i >= 1:
                    readout(i - 1)
                if i + 2 < PAIRS:
                    inputs(i + 2)
            readout(PAIRS - 1)

            def head_scores(h):
                pe.wait_ge(hg_dve, 2 * h + 1)
                if h >= 2:
                    pe.wait_ge(sc_done, h - 1)
                for blk in range(4):
                    m = slice(blk * 128, blk * 128 + 128)
                    ins = mm(PS[:, h % 2, m], ke2[:, h, m], qe1[:, h, m], start=True, stop=True)
                ins.then_inc(sc_psum, 1)
                pe.wait_ge(hg_dve, 2 * h + 2)
                if h >= 1:
                    pe.wait_ge(ktm_done, h)
                for blk in range(4):
                    m = slice(blk * 128, blk * 128 + 128)
                    ins = T(PS[:, 2, m], ke3[:, h, m], ident)
                ins.then_inc(ktr_psum, 1)

            def head_increments(h):
                pe.wait_ge(ktm_done, h + 1)
                if h == 0:
                    pe.wait_ge(y_sum, 4)
                    pe.wait_ge(proj_done, PAIRS)
                else:
                    pe.wait_ge(st_done, h)
                for c in range(NCHUNK - 1):
                    r = slice(32 * (c % 4), 32 * (c % 4) + 32)
                    ins = mm(PS[:, 3 + c % 4, (c // 4) * 128:(c // 4) * 128 + 128], ke3_tm[h % 2][r, c // 4, :],
                             v_tm[r, c // 4, h * 128:h * 128 + 128], start=True, stop=True, tile_position=(32 * (c % 4), 0))
                ins.then_inc(inc_psum, 1)

            def head_out(h):
                pe.wait_ge(sc_done, h + 1)
                pe.wait_ge(qm_done, h + 1)
                pe.wait_ge(st_done, h + 1)
                if h >= 1:
                    pe.wait_ge(o_out, h)
                for blk in range(4):
                    out = PS[:, 7, blk * 128:blk * 128 + 128]
                    mm(out, scores[h % 2][:, blk, :], v_tm[:, blk, h * 128:h * 128 + 128], start=True, stop=False)
                    for r in range(4):
                        if 4 * blk + r == 0:
                            continue
                        ins = mm(out, q_masked[h % 2][:, 640 * blk + 128 * r:640 * blk + 128 * r + 128],
                                 state[h % 2][:, 4 * blk + r - 1, :], start=False, stop=r == 3)
                ins.then_inc(o_psum, 1)

            head_scores(0)
            head_increments(0)
            head_scores(1)
            for h in range(HEADS):
                if h + 1 < HEADS:
                    head_increments(h + 1)
                head_out(h)
                if h + 2 < HEADS:
                    head_scores(h + 2)
            full(GLU0)
            pe.wait_ge(gelu_done, 4)
            for b in range(4):
                for k in range(4):
                    ins = mm(PS[:, (0, 1, 4, 5)[b], :], k512(GLU0)[:, k, b * 128:b * 128 + 128], catT[:, k, :], start=k == 0, stop=k == 3)
                ins.then_inc(glu_psum, 1)
            pending[0] = 1
            for h in range(HEADS):
                pe.wait_ge(on_done, h + 1)
                if h >= 2:
                    pe.wait_ge(left_lo_done, 4 + h - 1)
                for blk in range(4):
                    m = slice(blk * 128, blk * 128 + 128)
                    ins = T(PS[:, 2 + h % 2, m], o_all[:, h, m], ident)
                    if blk == 0:
                        give(ins)
                ins.then_inc(otr_psum, 1)

            def out_proj(layer, lo_place, lefts):
                def turn_tokens(tt):
                    c = TT * layer + tt
                    pe.wait_ge(mix_done, 8 * layer + TT + tt + 1)
                    for b in range(2):
                        if c >= 1:
                            pe.wait_ge((tok_even, tok_odd)[b], c)
                        for k in range(4):
                            at = (4 * b + k) * 128
                            ins = T(PS[:, b, k * 128:k * 128 + 128], x[:, tt, at:at + 128], ident)
                            if b == 0 and k == 0:
                                give(ins)
                        ins.then_inc(tok_psum, 1)

                def logits(tt):
                    w = par(f"router{layer}").rearrange("p (k n) -> p k n", n=20)
                    pe.wait_ge(tok_even, TT * layer + tt + 1)
                    pe.wait_ge(tok_odd, TT * layer + tt + 1)
                    if TT * layer + tt >= 2:
                        pe.wait_ge(logit_read, TT * layer + tt - 1)
                    for k in range(KD):
                        ins = mm(PS[:, 2 + tt % 2, 0:20], tokT[tt % 2][:, k, :], w[:, k, :], start=k == 0, stop=k == KD - 1)
                    ins.then_inc(logit_psum, 1)

                def products(s, tt):
                    m = slice(tt * 128, tt * 128 + 128)
                    for q in range(4):
                        k = 4 * (s % 2) + q
                        hi, lo = left_hi[:, k, m], left_lo[:, lo_place[k], m]
                        w = [v[s % 2][:, q * 512:q * 512 + 512] for v in (w_hi, w_lo)]
                        for n, (a, b) in enumerate(((hi, w[0]), (hi, w[1]), (lo, w[0]))):
                            ins = mm(PS[:, 4 + tt, :], a, b, start=k == 0 and n == 0, stop=k == KD - 1 and n == 2)
                            if q == 0 and n == 0:
                                give(ins)
                    return ins

                for s in range(OUT_SLOTS):
                    if s < 2:
                        pe.wait_ge(left_lo_done, lefts[s])
                    pe.wait_ge(w_lo_done, 4 * layer + s + 1)
                    pending[0] += 1
                    for tt in range(TT + 2 if s == 3 else TT):
                        if tt < TT:
                            if s == 2:
                                pe.wait_ge(mix_done, 8 * layer + tt + 1)
                            ins = products(s, tt)
                            if s % 2:
                                ins.then_inc(mix_psum, 1)
                            if s == 0 and tt == TT - 1:
                                ins.then_inc(w_used, 1)
                        if s == 3 and 1 <= tt <= TT:
                            turn_tokens(tt - 1)
                        if s == 3 and tt >= 2:
                            logits(tt - 2)

            def route(layer):
                pe.wait_ge(mask_done, layer + 1)
                mm(PS[:, 3, 0:64], con("before"), taken.rearrange("p t e -> p (t e)"), start=True, stop=False)
                for t in range(TT - 1):
                    ins = mm(PS[:, 3, 16 * (t + 1):64].rearrange("p (t e) -> p t e", e=16), con("ones"),
                             taken[:, t:t + 1, :].to_broadcast([P, TT - 1 - t, 16]), start=False, stop=t == TT - 2)
                ins.then_inc(rank_psum, 1)
                pe.wait_ge(hot_done, layer + 1)
                lists(128, row_values).then_inc(list_psum, 1)
                pe.wait_ge(flags_done, layer + 1)
                mm(PS[:, 2, 0:1], con("ones"), flag_f, start=True, stop=True).then_inc(flag_psum, 1)
                pe.wait_ge(weighed, layer + 1)
                lists(144, weight_values).then_inc(weights_psum, 1)

            def lists(at, values):
                for n in range(2 * TT):
                    ins = mm(PS[:, 3, at:at + NE], rank_hot[:, n, :], values[:, n, :], start=n == 0, stop=n == 2 * TT - 1)
                return ins

            def experts(layer):
                base, s0 = layer * NE, EXP0[layer]

                def row_turns(j, n, got):
                    pe.wait_ge(got_row[j], got)
                    if not isinstance(n, int) or n >= 1:
                        pe.wait_ge(xT_done, n * 2)
                    for b in range(2):
                        for k in range(4):
                            ins = T(PS[:, b, k * 128:k * 128 + 128], xrow[j][:, (4 * b + k) * 128:(4 * b + k) * 128 + 128], ident)
                            if b == 0 and k == 0:
                                give(ins)
                        ins.then_inc(xT_psum, 1)

                def gate_up(j, n, it, at):
                    pe.wait_ge(xT_done, n * 2 + 2)
                    if not isinstance(n, int) or n >= 1:
                        pe.wait_ge(hid_done, n)
                    for k in range(KD):
                        i = at + k // 4
                        if k % 4 == 0:
                            pe.wait_ge(slot_full[i % RING], (it + (i // RING + 1)) * 16)
                        ins = mm(PS[:, 2, :], xT[j][:, k, :], k512(i)[:, k % 4, :], start=k == 0, stop=k == KD - 1)
                        if k == 3:
                            ins.then_inc(slot_free, 1)
                    ins.then_inc(gu_psum, 1)
                    pending[0] = 1

                def hid_turns(n):
                    pe.wait_ge(hid_done, n + 1)
                    if not isinstance(n, int) or n >= 1:
                        pe.wait_ge(hidT_done, n)
                    for k in range(2):
                        ins = T(PS[:, 3, k * 128:k * 128 + 128], hid[:, k * 128:k * 128 + 128], ident)
                        if k == 0:
                            give(ins)
                    ins.then_inc(hidT_psum, 1)

                def down(j, n, it, at):
                    pe.wait_ge(hidT_done, n + 1)
                    if not isinstance(n, int) or n >= 1:
                        pe.wait_ge(yrow_done, n)
                    pe.wait_ge(slot_full[at % RING], (it + (at // RING + 1)) * 16)
                    w = slot(at).rearrange("p (k n) -> p k n", n=D)
                    for half in range(2):
                        for k in range(2):
                            ins = mm(PS[:, 4 + half, :], hidT[:, k, :], w[:, k, half * 512:half * 512 + 512],
                                     start=k == 0, stop=k == 1)
                            if half == 0 and k == 0:
                                give(ins)
                    ins.then_inc(y_psum2, 1)
                    pending[0] = 1

                def step(j, n, it, more=True):
                    hid_turns(n)
                    gate_up(1 - j, n + 1, it, s0 + 3 * j + 2)
                    if more:
                        row_turns(j, n + 2, (it + (base // 2 + 2)) * 16)
                    down(j, n, it, s0 + 3 * j + 4)

                row_turns(0, base, (base // 2 + 1) * 16)
                gate_up(0, base, 0, s0)
                row_turns(1, base + 1, (base // 2 + 1) * 16)
                step(0, base, 0)
                step(1, base + 1, 0)
                with pe.Fori(1, NE // 2 - 1) as it:
                    for j in range(2):
                        step(j, it * 2 + (base + j), it)
                step(0, base + NE - 2, NE // 2 - 1, more=False)
                hid_turns(base + NE - 1)
                down(1, base + NE - 1, 0, s0 + EXP_SLOTS * NE - 1)

            def experts_over(layer):
                def body(s):
                    for r in range(OVER // P):
                        pe.wait_ge(s["hot"], r + 1)
                        lists(128, row_values)
                        lists(144, weight_values).then_inc(s["list_psum"], 1)
                    with pe.Fori(0, NE) as e:
                        for r in range(OVER // P):
                            q = e * (OVER // P) + r
                            pe.wait_ge(s["row"], q * 16 + 16)
                            for k in range(KD):
                                ins = T(PS[:, k // 4, (k % 4) * 128:(k % 4) * 128 + 128], xrow[0][:, k * 128:k * 128 + 128], ident)
                            ins.then_inc(s["xT_psum"], 1)
                            pe.wait_ge(s["xT"], q + 1)
                            if r == 0:
                                pe.wait_ge(s["weights"], e * 32 + 32)
                            for k in range(KD):
                                ins = mm(PS[:, 2, :], xT[0][:, k, :], over_w[:, 512 * k:512 * k + 512], start=k == 0, stop=k == KD - 1)
                            ins.then_inc(s["gate_up"], 1)
                            pe.wait_ge(s["hid"], q + 1)
                            for k in range(2):
                                ins = T(PS[:, 3, k * 128:k * 128 + 128], hid[:, k * 128:k * 128 + 128], ident)
                            ins.then_inc(s["hidT_psum"], 1)
                            pe.wait_ge(s["hidT"], q + 1)
                            for half in range(2):
                                for k in range(2):
                                    at = 2 * SLOT + k * D + half * 512
                                    ins = mm(PS[:, 4 + half, :], hidT[:, k, :], over_w[:, at:at + 512], start=k == 0, stop=k == 1)
                            ins.then_inc(s["y_psum"], 1)
                if_over(pe, layer, body)

            out_proj(0, [(k + 4) % KD for k in range(KD)], (4, 8))
            route(0)
            experts(0)
            experts_over(0)
            turn_tile(1, 0)
            def project(tt):
                pe.wait_ge(hT_done, 2 * TT + 2 * tt + 2)
                b = 2 + 3 * (tt % 2)
                if tt >= 2:
                    pe.wait_ge(qkn_done, tt - 1)
                for part in range(3):
                    n = 512 if part < 2 else 256
                    for k in range(KD):
                        if tt == 0 and (k == 0 or k == 4 and part < 2):
                            full(QKV0 + 2 * part + k // 4)
                        w = k512(QKV0 + 2 * part + k // 4)[:, k % 4, :] if part < 2 else \
                            slot(QKV0 + 4).rearrange("p (k n) -> p k n", n=256)[:, k, :]
                        ins = mm(PS[:, b + part, 0:n], hT[:, k, tt * 128:tt * 128 + 128], w, start=k == 0, stop=k == KD - 1)
                        if tt == 3 and part < 2 and k % 4 == 3:
                            ins.then_inc(slot_free, 1)
                ins.then_inc(qkv_psum, 1)

            def turn_heads(tt, banks):
                pe.wait_ge(qkn_done, max(tt + 1, 4) if tt >= 2 else tt + 1)
                for g in range(3):
                    n = 3 * tt + g
                    if tt and g < 2:
                        pe.wait_ge(qT_done, 3 * tt)
                    if g == 2:
                        pe.wait_ge(qT_done, n - 1)
                    for j in range(4 if g < 2 else 1):
                        src = qn[:, tt, (4 * g + j) * 128:(4 * g + j) * 128 + 128] if g < 2 else kn[:, tt, :]
                        ins = T(PS[:, banks[g], j * 128:j * 128 + 128], src, ident)
                        if g == 0 and j == 0:
                            give(ins)
                    ins.then_inc(qtr_psum, 1)

            def att_scores(u):
                n, jq = u // 2, u % 2
                for t in range(2):
                    if u >= 1:
                        pe.wait_ge(s_biased, 2 * u + t - 1)
                    for j in (2 * t, 2 * t + 1):
                        for kv in range(2):
                            d = slice(64 * kv, 64 * kv + 64)
                            ins = mm(PS[:, 2 * t + kv, (j % 2) * 256:(j % 2) * 256 + 256],
                                     qT1[d, 4 * jq + j, n * 128:n * 128 + 128], kT1[d, n * 128:n * 128 + 256],
                                     start=True, stop=True, tile_position=(64 * kv, 0))
                            if u == 0 and t == 0 and j == 0 and kv == 0:
                                give(ins)
                    ins.then_inc(s_psum, 1)

            project(0)
            for t in range(1, TT):
                turn_tile(1, t)
            project(1)
            turn_heads(0, (0, 1, 0))
            project(2)
            turn_heads(1, (0, 1, 0))
            project(3)
            pending[0] = 1
            pe.wait_ge(qT_done, 6)
            pe.wait_ge(qkn_done, 3)
            att_scores(0)
            turn_heads(2, (5, 6, 7))
            turn_heads(3, (5, 6, 7))
            pe.wait_ge(qT_done, 12)
            for u in range(8):
                n = u // 2
                if u + 1 < 8:
                    att_scores(u + 1)
                for b in range(4):
                    pe.wait_ge((p_norm, p_norm_odd)[b // 2], u + 1)
                    if 4 * u + b >= 2:
                        pe.wait_ge(pt_done, 4 * u + b - 1)
                    kv, kb = b // 2, b % 2
                    for j in range(4):
                        ins = T(PS[:, 5 + b % 2, j * 128:j * 128 + 128], probs[u % 2][:, 2 * j + kv, kb * 128:kb * 128 + 128], ident)
                    ins.then_inc(pt_psum, 1)
                if u >= 1:
                    pe.wait_ge(left_lo_done, 8 + u)
                for b in range(4):
                    pe.wait_ge(pt_done, 4 * u + b + 1)
                    ins = mm(PS[:, 4, :], vpad[:, n + b % 2, b // 2, :], probsT[u % 2][:, b, :], start=b == 0, stop=b == 3)
                ins.then_inc(att_psum, 1)
            out_proj(1, list(range(KD)), (16, 16))
            route(1)
            experts(1)
            experts_over(1)


def laid_out(i):
    import numpy as np
    f = {k: np.asarray(v) for k, v in i.items()}

    def rows(w, k):
        return w.reshape(k, P, -1).transpose(1, 0, 2)

    stream = np.zeros((N_SLOTS, P, SLOT), np.float32)

    def put(at, w):
        w = w.reshape(P, -1)
        for s in range(w.shape[1] // SLOT):
            stream[at + s] = w[:, s * SLOT:(s + 1) * SLOT]

    w_in = f["even_in_proj"][0]
    for s, c in enumerate((0, 2, 1, 3, 4)):
        put(2 * s, rows(w_in[:, 512 * c:512 * (c + 1)], KD))
    put(GLU0, rows(f["s5_glu_w"][0], 4))
    def halves(w):
        return rows(w, KD).reshape(P, KD, 2, 512).transpose(0, 2, 1, 3)

    put(OUT0, halves(f["even_out_proj"][0]))
    qkv = f["odd_wqkv"][0]
    q = qkv[:, :QW].reshape(D, 2, 8, HD).transpose(0, 2, 1, 3).reshape(D, QW)
    put(QKV0, rows(q[:, :512], KD))
    put(QKV0 + 2, rows(q[:, 512:], KD))
    put(QKV0 + 4, rows(qkv[:, QW:], KD))
    put(OUT1, halves(f["odd_out_proj"][0].reshape(2, 8, HD, D).transpose(1, 0, 2, 3).reshape(QW, D)))
    for layer in range(2):
        for e in range(NE):
            at = EXP0[layer] + EXP_SLOTS * e
            gu = np.concatenate([f["moe_w_gate"][layer, e], f["moe_w_up"][layer, e]], 1)
            put(at - (e > 0), rows(gu, KD))
            put(at + 4 if e < NE - 1 else at + 2, rows(f["moe_w_down"][layer, e], 2))

    param = np.zeros((P, N_PARAM), np.float32)

    def setp(name, v):
        a, b = PARAM[name]
        param[:, a:b] = v.reshape(P, -1) if v.ndim > 1 else v[None, :]

    for n, g in enumerate((f["even_mix_norm"][0], f["moe_norm"][0], f["odd_mix_norm"][0], f["moe_norm"][1])):
        setp(f"gain{n}", g.reshape(KD, P).T)
    for layer in range(2):
        w = np.concatenate([f["moe_router_group"][layer], f["moe_router_expert"][layer]], 1)
        setp(f"router{layer}", rows(w, KD))
        setp(f"bias{layer}", np.concatenate([f["moe_router_group_bias"][layer], f["moe_router_expert_bias"][layer]]))
    setp("lam_re", f["s5_lambda_re"][0].reshape(PAIRS, P).T)
    setp("lam_im", f["s5_lambda_im"][0].reshape(PAIRS, P).T)
    setp("log_step", np.repeat(f["s5_log_step"][0].reshape(PAIRS, 2), 64, axis=1).T)
    for name in ("b_re", "b_im"):
        b = f["s5_" + name][0].reshape(PAIRS, 2, 64, 16)
        v = np.zeros((2, 64, PAIRS, 2, 16), np.float32)
        for g in range(2):
            v[g, :, :, g, :] = b[:, g].transpose(1, 0, 2)
        setp(name, v.reshape(P, -1))
    setp("d_skip", f["s5_d"][0].reshape(4, P).T)
    setp("bounds", f["hgrn_lower_bounds"].reshape(3, HEADS, P).transpose(2, 0, 1))
    setp("o_gain", f["hgrn_o_norm"][0])
    setp("q_gain", f["odd_q_norm"][0])
    setp("k_gain", f["odd_k_norm"][0])
    setp("sinks", f["odd_sinks"][0])
    cread = np.zeros((2, 64, 2, PAIRS, 2, 16), np.float32)
    for ri, name in enumerate(("s5_c_re", "s5_c_im")):
        c = f[name][0].reshape(PAIRS, 2, 16, 64)
        for pair in range(PAIRS):
            for g in range(2):
                cread[g, :, ri, pair, g, :] = c[pair, g].T
    cread = cread.reshape(P, -1)

    const = np.zeros((P, N_CONST), np.float32)

    def setc(name, v):
        a, b = CONST[name]
        const[:, a:b] = v

    p, c = np.arange(P)[:, None], np.arange(512)[None, :]
    setc("ident", np.eye(P))
    setc("time", c)
    far = np.float32(1.0e30)
    dist = p - c[:, :256] + P
    inside = (dist >= 0) & (dist < WIN)
    setc("dist", np.where(inside, dist, far))
    setc("dist_first", np.where(inside & (c[:, :256] >= P), dist, far))
    setc("chunk_causal", (p // CH == c[:, :P] // CH) & (p <= c[:, :P]))
    setc("chunk_reset", c % CH != 0)
    setc("before", p < c[:, :P])
    setc("ones", 1.0)
    setc("iota4", c[:, :4])
    n = c[:, :2 * TT]
    setc("row_of", P * (n % TT) + p + 1)
    setc("slope", -(2.0 ** (-8.0 * np.arange(1, NQ + 1) / NQ))[None, :])
    return {"x_in": f["x"][0], "stream": stream, "cread": cread, "const_in": const, "param_in": param}


def kernel(**inputs):
    import numpy as np
    import concourse.bacc as bacc
    from concourse.bass_utils import run_bass_kernel_spmd

    nc = bacc.Bacc("TRN2", target_bir_lowering=False, num_devices=1)
    arrays, args = {}, []
    for name, a in laid_out(inputs).items():
        arrays[name] = np.ascontiguousarray(a)
        args.append(nc.dram_tensor(name, a.shape, mybir.dt.from_np(a.dtype), kind="ExternalInput").ap())
    out = nc.dram_tensor("out", [SEQ, D], mybir.dt.float32, kind="ExternalOutput").ap()
    trunk(nc, *args, out)
    r = run_bass_kernel_spmd(nc, [arrays], core_ids=[0])
    return r.results[0]["out"].reshape(1, SEQ, D)
```
